# Optimizing a Trainium2 kernel written in Bass

```python
import jax, jax.numpy as jnp
from jax import lax
import numpy as np

D_MODEL = 1024
BATCH = 1
SEQ = 256
DEPTH = 2

CONV_GROUPS = 4
CONV_GROUP_DIM = 128
CONV_DIM = CONV_GROUPS * CONV_GROUP_DIM
CONV_WIDTH = 31
SGU_HEADS = 4
SGU_HEAD_DIM = 128
SGU_DIM = SGU_HEADS * SGU_HEAD_DIM
CHUNK = 128
EVEN_IN = 2 * CONV_DIM + 2 * SGU_DIM
EVEN_MIX = CONV_DIM + SGU_DIM

MLA_HEADS = 8
MLA_Q_RANK = 256
MLA_KV_RANK = 128
MLA_NOPE = 64
MLA_ROPE = 32
MLA_V = 64
ROPE_THETA = 10000.0
SWA_HEADS = 8
SWA_KV_HEADS = 2
SWA_HEAD_DIM = 64
WINDOW = 128
BLOCK = 128
ODD_SPLITS = (MLA_Q_RANK, MLA_KV_RANK, MLA_ROPE, SWA_HEADS * SWA_HEAD_DIM,
              SWA_KV_HEADS * SWA_HEAD_DIM, SWA_KV_HEADS * SWA_HEAD_DIM)
ODD_IN = sum(ODD_SPLITS)
ODD_MIX = MLA_HEADS * MLA_V + SWA_HEADS * SWA_HEAD_DIM

N_GROUPS = 4
EXPERTS_PER_GROUP = 8
TOP_K = 2
D_EXPERT = 256

EPS = 1e-6
NEG_INF = -1e30

kernel_name = "hybrid_conv_sgu_mla_swa_hmoe_encoder"

def _rmsnorm(x, g):
    xf = x.astype(jnp.float32)
    y = xf * lax.rsqrt(jnp.mean(xf * xf, axis=-1, keepdims=True) + EPS)
    return (y * g.astype(jnp.float32)).astype(x.dtype)

def _layernorm(x, g, b):
    xf = x.astype(jnp.float32)
    mu = jnp.mean(xf, axis=-1, keepdims=True)
    var = jnp.mean(jnp.square(xf - mu), axis=-1, keepdims=True)
    y = (xf - mu) * lax.rsqrt(var + EPS)
    return (y * g.astype(jnp.float32) + b.astype(jnp.float32)).astype(x.dtype)

def _split_at(p, sizes):
    offs = np.cumsum(sizes)[:-1].tolist()
    return jnp.split(p, offs, axis=-1)

def _conv_sgu_mixer(h, w_in, conv_w, conv_b, cnorm_g, cnorm_b, vnorm_g, vnorm_b, w_sp, b_sp, w_out):
    B, S, _ = h.shape
    p = h @ w_in
    a_val, a_gate, u, v = _split_at(p, (CONV_DIM, CONV_DIM, SGU_DIM, SGU_DIM))
    a = a_val * jax.nn.sigmoid(a_gate)
    a = lax.conv_general_dilated(a, conv_w[:, None, :], window_strides=(1,),
                                 padding=[(CONV_WIDTH // 2, CONV_WIDTH // 2)],
                                 dimension_numbers=('NWC', 'WIO', 'NWC'),
                                 feature_group_count=CONV_DIM) + conv_b
    a = _layernorm(a.reshape(B, S, CONV_GROUPS, CONV_GROUP_DIM),
                   cnorm_g.reshape(CONV_GROUPS, CONV_GROUP_DIM),
                   cnorm_b.reshape(CONV_GROUPS, CONV_GROUP_DIM)).reshape(B, S, CONV_DIM)
    a = jax.nn.silu(a)
    nc = S // CHUNK
    u = jax.nn.gelu(u).reshape(B, nc, CHUNK, SGU_HEADS, SGU_HEAD_DIM)
    v = jax.nn.gelu(v).reshape(B, nc, CHUNK, SGU_HEADS, SGU_HEAD_DIM)
    v = _layernorm(v, vnorm_g.reshape(SGU_HEADS, SGU_HEAD_DIM), vnorm_b.reshape(SGU_HEADS, SGU_HEAD_DIM))
    sv = jnp.einsum('hts,bnshc->bnthc', w_sp, v) + jnp.swapaxes(b_sp, 0, 1)[:, :, None]
    s_out = (u * sv).reshape(B, S, SGU_DIM)
    return jnp.concatenate([a, s_out], axis=-1) @ w_out

def _rope_tables(S, dim):
    pos = jnp.arange(S, dtype=jnp.float32)
    inv = 1.0 / (ROPE_THETA ** (jnp.arange(0, dim, 2, dtype=jnp.float32) / dim))
    ang = pos[:, None] * inv[None, :]
    ang = jnp.concatenate([ang, ang], axis=-1)
    return jnp.cos(ang), jnp.sin(ang)

def _apply_rope(x, cos, sin):
    xf = x.astype(jnp.float32)
    x1, x2 = jnp.split(xf, 2, axis=-1)
    rot = jnp.concatenate([-x2, x1], axis=-1)
    return (xf * cos + rot * sin).astype(x.dtype)

def _alibi_slopes(n_heads):
    return jnp.exp2(-8.0 * jnp.arange(1, n_heads + 1, dtype=jnp.float32) / n_heads)

def _dense_attention(q, k, v):
    B, S, H, dqk = q.shape
    scale = dqk ** -0.5
    nb = S // BLOCK
    qb = q.reshape(B, nb, BLOCK, H, dqk).transpose(1, 0, 2, 3, 4)

    def one_block(qblk):
        s = jnp.einsum('bqhd,bkhd->bhqk', qblk, k).astype(jnp.float32) * scale
        p = jax.nn.softmax(s, axis=-1).astype(v.dtype)
        return jnp.einsum('bhqk,bkhd->bqhd', p, v)

    out = lax.map(one_block, qb)
    return out.transpose(1, 0, 2, 3, 4).reshape(B, S, H, v.shape[-1])

def _window_gqa_attention(q, k, v, sink):
    B, S, Hq, dh = q.shape
    G = k.shape[2]
    R = Hq // G
    nb = S // BLOCK
    span = BLOCK + 2 * WINDOW
    qb = q.reshape(B, nb, BLOCK, G, R, dh)
    idx = jnp.arange(nb)[:, None] * BLOCK + jnp.arange(span)[None, :]
    kp = jnp.pad(k, ((0, 0), (WINDOW, WINDOW), (0, 0), (0, 0)))
    vp = jnp.pad(v, ((0, 0), (WINDOW, WINDOW), (0, 0), (0, 0)))
    kb = kp[:, idx]
    vb = vp[:, idx]
    s = jnp.einsum('bnqgrd,bnkgd->bngrqk', qb, kb).astype(jnp.float32) * (dh ** -0.5)
    qi = jnp.arange(BLOCK)
    kj = jnp.arange(span)
    dist = qi[:, None] + WINDOW - kj[None, :]
    in_win = jnp.abs(dist) <= WINDOW
    kpos = jnp.arange(nb)[:, None] * BLOCK - WINDOW + kj[None, :]
    in_seq = (kpos >= 0) & (kpos < S)
    mask = in_win[None] & in_seq[:, None, :]
    slopes = _alibi_slopes(Hq).reshape(G, R)
    bias = -slopes[:, :, None, None] * jnp.abs(dist).astype(jnp.float32)
    s = jnp.where(mask[None, :, None, None], s + bias, NEG_INF)
    sk = sink.astype(jnp.float32).reshape(G, R)[:, :, None]
    m = jnp.maximum(jnp.max(s, axis=-1), sk)
    e = jnp.exp(s - m[..., None])
    denom = jnp.sum(e, axis=-1) + jnp.exp(sk - m)
    pr = (e / denom[..., None]).astype(v.dtype)
    o = jnp.einsum('bngrqk,bnkgd->bnqgrd', pr, vb)
    return o.reshape(B, S, Hq, dh)

def _mla_swa_mixer(h, w_in, g_cq, w_uq, g_ckv, w_ukv, sink, w_out):
    B, S, _ = h.shape
    p = h @ w_in
    c_q, c_kv, k_pe, q_s, k_s, v_s = _split_at(p, ODD_SPLITS)
    cos, sin = _rope_tables(S, MLA_ROPE)
    q = (_rmsnorm(c_q, g_cq) @ w_uq).reshape(B, S, MLA_HEADS, MLA_NOPE + MLA_ROPE)
    q_nope, q_pe = jnp.split(q, [MLA_NOPE], axis=-1)
    q_pe = _apply_rope(q_pe, cos[:, None, :], sin[:, None, :])
    kv = (_rmsnorm(c_kv, g_ckv) @ w_ukv).reshape(B, S, MLA_HEADS, MLA_NOPE + MLA_V)
    k_nope, v_mla = jnp.split(kv, [MLA_NOPE], axis=-1)
    k_pe = _apply_rope(k_pe, cos, sin)
    q_full = jnp.concatenate([q_nope, q_pe], axis=-1)
    k_full = jnp.concatenate([k_nope, jnp.broadcast_to(k_pe[:, :, None, :], (B, S, MLA_HEADS, MLA_ROPE))], axis=-1)
    mla = _dense_attention(q_full, k_full, v_mla).reshape(B, S, MLA_HEADS * MLA_V)
    swa = _window_gqa_attention(q_s.reshape(B, S, SWA_HEADS, SWA_HEAD_DIM),
                                k_s.reshape(B, S, SWA_KV_HEADS, SWA_HEAD_DIM),
                                v_s.reshape(B, S, SWA_KV_HEADS, SWA_HEAD_DIM),
                                sink).reshape(B, S, SWA_HEADS * SWA_HEAD_DIM)
    return jnp.concatenate([mla, swa], axis=-1) @ w_out

def _hier_moe(h, w_group, b_group, w_router, b_router, w_gate, w_up, w_down):
    B, S, D = h.shape
    f32 = jnp.float32
    t = h.reshape(B * S, D)
    group_prob = jax.nn.softmax((t @ w_group).astype(f32) + b_group.astype(f32), axis=-1)
    g_p, g_idx = lax.top_k(group_prob, 1)
    exp_logits = jnp.einsum('td,gde->tge', t, w_router).astype(f32) + b_router.astype(f32)
    sel = jnp.take_along_axis(exp_logits, g_idx[:, :, None], axis=1)[:, 0]
    top_v, top_i = lax.top_k(sel, TOP_K)
    top_w = jax.nn.softmax(top_v, axis=-1) * g_p
    within = jnp.einsum('tk,tke->te', top_w, jax.nn.one_hot(top_i, EXPERTS_PER_GROUP, dtype=f32))
    gate = jax.nn.one_hot(g_idx[:, 0], N_GROUPS, dtype=f32)[:, :, None] * within[:, None, :]
    y = jnp.zeros((B * S, D), f32)
    for g in range(N_GROUPS):
        hid = jax.nn.silu(jnp.einsum('td,edf->tef', t, w_gate[g])) * jnp.einsum('td,edf->tef', t, w_up[g])
        hid = hid * gate[:, g, :, None].astype(hid.dtype)
        y = y + jnp.einsum('tef,efd->td', hid, w_down[g]).astype(f32)
    return y.astype(h.dtype).reshape(B, S, D)

def setup_inputs(seed: int = 0) -> dict:
    key = jax.random.key(seed)
    ks = list(jax.random.split(key, 32))
    f32 = jnp.float32
    ne = (DEPTH + 1) // 2
    no = DEPTH // 2

    def nrm(shape, scale):
        return jax.random.normal(ks.pop(), shape, f32) * scale

    def gain(shape):
        return 1.0 + nrm(shape, 0.1)

    D = D_MODEL
    ng, ne_g, F = N_GROUPS, EXPERTS_PER_GROUP, D_EXPERT
    return {
        "x": nrm((BATCH, SEQ, D), 1.0),
        "norm_mix": gain((DEPTH, D)),
        "norm_ffn": gain((DEPTH, D)),
        "norm_final": gain((D,)),
        "ev_w_in": nrm((ne, D, EVEN_IN), D ** -0.5),
        "ev_conv_w": nrm((ne, CONV_WIDTH, CONV_DIM), CONV_WIDTH ** -0.5),
        "ev_conv_b": nrm((ne, CONV_DIM), 0.02),
        "ev_cnorm_g": gain((ne, CONV_DIM)),
        "ev_cnorm_b": nrm((ne, CONV_DIM), 0.02),
        "ev_vnorm_g": gain((ne, SGU_DIM)),
        "ev_vnorm_b": nrm((ne, SGU_DIM), 0.02),
        "ev_w_sp": nrm((ne, SGU_HEADS, CHUNK, CHUNK), CHUNK ** -0.5),
        "ev_b_sp": gain((ne, SGU_HEADS, CHUNK)),
        "ev_w_out": nrm((ne, EVEN_MIX, D), EVEN_MIX ** -0.5),
        "od_w_in": nrm((no, D, ODD_IN), D ** -0.5),
        "od_g_cq": gain((no, MLA_Q_RANK)),
        "od_w_uq": nrm((no, MLA_Q_RANK, MLA_HEADS * (MLA_NOPE + MLA_ROPE)), MLA_Q_RANK ** -0.5),
        "od_g_ckv": gain((no, MLA_KV_RANK)),
        "od_w_ukv": nrm((no, MLA_KV_RANK, MLA_HEADS * (MLA_NOPE + MLA_V)), MLA_KV_RANK ** -0.5),
        "od_sink": nrm((no, SWA_HEADS), 1.0),
        "od_w_out": nrm((no, ODD_MIX, D), ODD_MIX ** -0.5),
        "moe_w_group": nrm((DEPTH, D, ng), D ** -0.5),
        "moe_b_group": nrm((DEPTH, ng), 0.01),
        "moe_w_router": nrm((DEPTH, ng, D, ne_g), D ** -0.5),
        "moe_b_router": nrm((DEPTH, ng, ne_g), 0.01),
        "moe_w_gate": nrm((DEPTH, ng, ne_g, D, F), D ** -0.5),
        "moe_w_up": nrm((DEPTH, ng, ne_g, D, F), D ** -0.5),
        "moe_w_down": nrm((DEPTH, ng, ne_g, F, D), F ** -0.5),
    }

def reference(x, norm_mix, norm_ffn, norm_final,
              ev_w_in, ev_conv_w, ev_conv_b, ev_cnorm_g, ev_cnorm_b, ev_vnorm_g, ev_vnorm_b,
              ev_w_sp, ev_b_sp, ev_w_out,
              od_w_in, od_g_cq, od_w_uq, od_g_ckv, od_w_ukv, od_sink, od_w_out,
              moe_w_group, moe_b_group, moe_w_router, moe_b_router, moe_w_gate, moe_w_up, moe_w_down):
    for layer in range(DEPTH):
        i = layer // 2
        h = _rmsnorm(x, norm_mix[layer])
        if layer % 2 == 0:
            x = x + _conv_sgu_mixer(h, ev_w_in[i], ev_conv_w[i], ev_conv_b[i], ev_cnorm_g[i], ev_cnorm_b[i],
                                    ev_vnorm_g[i], ev_vnorm_b[i], ev_w_sp[i], ev_b_sp[i], ev_w_out[i])
        else:
            x = x + _mla_swa_mixer(h, od_w_in[i], od_g_cq[i], od_w_uq[i], od_g_ckv[i], od_w_ukv[i],
                                   od_sink[i], od_w_out[i])
        h = _rmsnorm(x, norm_ffn[layer])
        x = x + _hier_moe(h, moe_w_group[layer], moe_b_group[layer], moe_w_router[layer], moe_b_router[layer],
                          moe_w_gate[layer], moe_w_up[layer], moe_w_down[layer])
    return _rmsnorm(x, norm_final)


_drawn_inputs = setup_inputs


def setup_inputs(seed=0):
    import zlib

    import numpy as np

    out = dict(_drawn_inputs(seed))
    spreads = {}
    factors = {'od_g_cq': 3.679, 'od_sink': 3.696, 'moe_b_group': 3.598}
    for name, (base, spread) in spreads.items():
        noise = np.random.default_rng([zlib.crc32(name.encode()), seed]).standard_normal(out[name].shape)
        drawn = base * np.exp(spread * noise) if base else spread * noise
        out[name] = __import__('jax').numpy.asarray(drawn.astype(out[name].dtype))
    for name, factor in factors.items():
        out[name] = (out[name] * factor).astype(out[name].dtype)
    return out
```

```python
import concourse.bass as bass
from concourse import mybir
from concourse.alu_op_type import AluOpType as ALU
from contextlib import ExitStack
import numpy as np

D, SEQ, P = 1024, 256, 128
NT = SEQ // P
KD = D // P
GROUPS, PER_GROUP, F = 4, 8, 256
EXPERTS = GROUPS * PER_GROUP
SLOTS = 32
QUAD = P // SLOTS
QUADS = EXPERTS // QUAD
ROUND = EXPERTS * SLOTS
MAX_ROUNDS = SEQ // SLOTS
FC = F // P
GU = 2 * KD * F
DN = FC * D
TAPS, CG = 31, 4
HALO = TAPS // 2
APAD = SEQ + 2 * HALO + 2
HEADS, NOPE, ROPE, VD = 8, 64, 32, 64
QK = NOPE + ROPE
QR, KVR = 256, 128
MLA_SCALE = float(QK) ** -0.5
SWA_D, KVH, WINDOW = 64, 2, 128
SWA_SCALE = float(SWA_D) ** -0.5
COL_A = QR + KVR + ROPE
COL_B = HEADS * SWA_D
COL_C = 2 * KVH * SWA_D
ODD_IN = COL_A + COL_B + COL_C
EPS = 1e-6
FAR = 1e30
LOW = -3e38
NROW = TAPS + 3

CONST = {}
_at = 0
for _n, _w in (("ident", P), ("before", P), ("ones", P), ("mean", P), ("slot_row", P), ("slot_col", 1),
               ("iota_e", EXPERTS), ("iota_g", GROUPS), ("steps", MAX_ROUNDS - 1), ("eps", 1),
               ("cos", NT * ROPE), ("sin", NT * ROPE), ("dist", NT * SEQ)):
    CONST[_n] = (_at, _at + _w)
    _at += _w
NCONST = _at
NFIRST = CONST["dist"][0]
NSCRATCH = 8320


def constants():
    c = np.zeros((P, NCONST), np.float32)

    def put(name, value):
        a, b = CONST[name]
        c[:, a:b] = np.asarray(value, np.float32).reshape(-1, b - a)

    i = np.arange(P)
    put("ident", np.eye(P))
    put("before", i[:, None] < i[None, :])
    put("ones", np.ones((P, P)))
    put("mean", np.full((P, P), 1.0 / P))
    put("slot_row", np.tile(i, (P, 1)))
    put("slot_col", i[:, None])
    put("iota_e", np.tile(np.arange(EXPERTS), (P, 1)))
    put("iota_g", np.tile(np.arange(GROUPS), (P, 1)))
    put("steps", np.tile(SLOTS * np.arange(1, MAX_ROUNDS), (P, 1)))
    put("eps", np.full((P, 1), EPS))
    inv = (np.float32(1.0) / (np.float32(10000.0) ** (np.arange(0, ROPE, 2, dtype=np.float32) / np.float32(ROPE)))).astype(np.float32)
    ang = np.arange(SEQ, dtype=np.float32)[:, None] * inv[None, :]
    ang = np.concatenate([ang, ang], axis=-1).astype(np.float32)
    sin = np.sin(ang)
    sin[:, :ROPE // 2] *= -1
    put("cos", np.cos(ang).reshape(NT, P, ROPE).transpose(1, 0, 2).reshape(P, -1))
    put("sin", sin.reshape(NT, P, ROPE).transpose(1, 0, 2).reshape(P, -1))
    dist = np.abs(np.arange(SEQ)[:, None] - np.arange(SEQ)[None, :]).astype(np.float32)
    dist[dist > WINDOW] = FAR
    put("dist", dist.reshape(NT, P, SEQ).transpose(1, 0, 2).reshape(P, -1))
    return c


def program(nc, x, norm_mix, norm_ffn, norm_final, ev_w_in, ev_conv_w, ev_conv_b, ev_cnorm_g, ev_cnorm_b,
            ev_vnorm_g, ev_vnorm_b, ev_w_sp, ev_b_sp, ev_w_out, od_w_in, od_g_cq, od_w_uq, od_g_ckv,
            od_w_ukv, od_sink, od_w_out, moe_w_group, moe_b_group, moe_w_router, moe_b_router,
            moe_w_gate, moe_w_up, moe_w_down, const, out):
    fp32, i32, u32 = mybir.dt.float32, mybir.dt.int32, mybir.dt.uint32
    ACT = mybir.ActivationFunctionType
    AX = mybir.AxisListType.X

    ctx = ExitStack()
    with ctx:
        def sb(name, shape, dt=fp32):
            return ctx.enter_context(nc.sbuf_tensor(name, shape, dt))

        def sem(name):
            return ctx.enter_context(nc.semaphore(name))

        scratch = sb("scratch", [P, NSCRATCH])
        place = [0]

        def carve(shape, dt=fp32, at=None):
            size = int(np.prod(shape[1:]))
            a = place[0] if at is None else at
            if at is None:
                place[0] += size
            assert a + size <= NSCRATCH, (a, size)
            v = scratch[0:shape[0], a:a + size]
            if dt != fp32:
                v = v.bitcast(dt)
            names = "abc"[:len(shape) - 1]
            if len(shape) > 2:
                v = v.rearrange(f"p ({' '.join(names)}) -> p {' '.join(names)}",
                                **{n: w for n, w in zip(names[1:], shape[2:])})
            return v

        ring_gu = sb("ring_gu", [P, QUAD, GU])
        ring_dn = sb("ring_dn", [P, QUAD, DN])
        wout = sb("wout", [P, QUAD, 2 * D])
        X = sb("X", [P, NT, D])
        xhat = sb("xhat", [P, NT, D])
        hT = sb("hT", [P, KD, SEQ])
        mixT = sb("mixT", [P, KD, SEQ])
        zeros = sb("zeros", [1, P])
        cst = sb("cst", [P, NCONST])
        hT_flat = hT[:, :, :].rearrange("p k s -> p (k s)")
        junk, junk_v = hT_flat[:, 0:D], hT_flat[:, D:2 * D]
        gain = sb("gain", [P, 4, KD])
        gfin = mixT[:, 0:4, :].rearrange("p k s -> p (k s)")
        stat = sb("stat", [P, 5, NT, 5])
        xhat_flat = xhat[:, :, :].rearrange("p t n -> p (t n)")
        mixT_flat = mixT[:, :, :].rearrange("p k s -> p (k s)")

        def rows3(v, b, c):
            return v.rearrange("p (b c) -> p b c", b=b, c=c)


        def C(name):
            a, b = CONST[name]
            return cst[:, a:b]

        ident, before, ones, meanm = C("ident"), C("before"), C("ones"), C("mean")
        eps_col = C("eps")

        chan_rows = carve([NROW, CG * P])
        chanp = carve([P, CG, NROW])
        wsp = carve([P, CG, P])
        wspT = carve([P, CG, P])
        bsp = carve([1, CG * P])
        vgb = carve([P, 2, CG * P])
        sig = rows3(xhat_flat[:, 0:D], CG, SEQ)
        aT = carve([P, CG, APAD])
        conv = carve([P, CG, SEQ])
        sq = sig
        uT = carve([P, CG, SEQ])
        vt = rows3(xhat_flat[:, D:2 * D], NT, CG * P)
        vn = vt
        vst = carve([P, NT * CG, 6])
        vag = carve([P, NT * CG, 2])
        vstd = carve([P, NT * CG])
        vrs = carve([P, NT * CG])

        even_end = place[0]
        place[0] = 0
        g_cq = sb("g_cq", [P, QR // P])
        g_ckv = sb("g_ckv", [P, 1])
        sink = sb("sink", [P, HEADS])
        qs_at = place[0]
        qs = carve([P, NT, COL_B])
        ksvs = carve([P, NT, COL_C])
        lat_at = place[0]
        lat = carve([P, NT, QR + KVR])
        cqT = carve([P, QR // P, SEQ])
        lsq = lat
        kpe = carve([P, NT, ROPE])
        lst = carve([P, 4, 2, NT])
        ckvT = carve([P, SEQ])
        qf_at = place[0]
        qf = carve([P, NT, HEADS * QK])
        kf = carve([P, NT, HEADS, QK])
        vm = carve([P, NT, HEADS, VD])
        rt1 = carve([P, 5 * ROPE])
        rt2 = carve([P, 5 * ROPE])
        qT = rows3(xhat_flat, HEADS, SEQ)
        kT = hT
        qsT = carve([P, HEADS // 2, SEQ], at=lat_at)
        ksT = carve([P, SEQ])
        sw = carve([P, 2, 2, SEQ], at=qs_at)
        prob = mixT_flat[:, 0:D].rearrange("p (a b c) -> p a b c", a=2, b=2)
        pT = mixT_flat[:, D:2 * D].rearrange("p (a b c) -> p a b c", a=2, b=4)
        UNITS = 2 * NT * (HEADS // 2)
        us = carve([P, UNITS, 6, 2])
        osb = carve([P, NT, D], at=qf_at)

        place[0] = 0
        NL = GROUPS + EXPERTS
        wrt_in = carve([P, 2, GROUPS, KD * PER_GROUP], at=even_end)
        wrt = sb("wrt", [P, 2, KD, NL])
        wgr = carve([P, 2, KD, GROUPS], at=even_end + 2 * KD * EXPERTS)
        brt = sb("brt", [P, 2, NL])
        gl = sb("gl", [P, NT, 8])
        rl = carve([P, NT, EXPERTS])
        gm8 = carve([P, NT, 8])
        gi8 = carve([P, NT, 8], u32)
        em8 = carve([P, NT, 8])
        ei8 = carve([P, NT, 8], u32)
        gif = carve([P, NT])
        goh = carve([P, NT, GROUPS])
        selp = carve([P, NT, EXPERTS])
        sel = carve([P, NT, PER_GROUP])
        eif = carve([P, NT, 2])
        exin = carve([P, NT, 5])
        exo = carve([P, NT, 5])
        gsum = carve([P, NT])
        den = carve([P, NT])
        den2 = carve([P, NT])
        weight = carve([P, NT, 2])
        eid = carve([P, NT, 2])
        eoh = carve([P, NT, 2, EXPERTS])
        member = carve([P, NT, EXPERTS])
        rkp = carve([P, NT, 2, EXPERTS])
        rank = carve([P, NT, 2])
        cmax = carve([P, 1])
        cge = carve([P, MAX_ROUNDS - 1])
        extra = carve([P, 1])
        nq = sb("nq", [P, 2], i32)
        rge = carve([P, NT, 2, MAX_ROUNDS - 1])
        turn = carve([P, NT, 2])
        key0 = carve([P, NT, 2])
        key = carve([P, NT, 2])
        keyrow = carve([P, 2, SEQ])
        wrow = carve([P, 2, SEQ])
        slot_row = carve([P, P])
        slot_col = carve([P, 1])
        pick = carve([P, NT, P])
        back = carve([P, 2, SEQ])
        backs = carve([P, SEQ])
        xs = carve([P, KD, P])
        sg = carve([P, F])
        hid = carve([P, F])
        hidT = carve([P, FC, P])
        ys = carve([P, D])

        B = [ctx.enter_context(nc.psum_tensor(f"B{i}", [P, 512], fp32)) for i in range(8)]

        x_in = [sem(f"x_in{t}") for t in range(NT)]
        wo_in = [sem(f"wo_in{j}") for j in range(QUAD)]
        dist_in, vec_in, weight_ok = sem("dist_in"), sem("vec_in"), sem("weight_ok")
        const_in, gain_in, even_in, odd_in, route_in, gfin_in = (
            sem(n) for n in ("const_in", "gain_in", "even_in", "odd_in", "route_in", "gfin_in"))
        gu_in = [sem(f"gu_in{j}") for j in range(QUAD)]
        dn_in = [sem(f"dn_in{j}") for j in range(QUAD)]
        zeros_ok = sem("zeros_ok")
        pads_done, route_w_done, route_w_part = sem("pads_done"), sem("route_w_done"), sem("route_w_part")
        act_sum, dve_sum, var_done, std_done, rstd_done = (
            sem(n) for n in ("act_sum", "dve_sum", "var_done", "std_done", "rstd_done"))
        xhat_act, xhat_dve, norm_T = sem("xhat_act"), sem("xhat_dve"), sem("norm_T")
        hT_dve, hT_act = sem("hT_dve"), sem("hT_act")
        x_new = sem("x_new")
        dve_step = sem("dve_step")
        act_step = sem("act_step")
        chan_T, wsp_T, chan_ok, wsp_ok = (sem(n) for n in ("chan_T", "wsp_T", "chan_ok", "wsp_ok"))
        vg_done, sig_done, a_done, v_done, u_done = (sem(n) for n in ("vg_done", "sig_done", "a_done", "v_done", "u_done"))
        gelu_v, gelu_u, vvar, vstd_ok, vn_done = (sem(n) for n in ("gelu_v", "gelu_u", "vvar", "vstd_ok", "vn_done"))
        sv_done, gated, conv_done, mean_done = (sem(n) for n in ("sv_done", "gated", "conv_done", "mean_done"))
        cen_done, sq_done, cvar_done, cstd_ok, cn_done, silu_done = (
            sem(n) for n in ("cen_done", "sq_done", "cvar_done", "cstd_ok", "cn_done", "silu_done"))
        out_done = sem("out_done")
        pa_done, pb_done, pc_done = (sem(n) for n in ("pa_done", "pb_done", "pc_done"))
        lsum, lvar, lstd, lrs = (sem(n) for n in ("lsum", "lvar", "lstd", "lrs"))
        cq_ok, ckv_ok, lat_T, latT_ok, qs_ok, ks_ok = (
            sem(n) for n in ("cq_ok", "ckv_ok", "lat_T", "latT_ok", "qs_ok", "ks_ok"))
        q_up, kv_up, q_nope, q_rope, k_nope, v_ok, k_rope = (
            sem(n) for n in ("q_up", "kv_up", "q_nope", "q_rope", "k_nope", "v_ok", "k_rope"))
        head_T, headT_act, headT_dve = sem("head_T"), sem("headT_act"), sem("headT_dve")
        score, biased, negmax, expd, sink_d, sink_e = (
            sem(n) for n in ("score", "biased", "negmax", "expd", "sink_d", "sink_e"))
        prob_T, pT_ok, pv, o_ok, o_T, oT_act, oT_dve = (
            sem(n) for n in ("prob_T", "pT_ok", "pv", "o_ok", "o_T", "oT_act", "oT_dve"))
        logits, ex_in, ex_out, member_ok, ranks, nq_ok, key_ok, rows_T, rows_ok = (
            sem(n) for n in ("logits", "ex_in", "ex_out", "member_ok", "ranks", "nq_ok", "key_ok", "rows_T", "rows_ok"))
        M = [{n: sem(f"{n}_{l}") for n in (
            "pick_ok", "gath0", "gath1", "xs0", "xs1", "gu_used", "silu_g", "hid_ok", "hid_T", "hidT_ok",
            "down0", "dn_used", "ys0", "ys1", "back_ok", "moe_step", "y_done")} for l in range(2)]
        o_sem = sem("o_sem")
        stored = sem("stored")

        block = ctx.enter_context(nc.Block())

        w_in0 = ev_w_in[0].rearrange("(p k) (b n) -> b p k n", k=KD, b=4)
        w_out0 = ev_w_out[0].rearrange("(j c p) n -> j p c n", p=P, c=2)
        w_out1 = od_w_out[0].rearrange("(j c p) n -> j p c n", p=P, c=2)
        w_in1 = od_w_in[0].rearrange("(p k) n -> p k n", k=KD)

        def gu_slot(j):
            return ring_gu[:, j, :].rearrange("p (k n) -> p k n", k=KD)

        wA = ring_gu[:, 0, 0:KD * COL_A].rearrange("p (k n) -> p k n", k=KD)
        wB = gu_slot(1)
        wC = ring_gu[:, 2, 0:KD * COL_C].rearrange("p (k n) -> p k n", k=KD)
        UQ0 = KD * COL_C
        NUQ = HEADS * QK
        NUKV = HEADS * (NOPE + VD)
        wuq = ring_gu[:, 2, UQ0:UQ0 + QR // P * NUQ].rearrange("p (c n) -> p c n", n=NUQ)
        wukv = ring_gu[:, 3, 0:NUKV]

        head_blocks = []
        for pair in range(0, HEADS, 2):
            head_blocks.append((qT[0:QK, pair:pair + 2, :].rearrange("p h s -> p (h s)"), QK,
                                [qf[:, t, h * QK:(h + 1) * QK] for h in (pair, pair + 1) for t in range(NT)]))
            head_blocks.append((kT[0:QK, pair:pair + 2, :].rearrange("p h s -> p (h s)"), QK,
                                [kf[:, t, h, :] for h in (pair, pair + 1) for t in range(NT)]))
        for r in range(0, HEADS // KVH, 2):
            head_blocks.append((qsT[:, r:r + 2, :].rearrange("p h s -> p (h s)"), P,
                                [qs[:, t, rr * P:(rr + 1) * P] for rr in (r, r + 1) for t in range(NT)]))
        head_blocks.append((ksT[:, :], P, [ksvs[:, t, 0:P] for t in range(NT)]))
        NHB = len(head_blocks)
        HB_ACT = NHB // 2
        HB_DVE = NHB - HB_ACT

        def score_bank(u, i):
            if u < UNITS // 2:
                return B[(0, 1, 6, 7)[u % 4]][:, i * SEQ:(i + 1) * SEQ]
            return B[u % 2 + 6 * i][:, 0:SEQ]

        hT_free = {0: (const_in, 16), 1: (u_done, 2), 2: (logits, 1), 3: (score, UNITS)}

        @block.sync
        def _(sp):
            for t in range(NT):
                sp.dma_start(X[:, t, :], x[0, t * P:(t + 1) * P, :]).then_inc(x_in[t], 16)
            sp.dma_start(cst[:, 0:NFIRST], const[:, 0:NFIRST]).then_inc(const_in, 16)
            sp.dma_start(gain[:, 0:4:2, :], norm_mix.rearrange("l (p k) -> p l k", k=KD)).then_inc(gain_in, 16)
            sp.dma_start(gain[:, 1:4:2, :], norm_ffn.rearrange("l (p k) -> p l k", k=KD)).then_inc(gain_in, 16)
            sp.dma_start(gu_slot(0), w_in0[0]).then_inc(gu_in[0], 16)
            sp.dma_start(chan_rows[0:TAPS, :], ev_conv_w[0]).then_inc(even_in, 16)
            for i, w in enumerate((ev_conv_b, ev_cnorm_g, ev_cnorm_b)):
                sp.dma_start(chan_rows[TAPS + i:TAPS + i + 1, :], w).then_inc(even_in, 16)
            sp.dma_start(wsp[:, :, :], ev_w_sp[0].rearrange("h t s -> t h s")).then_inc(even_in, 16)
            sp.dma_start(bsp[:, :], ev_b_sp.rearrange("a h t -> a (h t)")).then_inc(even_in, 16)
            sp.dma_start(gu_slot(1), w_in0[1]).then_inc(gu_in[1], 16)
            sp.dma_start(gu_slot(3), w_in0[3]).then_inc(gu_in[3], 16)
            sp.dma_start(vgb[:, 0, :], ev_vnorm_g.broadcast_to([P, CG * P])).then_inc(vec_in, 16)
            sp.dma_start(vgb[:, 1, :], ev_vnorm_b.broadcast_to([P, CG * P])).then_inc(vec_in, 16)
            sp.dma_start(gu_slot(2), w_in0[2]).then_inc(gu_in[2], 16)

            def load_w_out(w):
                for j in (2, 3, 0, 1):
                    sp.dma_start(wout[:, j, :].rearrange("p (c n) -> p c n", c=2), w[j]).then_inc(wo_in[j], 16)

            load_w_out(w_out0)
            for l in range(2):
                sp.dma_start(wgr[:, l, :, :], moe_w_group[l].rearrange("(p k) g -> p k g", k=KD)).then_inc(route_in, 16)
                sp.dma_start(wrt_in[:, l, :, :],
                             moe_w_router[l].rearrange("g (p k) e -> p g (k e)", k=KD)).then_inc(route_in, 16)
            sp.dma_start(brt[:, :, 0:GROUPS],
                         moe_b_group.rearrange("l (o g) -> o l g", o=1).broadcast_to([P, 2, GROUPS])).then_inc(route_in, 16)
            sp.dma_start(brt[:, :, GROUPS:NL],
                         moe_b_router.rearrange("l g (o e) -> o l (g e)", o=1).broadcast_to([P, 2, EXPERTS])
                         ).then_inc(route_in, 16)
            sp.dma_start(g_cq[:, :], od_g_cq[0].rearrange("(p c) -> p c", c=QR // P)).then_inc(odd_in, 16)
            sp.dma_start(g_ckv[:, :], od_g_ckv[0].rearrange("(p c) -> p c", c=1)).then_inc(odd_in, 16)
            sp.dma_start(sink[:, :], od_sink.broadcast_to([P, HEADS])).then_inc(odd_in, 16)
            sp.dma_start(cst[:, NFIRST:NCONST], const[:, NFIRST:NCONST]).then_inc(dist_in, 16)

            def load_gu(l, q, j):
                for half, w in enumerate((moe_w_gate, moe_w_up)):
                    w_e = w[l].rearrange("g e (p k) f -> (g e) p (k f)", k=KD)
                    sp.dma_start(ring_gu[:, j, half * KD * F:(half + 1) * KD * F],
                                 w_e[bass.ds(q * QUAD + j, 1), :, :].rearrange("o p f -> p (o f)")
                                 ).then_inc(gu_in[j], 16)

            def load_dn(l, q, j):
                w_e = moe_w_down[l].rearrange("g e (p c) n -> (g e) p (c n)", c=FC)
                sp.dma_start(ring_dn[:, j, :],
                             w_e[bass.ds(q * QUAD + j, 1), :, :].rearrange("o p f -> p (o f)")
                             ).then_inc(dn_in[j], 16)

            def experts(l, gu_free):
                for j in range(QUAD):
                    load_dn(l, 0, j)
                for j, (semaphore, count) in gu_free:
                    sp.wait_ge(semaphore, count)
                    load_gu(l, 0, j)
                with sp.Fori(1, QUADS) as q:
                    sp.wait_ge(M[l]["gu_used"], q)
                    for j in range(QUAD):
                        load_gu(l, q, j)
                    sp.wait_ge(M[l]["dn_used"], q)
                    for j in range(QUAD):
                        load_dn(l, q, j)
                sp.wait_ge(nq_ok, l + 1)
                n = sp.value_load(nq[0:1, l:l + 1], min_val=QUADS, max_val=QUADS * MAX_ROUNDS)
                with sp.If(n > QUADS):
                    with sp.Fori(1, n - (QUADS - 1)) as i:
                        sp.wait_ge(M[l]["gu_used"], i + (QUADS - 1))
                        e = sp.snap((i - 1) % QUADS, min_val=0, max_val=QUADS - 1)
                        for j in range(QUAD):
                            load_gu(l, e, j)
                        sp.wait_ge(M[l]["dn_used"], i + (QUADS - 1))
                        for j in range(QUAD):
                            load_dn(l, e, j)
                return n

            n0 = experts(0, ((0, (vg_done, 4)), (1, (vg_done, 4)), (3, (v_done, 2)), (2, (u_done, 2))))
            sp.wait_ge(M[0]["gu_used"], n0)
            sp.dma_start(wA, w_in1[:, :, 0:COL_A]).then_inc(gu_in[0], 32)
            sp.dma_start(wC, w_in1[:, :, COL_A + COL_B:ODD_IN]).then_inc(gu_in[2], 16)
            sp.dma_start(wuq, od_w_uq[0].rearrange("(p c) n -> p c n", c=QR // P)).then_inc(gu_in[2], 16)
            sp.dma_start(wB, w_in1[:, :, COL_A:COL_A + COL_B]).then_inc(gu_in[1], 32)
            sp.dma_start(wukv, od_w_ukv[0]).then_inc(gu_in[3], 32)
            load_w_out(w_out1)
            sp.wait_ge(M[0]["dn_used"], n0)
            experts(1, ((0, (pa_done, 2)), (1, (pb_done, 2)), (2, (q_up, 2)), (3, (kv_up, 2))))
            sp.dma_start(gfin, norm_final.rearrange("(o n) -> o n", o=1).broadcast_to([P, D])).then_inc(gfin_in, 16)
            for t in range(NT):
                sp.wait_ge(o_sem, t + 1)
                sp.dma_start(out[0, t * P:(t + 1) * P, :], xhat[:, t, :]).then_inc(stored, 16)
            sp.wait_ge(stored, 32)

        @block.gpsimd
        def _(pool):
            pool.memset(zeros[:, :], 0.0).then_inc(zeros_ok, 1)
            pool.memset(aT[:, :, 0:HALO], 0.0).then_inc(pads_done, 1)
            pool.memset(aT[:, :, HALO + SEQ:APAD], 0.0).then_inc(pads_done, 1)
            pool.memset(gl[:, :, GROUPS:8], LOW).then_inc(pads_done, 1)
            pool.wait_ge(route_in, 6 * 16)
            for l in range(2):
                pool.tensor_copy(wrt[:, l, :, 0:GROUPS], wgr[:, l, :, :]).then_inc(route_w_done, 1)
                for g in range(GROUPS):
                    pool.tensor_copy(
                        wrt[:, l, :, GROUPS + g * PER_GROUP:GROUPS + (g + 1) * PER_GROUP],
                        wrt_in[:, l, g, :].rearrange("p (k e) -> p k e", e=PER_GROUP)).then_inc(route_w_done, 1)

        @block.scalar
        def _(act):
            def norm(i):
                for t in range(NT):
                    if i == 0:
                        act.wait_ge(x_in[t], 16)
                    else:
                        act.wait_ge(x_new, 4 * i + 2 * (t - 1))
                    if t == 0 and i < 4:
                        act.wait_ge(hT_free[i][0], hT_free[i][1])
                    act.activation(junk[:, t * 512:(t + 1) * 512], X[:, t, 0:512], ACT.Square,
                                   accum_out=stat[:, i, t, 0:1]).then_inc(act_sum, 1)
                    act.wait_ge(var_done, NT * i + t + 1)
                    if i == 0:
                        act.wait_ge(const_in, 16)
                    act.activation(stat[:, i, t, 3:4], stat[:, i, t, 2:3], ACT.Sqrt, bias=eps_col).then_inc(std_done, 1)
                    if i == 4:
                        continue
                    act.wait_ge(rstd_done, NT * i + t + 1)
                    act.activation(xhat[:, t, 512:D], X[:, t, 512:D], ACT.Copy,
                                   scale=stat[:, i, t, 4:5]).then_inc(xhat_act, 1)
                if i == 4:
                    return
                if i == 0:
                    act.wait_ge(gain_in, 32)
                for t in range(NT):
                    act.wait_ge(norm_T, 4 * i + 2 * t + 2)
                    for k in range(4, KD):
                        j = act.activation(hT[:, k, t * P:(t + 1) * P], B[2 * t + 1][:, (k - 4) * P:(k - 3) * P], ACT.Copy,
                                           scale=gain[:, i, k:k + 1])
                    j.then_inc(hT_act, 1)

            def even_mixer():
                act.wait_ge(wsp_T, 1)
                act.activation(wspT[:, :, :].rearrange("p h t -> p (h t)"), B[1][:, :], ACT.Copy).then_inc(wsp_ok, 1)
                for c in range(CG):
                    act.wait_ge(vg_done, c + 1)
                    act.activation(sig[:, c, :], B[4 + c][:, SEQ:2 * SEQ], ACT.Sigmoid).then_inc(sig_done, 1)
                for t in range(NT):
                    act.wait_ge(v_done, t + 1)
                    act.activation(vt[:, t, :], B[t][:, :], ACT.Gelu_apprx_tanh).then_inc(gelu_v, 1)
                for b in range(2):
                    act.wait_ge(u_done, b + 1)
                    act.activation(uT[:, 2 * b:2 * b + 2, :].rearrange("p c s -> p (c s)"), B[2 + b][:, :],
                                   ACT.Gelu_apprx_tanh).then_inc(gelu_u, 1)
                act.wait_ge(vvar, NT)
                act.activation(vstd[:, :], vag[:, :, 1], ACT.Sqrt, bias=eps_col).then_inc(vstd_ok, 1)
                for b in range(2):
                    act.wait_ge(cen_done, b + 1)
                    act.activation(sq[:, 2 * b:2 * b + 2, :], conv[:, 2 * b:2 * b + 2, :], ACT.Square).then_inc(sq_done, 1)
                act.wait_ge(sq_done, 2)
                for b in range(2):
                    act.wait_ge(cvar_done, b + 1)
                    act.activation(sq[:, 2 * b:2 * b + 2, :].rearrange("p c s -> p (c s)"), B[2 + b][:, :],
                                   ACT.Sqrt, bias=eps_col).then_inc(cstd_ok, 1)
                for c in range(CG):
                    act.wait_ge(cn_done, c // 2 + 1)
                    act.activation(mixT[:, c, :], conv[:, c, :], ACT.Silu, scale=chanp[:, c, TAPS + 1:TAPS + 2],
                                   bias=chanp[:, c, TAPS + 2:TAPS + 3]).then_inc(silu_done, 1)

            def odd_mixer():
                for t in range(NT):
                    act.wait_ge(pa_done, t + 1)
                    act.activation(lsq[:, t, 0:QR], B[4 + t][:, 0:QR], ACT.Square,
                                   accum_out=lst[:, 0, 0, t:t + 1]).then_inc(lsum, 1)
                    act.activation(lsq[:, t, QR:QR + KVR], B[4 + t][:, QR:QR + KVR], ACT.Square,
                                   accum_out=lst[:, 0, 1, t:t + 1]).then_inc(lsum, 1)
                act.wait_ge(pc_done, 1)
                act.activation(ksvs[:, :, :].rearrange("p t n -> p (t n)"), B[0][:, :], ACT.Copy).then_inc(ks_ok, 1)
                act.wait_ge(lvar, 2)
                act.activation(lst[:, 2, :, :], lst[:, 1, :, :], ACT.Sqrt).then_inc(lstd, 1)
                for t in range(NT):
                    act.wait_ge(pb_done, t + 1)
                    act.activation(qs[:, t, :].rearrange("p (r g d) -> p g r d", g=KVH, d=SWA_D),
                                   B[6 + t][:, :].rearrange("p (g r d) -> p g r d", g=KVH, d=SWA_D), ACT.Copy).then_inc(qs_ok, 1)
                for t in range(NT):
                    act.wait_ge(q_up, t + 1)
                    for b, (h0, nh) in enumerate(((0, 5), (5, 3))):
                        src = B[4 + 2 * t + b][:, 0:nh * QK].rearrange("p (h d) -> p h d", d=QK)
                        dst = qf[:, t, h0 * QK:(h0 + nh) * QK].rearrange("p (h d) -> p h d", d=QK)
                        act.activation(dst[:, :, 0:NOPE], src[:, :, 0:NOPE], ACT.Copy).then_inc(q_nope, 1)
                for t in range(NT):
                    act.wait_ge(kv_up, t + 1)
                    for b in range(2):
                        src = B[2 * t + b][:, :].rearrange("p (h d) -> p h d", d=NOPE + VD)
                        act.activation(kf[:, t, 4 * b:4 * b + 4, 0:NOPE], src[:, :, 0:NOPE], ACT.Copy).then_inc(k_nope, 1)
                for n, (dst, rows, views) in enumerate(head_blocks):
                    if n % 2:
                        act.wait_ge(head_T, n + 1)
                        act.activation(dst, B[n % 8][0:rows, 0:len(views) * P], ACT.Copy).then_inc(headT_act, 1)
                def unit_exp(u):
                    window = u >= UNITS // 2
                    act.wait_ge(negmax, u + 1)
                    if u >= 2:
                        act.wait_ge(prob_T, u - 1)
                    for i in range(2):
                        src = sw[:, u % 2, i, :] if window else score_bank(u, i)
                        act.activation(prob[:, u % 2, i, :], src, ACT.Exp, bias=us[:, u, 1, i:i + 1],
                                       scale=SWA_SCALE if window else MLA_SCALE,
                                       accum_out=us[:, u, 2, i:i + 1]).then_inc(expd, 1)
                    if window:
                        act.wait_ge(sink_d, u - UNITS // 2 + 1)
                        act.activation(us[:, u, 3, :], us[:, u, 3, :], ACT.Exp).then_inc(sink_e, 1)

                def unit_pT(u):
                    act.wait_ge(prob_T, u + 1)
                    if u >= 2:
                        act.wait_ge(pv, u - 1)
                    act.activation(pT[:, u % 2, :, :].rearrange("p a b -> p (a b)"), B[2 + u % 2][:, :],
                                   ACT.Copy).then_inc(pT_ok, 1)

                for u in range(UNITS + 1):
                    if u < UNITS:
                        unit_exp(u)
                    if u >= 1:
                        unit_pT(u - 1)
                for b in range(1, 4, 2):
                    act.wait_ge(o_T, b + 1)
                    act.activation(mixT[:, 2 * b:2 * b + 2, :].rearrange("p c s -> p (c s)"), B[b][:, :],
                                   ACT.Copy).then_inc(oT_act, 1)

            def route(l):
                act.wait_ge(ex_in, l + 1)
                act.activation(exo[:, :, :], exin[:, :, :], ACT.Exp).then_inc(ex_out, 1)
                act.wait_ge(rows_T, 2 * l + 1)
                act.activation(wrow[:, :, :].rearrange("p a s -> p (a s)"), B[3][:, :], ACT.Copy).then_inc(rows_ok, 1)
                act.preload_act_table(ACT.Silu)
                act.wait_ge(rows_T, 2 * l + 2)
                act.activation(keyrow[:, :, :].rearrange("p a s -> p (a s)"), B[2][:, :], ACT.Copy).then_inc(rows_ok, 1)

            def experts(l):
                m = M[l]
                act.wait_ge(nq_ok, l + 1)
                n = act.value_load(nq[0:1, l:l + 1], min_val=QUADS, max_val=QUADS * MAX_ROUNDS)
                with act.Fori(0, n) as q:
                    act.wait_ge(m["gath1"], q + 1)
                    for k in range(4, KD):
                        i = act.activation(xs[:, k, :], B[1][:, (k - 4) * P:(k - 3) * P], ACT.Copy,
                                           scale=gain[:, 2 * l + 1, k:k + 1])
                    i.then_inc(m["xs1"], 1)
                    act.wait_ge(m["gu_used"], q + 1)
                    act.activation(sg[:, :], B[2][:, 0:F], ACT.Silu).then_inc(m["silu_g"], 1)
                    act.wait_ge(m["dn_used"], q + 1)
                    act.activation(ys[:, 512:1024], B[1][:, :], ACT.Copy).then_inc(m["ys1"], 1)

            norm(0)
            even_mixer()
            for l in range(2):
                if l == 1:
                    norm(2)
                    odd_mixer()
                norm(2 * l + 1)
                route(l)
                experts(l)
            norm(4)

        @block.vector
        def _(dve):
            steps = [0]

            def step(ins):
                steps[0] += 1
                ins.then_inc(dve_step, 1)
                return steps[0]

            def chain(ins):
                dve.wait_ge(dve_step, step(ins))

            def norm(i, out_counts=None):
                for t in range(NT):
                    if i == 0:
                        dve.wait_ge(x_in[t], 16)
                    for half in range(2 if i else 0):
                        if out_counts is not None:
                            dve.wait_ge(out_done, out_counts + 2 * t + half + 1)
                        v = X[:, t, half * 512:(half + 1) * 512]
                        dve.tensor_tensor(v, B[4 + 2 * t + half][:, :], v, ALU.add).then_inc(x_new, 1)
                    if i:
                        dve.wait_ge(x_new, 4 * i + 2 * (t - 1))
                    if t == 0 and i < 4:
                        dve.wait_ge(hT_free[i][0], hT_free[i][1])
                    dve.tensor_tensor_reduce(out=junk_v[:, t * 512:(t + 1) * 512], in0=X[:, t, 512:D], in1=X[:, t, 512:D],
                                             scale=1.0, scalar=0.0, op0=ALU.mult, op1=ALU.add,
                                             accum_out=stat[:, i, t, 1:2]).then_inc(dve_sum, 1)
                    dve.wait_ge(dve_sum, NT * i + t + 1)
                    dve.wait_ge(act_sum, NT * i + t + 1)
                    dve.tensor_scalar(stat[:, i, t, 2:3], stat[:, i, t, 0:1], stat[:, i, t, 1:2], 1.0 / D,
                                      ALU.add, ALU.mult).then_inc(var_done, 1)
                    dve.wait_ge(std_done, NT * i + t + 1)
                    dve.reciprocal(stat[:, i, t, 4:5], stat[:, i, t, 3:4]).then_inc(rstd_done, 1)
                    dve.wait_ge(rstd_done, NT * i + t + 1)
                    if i == 4:
                        if t == 0:
                            dve.wait_ge(gfin_in, 16)
                        dve.scalar_tensor_tensor(out=xhat[:, t, :], in0=X[:, t, :], scalar=stat[:, i, t, 4:5], in1=gfin,
                                                 op0=ALU.mult, op1=ALU.mult).then_inc(o_sem, 1)
                        continue
                    dve.tensor_scalar(xhat[:, t, 0:512], X[:, t, 0:512], stat[:, i, t, 4:5], None,
                                      ALU.mult).then_inc(xhat_dve, 1)
                if i == 4:
                    return
                if i == 0:
                    dve.wait_ge(gain_in, 32)
                for t in range(NT):
                    dve.wait_ge(norm_T, 4 * i + 2 * t + 1)
                    dve.tensor_tensor(hT[:, 0:4, t * P:(t + 1) * P], B[2 * t][:, :].rearrange("p (k s) -> p k s", s=P),
                                      gain[:, i, 0:4].unsqueeze(2).broadcast_to([P, 4, P]), ALU.mult).then_inc(hT_dve, 1)

            def even_mixer():
                dve.wait_ge(chan_T, 1)
                chain(dve.tensor_copy(chanp[:, :, :].rearrange("p c r -> p (c r)"), B[0][:, 0:CG * NROW]))
                dve.wait_ge(pads_done, 3)

                def conv_groups(groups, between=None):
                    for c in groups:
                        dve.wait_ge(sig_done, c + 1)
                        dve.tensor_tensor(aT[:, c, HALO:HALO + SEQ], B[4 + c][:, 0:SEQ], sig[:, c, :], ALU.mult).then_inc(a_done, 1)
                    dve.wait_ge(a_done, groups[-1] + 1)
                    last = {}
                    for j in range(TAPS):
                        if j == TAPS // 2 and between is not None:
                            between()
                        for c in groups:
                            src, w = aT[:, c, j:j + SEQ], chanp[:, c, j:j + 1]
                            if j == 0:
                                last[c] = step(dve.tensor_scalar(conv[:, c, :], src, w, chanp[:, c, TAPS:TAPS + 1],
                                                                 ALU.mult, ALU.add))
                                continue
                            dve.wait_ge(dve_step, last[c])
                            ins = dve.scalar_tensor_tensor(out=conv[:, c, :], in0=src, scalar=w, in1=conv[:, c, :],
                                                           op0=ALU.mult, op1=ALU.add)
                            if j < TAPS - 1:
                                last[c] = step(ins)
                            else:
                                ins.then_inc(conv_done, 1)

                def v_norm():
                    for t in range(NT):
                        dve.wait_ge(gelu_v, t + 1)
                        for h in range(CG):
                            k = step(dve.bn_stats(vst[:, t * CG + h, :], vt[:, t, h * P:(h + 1) * P]))
                        dve.wait_ge(dve_step, k)
                        for h in range(CG):
                            i = dve.bn_aggr(vag[:, t * CG + h, :], vst[:, t * CG + h, :])
                        i.then_inc(vvar, 1)
                    dve.wait_ge(vvar, NT)
                    dve.wait_ge(vstd_ok, 1)
                    chain(dve.reciprocal(vrs[:, :], vstd[:, :]))
                    for t in range(NT):
                        for h in range(CG):
                            n = t * CG + h
                            k = step(dve.tensor_scalar(vn[:, t, h * P:(h + 1) * P], vt[:, t, h * P:(h + 1) * P],
                                                       vag[:, n, 0:1], vrs[:, n:n + 1], ALU.subtract, ALU.mult))
                    dve.wait_ge(dve_step, k)
                    dve.wait_ge(vec_in, 2 * 16)
                    g_row = vgb[:, 0:1, :].broadcast_to([P, NT, CG * P])
                    b_row = vgb[:, 1:2, :].broadcast_to([P, NT, CG * P])
                    chain(dve.tensor_tensor(vn[:, :, :], vn[:, :, :], g_row, ALU.mult))
                    dve.tensor_tensor(vn[:, :, :], vn[:, :, :], b_row, ALU.add).then_inc(vn_done, 1)

                conv_groups((0, 1))
                conv_groups((2, 3), v_norm)
                dve.wait_ge(conv_done, 4)
                for b in range(2):
                    c = conv[:, 2 * b:2 * b + 2, :].rearrange("p c s -> p (c s)")
                    dve.wait_ge(mean_done, b + 1)
                    dve.tensor_tensor(c, c, B[2 + b][:, :], ALU.subtract).then_inc(cen_done, 1)
                for b in range(2):
                    dve.wait_ge(gelu_u, b + 1)
                    dve.wait_ge(sv_done, b + 1)
                    dve.tensor_tensor(mixT[:, 4 + 2 * b:6 + 2 * b, :].rearrange("p c s -> p (c s)"), B[b][:, :],
                                      uT[:, 2 * b:2 * b + 2, :].rearrange("p c s -> p (c s)"), ALU.mult).then_inc(gated, 1)
                dve.wait_ge(cen_done, 2)
                for b in range(2):
                    c = conv[:, 2 * b:2 * b + 2, :].rearrange("p c s -> p (c s)")
                    s = sq[:, 2 * b:2 * b + 2, :].rearrange("p c s -> p (c s)")
                    dve.wait_ge(cstd_ok, b + 1)
                    chain(dve.reciprocal(s, s))
                    dve.tensor_tensor(c, c, s, ALU.mult).then_inc(cn_done, 1)

            def odd_mixer():
                dve.wait_ge(odd_in, 3 * 16)
                dve.wait_ge(lsum, 4)
                dve.tensor_scalar(lst[:, 1, 0, :], lst[:, 0, 0, :], 1.0 / QR, EPS, ALU.mult, ALU.add).then_inc(lvar, 1)
                dve.tensor_scalar(lst[:, 1, 1, :], lst[:, 0, 1, :], 1.0 / KVR, EPS, ALU.mult, ALU.add).then_inc(lvar, 1)

                def rope(dst, src, n, t, first=False):
                    def tab(name):
                        a = CONST[name][0] + t * ROPE
                        return cst[:, a:a + ROPE].unsqueeze(1).broadcast_to([P, n, ROPE])
                    cos, sin = tab("cos"), tab("sin")
                    a = rt1[:, 0:n * ROPE].rearrange("p (h d) -> p h d", d=ROPE)
                    b = rt2[:, 0:n * ROPE].rearrange("p (h d) -> p h d", d=ROPE)
                    H = ROPE // 2
                    dve.wait_ge(dve_step, steps[0])
                    step(dve.tensor_tensor(a, src, cos, ALU.mult))
                    step(dve.tensor_tensor(b[:, :, 0:H], src[:, :, H:ROPE], sin[:, :, 0:H], ALU.mult))
                    chain(dve.tensor_tensor(b[:, :, H:ROPE], src[:, :, 0:H], sin[:, :, H:ROPE], ALU.mult))
                    return dve.tensor_tensor(dst, a, b, ALU.add)

                for t in range(NT):
                    step(rope(kpe[:, t:t + 1, :], B[4 + t][:, QR + KVR:COL_A].rearrange("p (h d) -> p h d", h=1), 1, t))
                dve.wait_ge(dve_step, steps[0])
                for t in range(NT):
                    dve.tensor_copy(kf[:, t, :, NOPE:QK], kpe[:, t:t + 1, :].broadcast_to([P, HEADS, ROPE])).then_inc(k_rope, 1)
                dve.wait_ge(lstd, 1)
                dve.reciprocal(lst[:, 3, :, :], lst[:, 2, :, :]).then_inc(lrs, 1)
                dve.wait_ge(lrs, 1)
                for t in range(NT):
                    dve.tensor_scalar(lat[:, t, 0:QR], B[4 + t][:, 0:QR], lst[:, 3, 0, t:t + 1], None,
                                      ALU.mult).then_inc(cq_ok, 1)
                for t in range(NT):
                    dve.tensor_scalar(lat[:, t, QR:QR + KVR], B[4 + t][:, QR:QR + KVR], lst[:, 3, 1, t:t + 1], None,
                                      ALU.mult).then_inc(ckv_ok, 1)
                dve.wait_ge(lat_T, 1)
                for c in range(QR // P):
                    dve.tensor_scalar(cqT[:, c, :], B[1][:, c * SEQ:(c + 1) * SEQ], g_cq[:, c:c + 1], None,
                                      ALU.mult).then_inc(latT_ok, 1)
                dve.wait_ge(lat_T, 2)
                dve.tensor_scalar(ckvT[:, :], B[2][:, 0:SEQ], g_ckv[:, 0:1], None, ALU.mult).then_inc(latT_ok, 1)
                for t in range(NT):
                    dve.wait_ge(q_up, t + 1)
                    for b, (h0, nh) in enumerate(((0, 5), (5, 3))):
                        src = B[4 + 2 * t + b][:, 0:nh * QK].rearrange("p (h d) -> p h d", d=QK)
                        dst = qf[:, t, h0 * QK:(h0 + nh) * QK].rearrange("p (h d) -> p h d", d=QK)
                        dve.wait_ge(q_nope, 2 * t + b + 1)
                        rope(dst[:, :, NOPE:QK], src[:, :, NOPE:QK], nh, t).then_inc(q_rope, 1)
                        dve.wait_ge(q_rope, 2 * t + b + 1)
                for t in range(NT):
                    dve.wait_ge(kv_up, t + 1)
                    for b in range(2):
                        src = B[2 * t + b][:, :].rearrange("p (h d) -> p h d", d=NOPE + VD)
                        dve.wait_ge(k_nope, 2 * t + b + 1)
                        dve.tensor_copy(vm[:, t, 4 * b:4 * b + 4, :], src[:, :, NOPE:NOPE + VD]).then_inc(v_ok, 1)
                for n, (dst, rows, views) in enumerate(head_blocks):
                    if n % 2 == 0:
                        dve.wait_ge(head_T, n + 1)
                        dve.tensor_copy(dst, B[n % 8][0:rows, 0:len(views) * P]).then_inc(headT_dve, 1)

                def unit_max(u):
                    window = u >= UNITS // 2
                    w, t = (u - UNITS // 2 if window else u) // NT, u % NT
                    dve.wait_ge(score, u + 1)
                    if window:
                        if u - UNITS // 2 >= 2:
                            dve.wait_ge(expd, 2 * (u - 1))
                        d0 = CONST["dist"][0] + t * SEQ
                        for i in range(2):
                            slope = 2.0 ** -(w + 4 * i + 1)
                            k = step(dve.scalar_tensor_tensor(out=sw[:, u % 2, i, :], in0=cst[:, d0:d0 + SEQ],
                                                              scalar=-slope / SWA_SCALE, in1=score_bank(u, i),
                                                              op0=ALU.mult, op1=ALU.add))
                        dve.wait_ge(dve_step, k)
                        i = dve.tensor_reduce(us[:, u, 0, :], sw[:, u % 2, :, :], AX, ALU.max)
                        i.then_inc(biased, 1)
                        dve.wait_ge(biased, u - UNITS // 2 + 1)
                        chain(dve.scalar_tensor_tensor(out=us[:, u, 0, :], in0=us[:, u, 0, :], scalar=SWA_SCALE,
                                                       in1=sink[:, w:HEADS:4], op0=ALU.mult, op1=ALU.max))
                        dve.tensor_scalar(us[:, u, 1, :], us[:, u, 0, :], -1.0, None, ALU.mult).then_inc(negmax, 1)
                        dve.tensor_tensor(us[:, u, 3, :], sink[:, w:HEADS:4], us[:, u, 0, :], ALU.subtract).then_inc(sink_d, 1)
                    else:
                        chain(dve.tensor_reduce(us[:, u, 0, :], B[(0, 1, 6, 7)[u % 4]][:, :].rearrange("p (i s) -> p i s", i=2), AX, ALU.max))
                        dve.tensor_scalar(us[:, u, 1, :], us[:, u, 0, :], -MLA_SCALE, None, ALU.mult).then_inc(negmax, 1)

                def unit_out(u):
                    window = u >= UNITS // 2
                    w, t = (u - UNITS // 2 if window else u) // NT, u % NT
                    dve.wait_ge(expd, 2 * u + 2)
                    total = us[:, u, 2, :]
                    if window:
                        dve.wait_ge(sink_e, u - UNITS // 2 + 1)
                        total = us[:, u, 4, :]
                        chain(dve.tensor_tensor(total, us[:, u, 2, :], us[:, u, 3, :], ALU.add))
                    chain(dve.reciprocal(us[:, u, 5, :], total))
                    if window:
                        dst = osb[:, t, HEADS * VD:D].rearrange("p (g r d) -> p g r d", g=KVH, d=SWA_D)[:, :, w, :]
                    else:
                        dst = osb[:, t, w * P:(w + 1) * P].rearrange("p (g d) -> p g d", g=2)
                    dve.wait_ge(pv, u + 1)
                    dve.tensor_tensor(dst, B[4 + u % 2][:, 0:P].rearrange("p (g d) -> p g d", g=2),
                                      us[:, u, 5, :].unsqueeze(2).broadcast_to([P, 2, VD]), ALU.mult).then_inc(o_ok, 1)

                dve.wait_ge(dist_in, 16)
                for u in range(UNITS + 2):
                    if u < UNITS:
                        unit_max(u)
                    if u >= 2:
                        unit_out(u - 2)
                for b in range(0, 4, 2):
                    dve.wait_ge(o_T, b + 1)
                    dve.tensor_copy(mixT[:, 2 * b:2 * b + 2, :].rearrange("p c s -> p (c s)"), B[b][:, :]).then_inc(oT_dve, 1)

            def route(l):
                if l == 0:
                    dve.wait_ge(route_in, 6 * 16)
                dve.wait_ge(logits, l + 1)
                L = B[0][:, 0:NT * 64].rearrange("p (t n) -> p t n", t=NT)
                step(dve.tensor_tensor(gl[:, :, 0:GROUPS], L[:, :, 0:GROUPS],
                                       brt[:, l:l + 1, 0:GROUPS].broadcast_to([P, NT, GROUPS]), ALU.add))
                chain(dve.tensor_tensor(rl[:, :, :], L[:, :, GROUPS:NL],
                                        brt[:, l:l + 1, GROUPS:NL].broadcast_to([P, NT, EXPERTS]), ALU.add))
                for t in range(NT):
                    k = step(dve.max(gm8[:, t, :], gl[:, t, :]))
                dve.wait_ge(dve_step, k)
                for t in range(NT):
                    step(dve.max_index(gi8[:, t, :], gm8[:, t, :], gl[:, t, :]))
                chain(dve.tensor_tensor(exin[:, :, 0:GROUPS], gl[:, :, 0:GROUPS],
                                        gm8[:, :, 0:1].broadcast_to([P, NT, GROUPS]), ALU.subtract))
                chain(dve.tensor_copy(gif[:, :], gi8[:, :, 0]))
                iota_g = C("iota_g").unsqueeze(1).broadcast_to([P, NT, GROUPS])
                chain(dve.tensor_tensor(goh[:, :, :], iota_g, gif[:, :].unsqueeze(2).broadcast_to([P, NT, GROUPS]),
                                        ALU.is_equal))
                for t in range(NT):
                    k = step(dve.tensor_tensor(selp[:, t, :].rearrange("p (g e) -> p g e", g=GROUPS),
                                               rl[:, t, :].rearrange("p (g e) -> p g e", g=GROUPS),
                                               goh[:, t, :].unsqueeze(2).broadcast_to([P, GROUPS, PER_GROUP]), ALU.mult))
                dve.wait_ge(dve_step, k)
                chain(dve.tensor_reduce(sel[:, :, :], selp[:, :, :].rearrange("p t (g e) -> p t e g", g=GROUPS), AX, ALU.add))
                for t in range(NT):
                    k = step(dve.max(em8[:, t, :], sel[:, t, :]))
                dve.wait_ge(dve_step, k)
                for t in range(NT):
                    step(dve.max_index(ei8[:, t, :], em8[:, t, :], sel[:, t, :]))
                dve.tensor_tensor(exin[:, :, 4], em8[:, :, 1], em8[:, :, 0], ALU.subtract).then_inc(ex_in, 1)
                dve.wait_ge(dve_step, steps[0])
                chain(dve.tensor_copy(eif[:, :, :], ei8[:, :, 0:2]))
                chain(dve.scalar_tensor_tensor(out=eid[:, :, :], in0=gif[:, :].unsqueeze(2).broadcast_to([P, NT, 2]),
                                               scalar=float(PER_GROUP), in1=eif[:, :, :], op0=ALU.mult, op1=ALU.add))
                e4 = eoh[:, :, :, :].rearrange("p t k e -> p (t k) e")
                eid4 = eid[:, :, :].rearrange("p t k -> p (t k)")
                chain(dve.tensor_tensor(e4, C("iota_e").unsqueeze(1).broadcast_to([P, NT * 2, EXPERTS]),
                                        eid4.unsqueeze(2).broadcast_to([P, NT * 2, EXPERTS]), ALU.is_equal))
                dve.tensor_tensor(member[:, :, :], eoh[:, :, 0, :], eoh[:, :, 1, :], ALU.add).then_inc(member_ok, 1)
                dve.wait_ge(ex_out, l + 1)
                step(dve.tensor_reduce(gsum[:, :], exo[:, :, 0:GROUPS], AX, ALU.add))
                chain(dve.tensor_scalar(den[:, :], exo[:, :, 4], 1.0, None, ALU.add))
                chain(dve.tensor_tensor(den2[:, :], den[:, :], gsum[:, :], ALU.mult))
                chain(dve.reciprocal(weight[:, :, 0], den2[:, :]))
                dve.tensor_tensor(weight[:, :, 1], weight[:, :, 0], exo[:, :, 4], ALU.mult).then_inc(weight_ok, 1)
                dve.wait_ge(ranks, l + 1)
                chain(dve.tensor_reduce(cmax[:, :], B[1][:, 64:64 + EXPERTS], AX, ALU.max))
                chain(dve.tensor_scalar(cge[:, :], C("steps"), cmax[:, 0:1], None, ALU.is_lt))
                chain(dve.tensor_reduce(extra[:, :], cge[:, :], AX, ALU.add))
                dve.tensor_scalar(nq[:, l:l + 1], extra[:, :], float(QUADS), float(QUADS), ALU.mult, ALU.add).then_inc(nq_ok, 1)
                for t in range(NT):
                    k = step(dve.tensor_tensor(rkp[:, t, :, :], eoh[:, t, :, :],
                                               B[1][:, t * EXPERTS:(t + 1) * EXPERTS].unsqueeze(1).broadcast_to([P, 2, EXPERTS]),
                                               ALU.mult))
                dve.wait_ge(dve_step, k)
                rank4 = rank[:, :, :].rearrange("p t k -> p (t k)")
                chain(dve.tensor_reduce(rank4, rkp[:, :, :, :].rearrange("p t k e -> p (t k) e"), AX, ALU.add))
                NS = MAX_ROUNDS - 1
                rge4 = rge[:, :, :, :].rearrange("p t k e -> p (t k) e")
                chain(dve.tensor_tensor(rge4, rank4.unsqueeze(2).broadcast_to([P, NT * 2, NS]),
                                        C("steps").unsqueeze(1).broadcast_to([P, NT * 2, NS]), ALU.is_ge))
                turn4 = turn[:, :, :].rearrange("p t k -> p (t k)")
                key04 = key0[:, :, :].rearrange("p t k -> p (t k)")
                key4 = key[:, :, :].rearrange("p t k -> p (t k)")
                chain(dve.tensor_reduce(turn4, rge4, AX, ALU.add))
                chain(dve.scalar_tensor_tensor(out=key04, in0=turn4, scalar=float(ROUND - SLOTS), in1=rank4,
                                               op0=ALU.mult, op1=ALU.add))
                dve.scalar_tensor_tensor(out=key4, in0=eid4, scalar=float(SLOTS), in1=key04,
                                         op0=ALU.mult, op1=ALU.add).then_inc(key_ok, 1)
                step(dve.tensor_copy(slot_row[:, :], C("slot_row")))
                chain(dve.tensor_copy(slot_col[:, :], C("slot_col")))
                dve.wait_ge(key_ok, l + 1)

            def experts(l):
                m = M[l]
                n = dve.value_load(nq[0:1, l:l + 1], min_val=QUADS, max_val=QUADS * MAX_ROUNDS)
                PER = 5
                with dve.Fori(0, n) as q:
                    for t in range(NT):
                        dve.tensor_scalar(pick[:, t, :], slot_row[:, :], key[:, t, 0:1], None, ALU.is_equal
                                          ).then_inc(m["moe_step"], 1)
                    for t in range(NT):
                        dve.wait_ge(m["moe_step"], q * PER + (t + 1))
                        dve.scalar_tensor_tensor(out=pick[:, t, :], in0=slot_row[:, :], scalar=key[:, t, 1:2],
                                                 in1=pick[:, t, :], op0=ALU.is_equal, op1=ALU.add).then_inc(m["pick_ok"], 1)
                    dve.wait_ge(m["gath0"], q + 1)
                    for k in range(4):
                        i = dve.tensor_scalar(xs[:, k, :], B[0][:, k * P:(k + 1) * P], gain[:, 2 * l + 1, k:k + 1],
                                              None, ALU.mult)
                    i.then_inc(m["xs0"], 1)
                    dve.wait_ge(rows_ok, 2 * l + 2)
                    dve.scalar_tensor_tensor(out=back[:, :, :].rearrange("p a s -> p (a s)"),
                                             in0=keyrow[:, :, :].rearrange("p a s -> p (a s)"), scalar=slot_col[:, 0:1],
                                             in1=wrow[:, :, :].rearrange("p a s -> p (a s)"),
                                             op0=ALU.is_equal, op1=ALU.mult).then_inc(m["moe_step"], 1)
                    dve.wait_ge(m["moe_step"], q * PER + 3)
                    dve.tensor_tensor(backs[:, :], back[:, 0, :], back[:, 1, :], ALU.add).then_inc(m["back_ok"], 1)
                    dve.tensor_scalar(slot_row[:, :], slot_row[:, :], float(P), None, ALU.add).then_inc(m["moe_step"], 1)
                    dve.tensor_scalar(slot_col[:, :], slot_col[:, :], float(P), None, ALU.add).then_inc(m["moe_step"], 1)
                    dve.wait_ge(m["silu_g"], q + 1)
                    dve.tensor_tensor(hid[:, :], B[2][:, F:2 * F], sg[:, :], ALU.mult).then_inc(m["hid_ok"], 1)
                    dve.wait_ge(m["hid_T"], q + 1)
                    dve.tensor_copy(hidT[:, :, :].rearrange("p c s -> p (c s)"), B[3][:, 0:FC * P]).then_inc(m["hidT_ok"], 1)
                    dve.wait_ge(m["down0"], q + 1)
                    dve.tensor_copy(ys[:, 0:512], B[0][:, :]).then_inc(m["ys0"], 1)
                    dve.wait_ge(m["moe_step"], q * PER + PER)
                dve.wait_ge(m["y_done"], 1)

            norm(0)
            even_mixer()
            for l in range(2):
                if l == 1:
                    norm(2)
                    odd_mixer()
                norm(2 * l + 1, out_counts=4 * l)
                route(l)
                experts(l)
            norm(4)

        @block.tensor
        def _(pe):
            def norm(i, after_first=None):
                xh = xhat[:, :, :].rearrange("p t (d k) -> p t d k", k=KD)
                for t in range(NT):
                    pe.wait_ge(xhat_dve, NT * i + t + 1)
                    pe.wait_ge(xhat_act, NT * i + t + 1)
                    for k in range(KD):
                        mm = pe.transpose(B[2 * t + k // 4][:, (k % 4) * P:(k % 4 + 1) * P], xh[:, t, :, k], ident)
                        if k % 4 == 3:
                            mm.then_inc(norm_T, 1)
                pe.wait_ge(hT_dve, NT * i + 1)
                pe.wait_ge(hT_act, NT * i + 1)
                if after_first is not None:
                    after_first()
                pe.wait_ge(hT_dve, NT * i + NT)
                pe.wait_ge(hT_act, NT * i + NT)

            def product(dst, pairs, then=None):
                for n, (a, b) in enumerate(pairs):
                    mm = pe.matmul(dst, a, b, start=n == 0, stop=n == len(pairs) - 1)
                if then is not None:
                    mm.then_inc(then, 1)

            def tok(k, t):
                return hT[:, k, t * P:(t + 1) * P]

            def even_mixer():
                for j in range(2):
                    pe.wait_ge(gu_in[j], 16)
                    for c in range(CG):
                        product(B[4 + c][:, j * SEQ:(j + 1) * SEQ],
                                [(gu_slot(j)[:, k, c * P:(c + 1) * P], hT[:, k, :]) for k in range(KD)],
                                vg_done if j else None)
                    if j == 0:
                        pe.wait_ge(even_in, 6 * 16)
                        for c in range(CG):
                            mm = pe.transpose(B[0][:, c * NROW:(c + 1) * NROW], chan_rows[:, c * P:(c + 1) * P],
                                              ident[0:NROW, 0:NROW])
                        mm.then_inc(chan_T, 1)
                        for h in range(CG):
                            mm = pe.transpose(B[1][:, h * P:(h + 1) * P], wsp[:, h, :], ident)
                        mm.then_inc(wsp_T, 1)
                pe.wait_ge(gu_in[3], 16)
                pe.wait_ge(a_done, 1)
                pe.wait_ge(wsp_ok, 1)
                for t in range(NT):
                    product(B[t][:, :], [(tok(k, t), gu_slot(3)[:, k, :]) for k in range(KD)], v_done)
                pe.wait_ge(gu_in[2], 16)
                for b in range(2):
                    for i in range(2):
                        c = 2 * b + i
                        product(B[2 + b][:, i * SEQ:(i + 1) * SEQ],
                                [(gu_slot(2)[:, k, c * P:(c + 1) * P], hT[:, k, :]) for k in range(KD)],
                                u_done if i else None)
                pe.wait_ge(vn_done, 1)
                pe.wait_ge(gelu_v, NT)
                for h in range(CG):
                    for n in range(NT):
                        dst = B[h // 2][:, (h % 2) * SEQ + n * P:(h % 2) * SEQ + (n + 1) * P]
                        pe.matmul(dst, vn[:, n, h * P:(h + 1) * P], wspT[:, h, :], start=True, stop=False)
                        mm = pe.matmul(dst, ones[0:1, :], bsp[0:1, h * P:(h + 1) * P], start=False, stop=True)
                    if h % 2:
                        mm.then_inc(sv_done, 1)
                pe.wait_ge(gelu_u, 2)
                pe.wait_ge(conv_done, 4)
                for b in range(2):
                    pe.matmul(B[2 + b][:, :], meanm, conv[:, 2 * b:2 * b + 2, :].rearrange("p c s -> p (c s)"),
                              start=True, stop=True).then_inc(mean_done, 1)
                pe.wait_ge(gated, 2)
                for j in (2, 3):
                    pe.wait_ge(wo_in[j], 16)
                pe.wait_ge(a_done, 4)
                w_out(range(4, 8), 0, True, False)
                for b in range(2):
                    pe.wait_ge(sq_done, b + 1)
                    pe.matmul(B[2 + b][:, :], meanm, sq[:, 2 * b:2 * b + 2, :].rearrange("p c s -> p (c s)"),
                              start=True, stop=True).then_inc(cvar_done, 1)
                w_out(range(4, 8), 1, True, False)
                for j in (0, 1):
                    pe.wait_ge(wo_in[j], 16)
                pe.wait_ge(silu_done, 4)
                for t in range(NT):
                    w_out(range(0, 4), t, False, True)

            def w_out(chunks, t, first, last):
                for half in range(2):
                    for kk in chunks:
                        mm = pe.matmul(B[4 + 2 * t + half][:, :], mixT[:, kk, t * P:(t + 1) * P],
                                       wout[:, kk // 2, (kk % 2) * D + half * 512:(kk % 2) * D + (half + 1) * 512],
                                       start=first and kk == chunks[0], stop=last and kk == chunks[-1])
                    if last:
                        mm.then_inc(out_done, 1)

            def odd_mixer(n0):
                pe.wait_ge(gu_in[0], n0 + 32)
                for t in range(NT):
                    product(B[4 + t][:, 0:COL_A], [(tok(k, t), wA[:, k, :]) for k in range(KD)], pa_done)
                pe.wait_ge(gu_in[2], n0 + 32)
                for t in range(NT):
                    product(B[0][:, t * COL_C:(t + 1) * COL_C], [(tok(k, t), wC[:, k, :]) for k in range(KD)],
                            pc_done if t else None)
                pe.wait_ge(gu_in[1], n0 + 32)
                for t in range(NT):
                    product(B[6 + t][:, :], [(tok(k, t), wB[:, k, :]) for k in range(KD)], pb_done)
                pe.wait_ge(cq_ok, NT)
                cq = lat[:, :, 0:QR].rearrange("p t (r c) -> p t r c", c=QR // P)
                for c in range(QR // P):
                    for t in range(NT):
                        mm = pe.transpose(B[1][:, c * SEQ + t * P:c * SEQ + (t + 1) * P], cq[:, t, :, c], ident)
                mm.then_inc(lat_T, 1)
                pe.wait_ge(ckv_ok, NT)
                for t in range(NT):
                    mm = pe.transpose(B[2][:, t * P:(t + 1) * P], lat[:, t, QR:QR + KVR], ident)
                mm.then_inc(lat_T, 1)
                pe.wait_ge(latT_ok, 2)
                for t in range(NT):
                    if t:
                        pe.wait_ge(qs_ok, NT)
                    for b, (h0, nh) in enumerate(((0, 5), (5, 3))):
                        product(B[4 + 2 * t + b][:, 0:nh * QK],
                                [(cqT[:, c, t * P:(t + 1) * P], wuq[:, c, h0 * QK:(h0 + nh) * QK]) for c in range(QR // P)],
                                q_up if b else None)
                pe.wait_ge(gu_in[3], n0 + 32)
                pe.wait_ge(latT_ok, 3)
                pe.wait_ge(ks_ok, 1)
                for t in range(NT):
                    for b in range(2):
                        product(B[2 * t + b][:, :], [(ckvT[:, t * P:(t + 1) * P], wukv[:, b * 512:(b + 1) * 512])],
                                kv_up if b else None)
                pe.wait_ge(q_nope, 4)
                pe.wait_ge(q_rope, 4)
                pe.wait_ge(k_nope, 4)
                pe.wait_ge(k_rope, 2)
                pe.wait_ge(v_ok, 4)
                for n, (dst, rows, views) in enumerate(head_blocks):
                    if n >= 8:
                        m = n - 8
                        pe.wait_ge(headT_act if m % 2 else headT_dve, m // 2 + 1)
                    for i, v in enumerate(views):
                        mm = pe.transpose(B[n % 8][0:rows, i * P:(i + 1) * P], v, ident)
                    mm.then_inc(head_T, 1)
                pe.wait_ge(headT_act, HB_ACT)
                pe.wait_ge(headT_dve, HB_DVE)

                def unit_score(u):
                    window = u >= UNITS // 2
                    w, t = (u - UNITS // 2 if window else u) // NT, u % NT
                    h = UNITS // 2
                    if u >= h + 2:
                        pe.wait_ge(biased, u - 2 - h + 1)
                    elif u >= 4:
                        pe.wait_ge(expd, 2 * (u - 4) + 2 if u < h else 2 * h)
                    for i in range(2):
                        dst = score_bank(u, i)
                        if window:
                            r = slice(64 * i, 64 * i + 64)
                            mm = pe.matmul(dst, qsT[r, w, t * P:(t + 1) * P], ksT[r, :], start=True, stop=True)
                        else:
                            mm = pe.matmul(dst, qT[0:QK, 2 * w + i, t * P:(t + 1) * P], kT[0:QK, 2 * w + i, :],
                                           start=True, stop=True)
                    mm.then_inc(score, 1)

                def unit_prob_T(u):
                    pe.wait_ge(expd, 2 * u + 2)
                    if u >= 2:
                        pe.wait_ge(pT_ok, u - 1)
                    for i in range(2):
                        for kc in range(NT):
                            mm = pe.transpose(B[2 + u % 2][:, (2 * i + kc) * P:(2 * i + kc + 1) * P],
                                              prob[:, u % 2, i, kc * P:(kc + 1) * P], ident)
                    mm.then_inc(prob_T, 1)

                def unit_out(u):
                    window = u >= UNITS // 2
                    w = (u - UNITS // 2 if window else u) // NT
                    pe.wait_ge(pT_ok, u + 1)
                    if u >= 2:
                        pe.wait_ge(o_ok, u - 1)
                    for i in range(2):
                        dst = B[4 + u % 2][:, i * VD:(i + 1) * VD]
                        product(dst, [(pT[:, u % 2, 2 * i + kc, :],
                                       ksvs[:, kc, P + i * SWA_D:P + (i + 1) * SWA_D] if window else vm[:, kc, 2 * w + i, :])
                                      for kc in range(NT)], pv if i else None)

                for u in range(UNITS + 2):
                    if u < UNITS:
                        unit_score(u)
                    if 1 <= u <= UNITS:
                        unit_prob_T(u - 1)
                    if u >= 2:
                        unit_out(u - 2)
                pe.wait_ge(o_ok, UNITS)
                for b in range(4):
                    for kk in range(2):
                        for t in range(NT):
                            mm = pe.transpose(B[b][:, kk * SEQ + t * P:kk * SEQ + (t + 1) * P],
                                              osb[:, t, (2 * b + kk) * P:(2 * b + kk + 1) * P], ident)
                    mm.then_inc(o_T, 1)
                for j in range(QUAD):
                    pe.wait_ge(wo_in[j], 32)
                pe.wait_ge(oT_act, 2)
                pe.wait_ge(oT_dve, 2)
                for t in range(NT):
                    w_out(range(0, 8), t, True, True)

            def logits_of(l, t):
                if l == 0 and t == 0:
                    pe.wait_ge(route_w_done, 10)
                product(B[0][:, t * 64:t * 64 + NL], [(tok(k, t), wrt[:, l, k, :]) for k in range(KD)],
                        logits if t else None)

            def route(l):
                for b in range(4):
                    pe.matmul(B[4 + b][:, :], zeros[:, :], cst[0:1, 0:512], start=True, stop=False)
                pe.wait_ge(member_ok, l + 1)
                product(B[1][:, 0:EXPERTS], [(before, member[:, 0, :])])
                product(B[1][:, EXPERTS:2 * EXPERTS], [(before, member[:, 1, :]), (ones, member[:, 0, :])])
                product(B[1][:, 64:64 + EXPERTS], [(ones, member[:, 0, :]), (ones, member[:, 1, :])], ranks)
                for b, cols, ready in ((3, weight, weight_ok), (2, key, key_ok)):
                    pe.wait_ge(ready, l + 1)
                    for k in range(2):
                        for t in range(NT):
                            product(B[b][:, k * SEQ + t * P:k * SEQ + (t + 1) * P],
                                    [(cols[:, t, k:k + 1].broadcast_to([P, P]), ident)],
                                    rows_T if (k, t) == (1, 1) else None)

            def experts(l, g0, d0):
                m = M[l]
                n = pe.value_load(nq[0:1, l:l + 1], min_val=QUADS, max_val=QUADS * MAX_ROUNDS)
                with pe.Fori(0, n) as q:
                    pe.wait_ge(m["pick_ok"], q * 2 + 2)
                    xh = xhat[:, :, :].rearrange("p t (d k) -> p t d k", k=KD)
                    for k in range(KD):
                        for t in range(NT):
                            mm = pe.matmul(B[k // 4][:, (k % 4) * P:(k % 4 + 1) * P], xh[:, t, :, k], pick[:, t, :],
                                           start=t == 0, stop=t == NT - 1)
                        if k == 3:
                            mm.then_inc(m["gath0"], 1)
                    mm.then_inc(m["gath1"], 1)
                    pe.wait_ge(m["xs0"], q + 1)
                    pe.wait_ge(m["xs1"], q + 1)
                    pe.wait_ge(rows_ok, 2 * l + 2)
                    for j in range(QUAD):
                        pe.wait_ge(gu_in[j], q * 32 + (g0 + 32))
                    for k in range(KD):
                        for j in range(QUAD):
                            w = ring_gu[:, j, :].rearrange("p (a k f) -> p a k f", a=2, k=KD)[:, :, k, :]
                            mm = pe.matmul(B[2][SLOTS * j:SLOTS * (j + 1), :], xs[:, k, SLOTS * j:SLOTS * (j + 1)], w,
                                           start=k == 0, stop=k == KD - 1, tile_position=(0, SLOTS * j))
                    mm.then_inc(m["gu_used"], 1)
                    pe.wait_ge(m["hid_ok"], q + 1)
                    hv = hid[:, :].rearrange("p (f c) -> p f c", c=FC)
                    for c in range(FC):
                        mm = pe.transpose(B[3][:, c * P:(c + 1) * P], hv[:, :, c], ident)
                    mm.then_inc(m["hid_T"], 1)
                    pe.wait_ge(m["hidT_ok"], q + 1)
                    for j in range(QUAD):
                        pe.wait_ge(dn_in[j], q * 16 + (d0 + 16))
                    for half in range(2):
                        for c in range(FC):
                            for j in range(QUAD):
                                mm = pe.matmul(B[half][SLOTS * j:SLOTS * (j + 1), :], hidT[:, c, SLOTS * j:SLOTS * (j + 1)],
                                               ring_dn[:, j, c * D + half * 512:c * D + (half + 1) * 512],
                                               start=c == 0, stop=c == FC - 1, tile_position=(0, SLOTS * j))
                        mm.then_inc(m["dn_used"] if half else m["down0"], 1)
                    pe.wait_ge(m["back_ok"], q + 1)
                    pe.wait_ge(m["ys0"], q + 1)
                    pe.wait_ge(m["ys1"], q + 1)
                    for half in range(2):
                        for t in range(NT):
                            pe.matmul(B[4 + 2 * t + half][:, :], backs[:, t * P:(t + 1) * P], ys[:, half * 512:(half + 1) * 512],
                                      start=False, stop=False)
                for b in range(4):
                    mm = pe.matmul(B[4 + b][:, :], zeros[:, :], cst[0:1, 0:512], start=False, stop=True)
                mm.then_inc(m["y_done"], 1)
                return n

            pe.wait_ge(const_in, 16)
            pe.wait_ge(zeros_ok, 1)
            norm(0)
            even_mixer()
            norm(1, lambda: logits_of(0, 0))
            logits_of(0, 1)
            route(0)
            n0 = experts(0, 16, 0)
            norm(2)
            odd_mixer(n0 * 32 + 16)
            norm(3, lambda: logits_of(1, 0))
            logits_of(1, 1)
            route(1)
            experts(1, n0 * 32 + 48, n0 * 16)


_INS = ['x', 'norm_mix', 'norm_ffn', 'norm_final', 'ev_w_in', 'ev_conv_w', 'ev_conv_b', 'ev_cnorm_g', 'ev_cnorm_b',
        'ev_vnorm_g', 'ev_vnorm_b', 'ev_w_sp', 'ev_b_sp', 'ev_w_out', 'od_w_in', 'od_g_cq', 'od_w_uq', 'od_g_ckv',
        'od_w_ukv', 'od_sink', 'od_w_out', 'moe_w_group', 'moe_b_group', 'moe_w_router', 'moe_b_router',
        'moe_w_gate', 'moe_w_up', 'moe_w_down']


def kernel(**inputs):
    import concourse.bacc as bacc
    from concourse.bass_utils import run_bass_kernel_spmd as run

    nc = bacc.Bacc("TRN2", target_bir_lowering=False, num_devices=1)
    arrays, args = {}, []
    for name in _INS:
        a = np.ascontiguousarray(inputs[name])
        arrays[f"in_{name}"] = a
        args.append(nc.dram_tensor(f"in_{name}", a.shape, mybir.dt.from_np(a.dtype), kind="ExternalInput").ap())
    arrays["constants"] = constants()
    args.append(nc.dram_tensor("constants", (P, NCONST), mybir.dt.float32, kind="ExternalInput").ap())
    args.append(nc.dram_tensor("out_x", (1, SEQ, D), mybir.dt.float32, kind="ExternalOutput").ap())
    program(nc, *args)
    return run(nc, [arrays], core_ids=[0]).results[0]["out_x"]
```

```python
import concourse.bass as bass
from concourse import mybir
from concourse.alu_op_type import AluOpType as ALU
from contextlib import ExitStack
import numpy as np

D, SEQ, P = 1024, 256, 128
NT = SEQ // P
KD = D // P
GROUPS, PER_GROUP, F = 4, 8, 256
EXPERTS = GROUPS * PER_GROUP
SLOTS = 32
QUAD = P // SLOTS
QUADS = EXPERTS // QUAD
ROUND = EXPERTS * SLOTS
MAX_ROUNDS = SEQ // SLOTS
FC = F // P
GU = 2 * KD * F
DN = FC * D
TAPS, CG = 31, 4
HALO = TAPS // 2
APAD = SEQ + 2 * HALO + 2
HEADS, NOPE, ROPE, VD = 8, 64, 32, 64
QK = NOPE + ROPE
QR, KVR = 256, 128
MLA_SCALE = float(QK) ** -0.5
SWA_D, KVH, WINDOW = 64, 2, 128
SWA_SCALE = float(SWA_D) ** -0.5
COL_A = QR + KVR + ROPE
COL_B = HEADS * SWA_D
COL_C = 2 * KVH * SWA_D
ODD_IN = COL_A + COL_B + COL_C
EPS = 1e-6
FAR = 1e30
LOW = -3e38
NROW = TAPS + 3

CONST = {}
_at = 0
for _n, _w in (("ident", P), ("before", P), ("ones", P), ("mean", P), ("slot_row", P), ("slot_col", 1),
               ("iota_e", EXPERTS), ("iota_g", GROUPS), ("steps", MAX_ROUNDS - 1), ("eps", 1),
               ("cos", NT * ROPE), ("sin", NT * ROPE), ("dist", NT * SEQ)):
    CONST[_n] = (_at, _at + _w)
    _at += _w
NCONST = _at
NFIRST = CONST["dist"][0]
NSCRATCH = 8320


def constants():
    c = np.zeros((P, NCONST), np.float32)

    def put(name, value):
        a, b = CONST[name]
        c[:, a:b] = np.asarray(value, np.float32).reshape(-1, b - a)

    i = np.arange(P)
    put("ident", np.eye(P))
    put("before", i[:, None] < i[None, :])
    put("ones", np.ones((P, P)))
    put("mean", np.full((P, P), 1.0 / P))
    put("slot_row", np.tile(i, (P, 1)))
    put("slot_col", i[:, None])
    put("iota_e", np.tile(np.arange(EXPERTS), (P, 1)))
    put("iota_g", np.tile(np.arange(GROUPS), (P, 1)))
    put("steps", np.tile(SLOTS * np.arange(1, MAX_ROUNDS), (P, 1)))
    put("eps", np.full((P, 1), EPS))
    inv = (np.float32(1.0) / (np.float32(10000.0) ** (np.arange(0, ROPE, 2, dtype=np.float32) / np.float32(ROPE)))).astype(np.float32)
    ang = np.arange(SEQ, dtype=np.float32)[:, None] * inv[None, :]
    ang = np.concatenate([ang, ang], axis=-1).astype(np.float32)
    sin = np.sin(ang)
    sin[:, :ROPE // 2] *= -1
    put("cos", np.cos(ang).reshape(NT, P, ROPE).transpose(1, 0, 2).reshape(P, -1))
    put("sin", sin.reshape(NT, P, ROPE).transpose(1, 0, 2).reshape(P, -1))
    dist = np.abs(np.arange(SEQ)[:, None] - np.arange(SEQ)[None, :]).astype(np.float32)
    dist[dist > WINDOW] = FAR
    put("dist", dist.reshape(NT, P, SEQ).transpose(1, 0, 2).reshape(P, -1))
    return c


def program(nc, x, norm_mix, norm_ffn, norm_final, ev_w_in, ev_conv_w, ev_conv_b, ev_cnorm_g, ev_cnorm_b,
            ev_vnorm_g, ev_vnorm_b, ev_w_sp, ev_b_sp, ev_w_out, od_w_in, od_g_cq, od_w_uq, od_g_ckv,
            od_w_ukv, od_sink, od_w_out, moe_w_group, moe_b_group, moe_w_router, moe_b_router,
            moe_w_gate, moe_w_up, moe_w_down, const, out):
    fp32, i32, u32 = mybir.dt.float32, mybir.dt.int32, mybir.dt.uint32
    ACT = mybir.ActivationFunctionType
    AX = mybir.AxisListType.X

    ctx = ExitStack()
    with ctx:
        def sb(name, shape, dt=fp32):
            return ctx.enter_context(nc.sbuf_tensor(name, shape, dt))

        def sem(name):
            return ctx.enter_context(nc.semaphore(name))

        scratch = sb("scratch", [P, NSCRATCH])
        place = [0]

        def carve(shape, dt=fp32, at=None):
            size = int(np.prod(shape[1:]))
            a = place[0] if at is None else at
            if at is None:
                place[0] += size
            assert a + size <= NSCRATCH, (a, size)
            v = scratch[0:shape[0], a:a + size]
            if dt != fp32:
                v = v.bitcast(dt)
            names = "abc"[:len(shape) - 1]
            if len(shape) > 2:
                v = v.rearrange(f"p ({' '.join(names)}) -> p {' '.join(names)}",
                                **{n: w for n, w in zip(names[1:], shape[2:])})
            return v

        ring_gu = sb("ring_gu", [P, QUAD, GU])
        ring_dn = sb("ring_dn", [P, QUAD, DN])
        wout = sb("wout", [P, QUAD, 2 * D])
        X = sb("X", [P, NT, D])
        xhat = sb("xhat", [P, NT, D])
        hT = sb("hT", [P, KD, SEQ])
        mixT = sb("mixT", [P, KD, SEQ])
        zeros = sb("zeros", [1, 512], mybir.dt.bfloat16)
        cst = sb("cst", [P, NCONST])
        gain = sb("gain", [P, 4, KD])
        gfin = mixT[:, 0:4, :].rearrange("p k s -> p (k s)")
        stat = sb("stat", [P, 5, NT, 5])
        xhat_flat = xhat[:, :, :].rearrange("p t n -> p (t n)")
        mixT_flat = mixT[:, :, :].rearrange("p k s -> p (k s)")

        def rows3(v, b, c):
            return v.rearrange("p (b c) -> p b c", b=b, c=c)


        def C(name):
            a, b = CONST[name]
            return cst[:, a:b]

        ident, before, ones, meanm = C("ident"), C("before"), C("ones"), C("mean")
        eps_col = C("eps")

        chan_rows = carve([NROW, CG * P])
        chanp = carve([P, CG, NROW])
        wsp = carve([P, CG, P])
        wspT = carve([P, CG, P])
        bsp = carve([1, CG * P])
        vgb = carve([P, 2, CG * P])
        sig = rows3(xhat_flat[:, 0:D], CG, SEQ)
        aT = carve([P, CG, APAD])
        conv = carve([P, CG, SEQ])
        junk, junk_v = (conv[:, a:a + 2, :].rearrange("p c s -> p (c s)") for a in (0, 2))
        DIAGS = 8
        PE_TAPS = 26
        diag = rows3(mixT_flat[:, 0:DIAGS * P], DIAGS, P)
        sq = sig
        uT = carve([P, CG, SEQ])
        vt = rows3(xhat_flat[:, D:2 * D], NT, CG * P)
        vn = vt
        vst = carve([P, NT * CG, 6])
        vag = carve([P, NT * CG, 2])
        vstd = carve([P, NT * CG])
        vrs = carve([P, NT * CG])
        vnb = carve([P, NT * CG])

        even_end = place[0]
        place[0] = 0
        g_cq = sb("g_cq", [P, QR // P])
        g_ckv = sb("g_ckv", [P, 1])
        sink = sb("sink", [P, HEADS])
        qs_at = place[0]
        qs = carve([P, NT, COL_B])
        ksvs = carve([P, NT, COL_C])
        lat_at = place[0]
        lat = carve([P, NT, QR + KVR])
        cqT = carve([P, QR // P, SEQ])
        lsq = lat
        kpe = carve([P, NT, ROPE])
        lst = carve([P, 4, 2, NT])
        ckvT = carve([P, SEQ])
        qf_at = place[0]
        qf = carve([P, NT, HEADS * QK])
        kf = carve([P, NT, HEADS, QK])
        vm = carve([P, NT, HEADS, VD])
        rt1 = carve([P, 5 * ROPE])
        rt2 = carve([P, 5 * ROPE])
        qT = rows3(xhat_flat, HEADS, SEQ)
        kT = hT
        qsT = carve([P, HEADS // 2, SEQ], at=lat_at)
        ksT = carve([P, SEQ])
        sw = carve([P, 2, 2, SEQ], at=qs_at)
        prob = mixT_flat[:, 0:D].rearrange("p (a b c) -> p a b c", a=2, b=2)
        pT = mixT_flat[:, D:2 * D].rearrange("p (a b c) -> p a b c", a=2, b=4)
        UNITS = 2 * NT * (HEADS // 2)
        us = carve([P, UNITS, 6, 2])
        osb = carve([P, NT, D], at=qf_at)

        place[0] = 0
        NL = GROUPS + EXPERTS
        wrt_in = carve([P, 2, GROUPS, KD * PER_GROUP], at=even_end)
        wrt = sb("wrt", [P, 2, KD, NL])
        wgr = carve([P, 2, KD, GROUPS], at=even_end + 2 * KD * EXPERTS)
        brt = sb("brt", [P, 2, NL])
        gl = sb("gl", [P, NT, 8])
        rl = carve([P, NT, EXPERTS])
        gm8 = carve([P, NT, 8])
        gi8 = carve([P, NT, 8], u32)
        em8 = carve([P, NT, 8])
        ei8 = carve([P, NT, 8], u32)
        gif = carve([P, NT])
        goh = carve([P, NT, GROUPS])
        selp = carve([P, NT, EXPERTS])
        sel = carve([P, NT, PER_GROUP])
        eif = carve([P, NT, 2])
        exin = carve([P, NT, 5])
        exo = carve([P, NT, 5])
        gsum = carve([P, NT])
        den = carve([P, NT])
        den2 = carve([P, NT])
        weight = carve([P, NT, 2])
        eid = carve([P, NT, 2])
        eoh = carve([P, NT, 2, EXPERTS])
        member = carve([P, NT, EXPERTS])
        rkp = carve([P, NT, 2, EXPERTS])
        rank = carve([P, NT, 2])
        cmax = carve([P, 1])
        cge = carve([P, MAX_ROUNDS - 1])
        extra = carve([P, 1])
        nq = sb("nq", [P, 2], i32)
        rge = carve([P, NT, 2, MAX_ROUNDS - 1])
        turn = carve([P, NT, 2])
        key0 = carve([P, NT, 2])
        key = carve([P, NT, 2])
        keyrow = carve([P, 2, SEQ])
        wrow = carve([P, 2, SEQ])
        slot_row = carve([P, P])
        slot_col = carve([P, 1])
        pick = carve([P, NT, P])
        back = carve([P, 2, SEQ])
        backs = carve([P, SEQ])
        xs = carve([P, KD, P])
        sg = carve([P, F])
        hid = carve([P, F])
        hidT = carve([P, FC, P])
        ys = carve([P, D])
        SPARE_GU, SPARE_DN = 2, 3
        spare_gu = [wout[:, 2 * j:2 * j + 2, :].rearrange("p a n -> p (a n)") for j in range(SPARE_GU)]
        assert place[0] <= NSCRATCH - DN
        spare_dn = [hT[:, :, :].rearrange("p k s -> p (k s)"), mixT_flat, carve([P, DN], at=NSCRATCH - DN)]

        B = [ctx.enter_context(nc.psum_tensor(f"B{i}", [P, 512], fp32)) for i in range(8)]

        x_in = [sem(f"x_in{t}") for t in range(NT)]
        wo_in = [sem(f"wo_in{j}") for j in range(QUAD)]
        dist_in, vec_in, weight_ok = sem("dist_in"), sem("vec_in"), sem("weight_ok")
        const_in, gain_in, even_in, odd_in, route_in, gfin_in = (
            sem(n) for n in ("const_in", "gain_in", "even_in", "odd_in", "route_in", "gfin_in"))
        gu_in = [sem(f"gu_in{j}") for j in range(QUAD)]
        dn_in = [sem(f"dn_in{j}") for j in range(QUAD)]
        spare_gu_in = [sem(f"spare_gu_in{j}") for j in range(SPARE_GU)]
        spare_dn_in = [sem(f"spare_dn_in{j}") for j in range(SPARE_DN)]
        zeros_ok = sem("zeros_ok")
        pads_done, route_w_done, route_w_part = sem("pads_done"), sem("route_w_done"), sem("route_w_part")
        act_sum, dve_sum, var_done, std_done, rstd_done = (
            sem(n) for n in ("act_sum", "dve_sum", "var_done", "std_done", "rstd_done"))
        xhat_act, xhat_dve, norm_T = sem("xhat_act"), sem("xhat_dve"), sem("norm_T")
        hT_dve, hT_act = sem("hT_dve"), sem("hT_act")
        x_new = sem("x_new")
        dve_step = sem("dve_step")
        act_step = sem("act_step")
        chan_T, wsp_T, chan_ok, wsp_ok = (sem(n) for n in ("chan_T", "wsp_T", "chan_ok", "wsp_ok"))
        vg_done, sig_done, a_done, v_done, u_done = (sem(n) for n in ("vg_done", "sig_done", "a_done", "v_done", "u_done"))
        gelu_v, gelu_u, vvar, vstd_ok, vrs_ok, v_scaled, vn_done = (
            sem(n) for n in ("gelu_v", "gelu_u", "vvar", "vstd_ok", "vrs_ok", "v_scaled", "vn_done"))
        sv_done, gated, conv_done, mean_done = (sem(n) for n in ("sv_done", "gated", "conv_done", "mean_done"))
        cen_done, sq_done, cvar_done, cstd_ok, cn_done, silu_done = (
            sem(n) for n in ("cen_done", "sq_done", "cvar_done", "cstd_ok", "cn_done", "silu_done"))
        taps_ok, diag_ok, diag_used, conv3_ok = (sem(n) for n in ("taps_ok", "diag_ok", "diag_used", "conv3_ok"))
        out_done = sem("out_done")
        pa_done, pb_done, pc_done = (sem(n) for n in ("pa_done", "pb_done", "pc_done"))
        lsum, lvar, lstd, lrs = (sem(n) for n in ("lsum", "lvar", "lstd", "lrs"))
        cq_ok, ckv_ok, lat_T, latT_ok, qs_ok, ks_ok = (
            sem(n) for n in ("cq_ok", "ckv_ok", "lat_T", "latT_ok", "qs_ok", "ks_ok"))
        q_up, kv_up, q_nope, q_rope, k_nope, v_ok, k_rope = (
            sem(n) for n in ("q_up", "kv_up", "q_nope", "q_rope", "k_nope", "v_ok", "k_rope"))
        head_T, headT_act, headT_dve = sem("head_T"), sem("headT_act"), sem("headT_dve")
        score, biased, negmax, expd, sink_d, sink_e = (
            sem(n) for n in ("score", "biased", "negmax", "expd", "sink_d", "sink_e"))
        prob_T, pT_ok, pv, o_ok, o_T, oT_act, oT_dve = (
            sem(n) for n in ("prob_T", "pT_ok", "pv", "o_ok", "o_T", "oT_act", "oT_dve"))
        logits, ex_in, ex_out, member_ok, ranks, nq_ok, key_ok, rows_T, rows_ok = (
            sem(n) for n in ("logits", "ex_in", "ex_out", "member_ok", "ranks", "nq_ok", "key_ok", "rows_T", "rows_ok"))
        M = [{n: sem(f"{n}_{l}") for n in (
            "pick_ok", "gath0", "gath1", "xs0", "xs1", "gu_used", "silu_g", "hid_ok", "hid_T", "hidT_ok",
            "down0", "dn_used", "ys0", "ys1", "back_ok", "moe_step", "y_done")} for l in range(2)]
        o_sem = sem("o_sem")
        stored = sem("stored")

        block = ctx.enter_context(nc.Block())

        w_in0 = ev_w_in[0].rearrange("(p k) (b n) -> b p k n", k=KD, b=4)
        w_out0 = ev_w_out[0].rearrange("(j c p) n -> j p c n", p=P, c=2)
        w_out1 = od_w_out[0].rearrange("(j c p) n -> j p c n", p=P, c=2)
        w_in1 = od_w_in[0].rearrange("(p k) n -> p k n", k=KD)

        def gu_slot(j):
            return ring_gu[:, j, :].rearrange("p (k n) -> p k n", k=KD)

        wA = ring_gu[:, 0, 0:KD * COL_A].rearrange("p (k n) -> p k n", k=KD)
        wB = gu_slot(1)
        wC = ring_gu[:, 2, 0:KD * COL_C].rearrange("p (k n) -> p k n", k=KD)
        UQ0 = KD * COL_C
        NUQ = HEADS * QK
        NUKV = HEADS * (NOPE + VD)
        wuq = ring_gu[:, 2, UQ0:UQ0 + QR // P * NUQ].rearrange("p (c n) -> p c n", n=NUQ)
        wukv = ring_gu[:, 3, 0:NUKV]

        head_blocks = []
        for pair in range(0, HEADS, 2):
            head_blocks.append((qT[0:QK, pair:pair + 2, :].rearrange("p h s -> p (h s)"), QK,
                                [qf[:, t, h * QK:(h + 1) * QK] for h in (pair, pair + 1) for t in range(NT)]))
            head_blocks.append((kT[0:QK, pair:pair + 2, :].rearrange("p h s -> p (h s)"), QK,
                                [kf[:, t, h, :] for h in (pair, pair + 1) for t in range(NT)]))
        for r in range(0, HEADS // KVH, 2):
            head_blocks.append((qsT[:, r:r + 2, :].rearrange("p h s -> p (h s)"), P,
                                [qs[:, t, rr * P:(rr + 1) * P] for rr in (r, r + 1) for t in range(NT)]))
        head_blocks.append((ksT[:, :], P, [ksvs[:, t, 0:P] for t in range(NT)]))
        NHB = len(head_blocks)
        HB_ACT = NHB // 2
        HB_DVE = NHB - HB_ACT

        def norm_order(i, early):
            if i == 4:
                return (("sums", 0), ("sums", 1))
            if early:
                return (("sums", 0), ("gains", 0), ("sums", 1), ("gains", 1))
            return (("sums", 0), ("sums", 1), ("gains", 0), ("gains", 1))

        def score_bank(u, i):
            if u < UNITS // 2:
                return B[(0, 1, 6, 7)[u % 4]][:, i * SEQ:(i + 1) * SEQ]
            return B[u % 2 + 6 * i][:, 0:SEQ]

        @block.sync
        def _(sp):
            for t in range(NT):
                sp.dma_start(X[:, t, :], x[0, t * P:(t + 1) * P, :]).then_inc(x_in[t], 16)
            sp.dma_start(cst[:, 0:NFIRST], const[:, 0:NFIRST]).then_inc(const_in, 16)
            sp.dma_start(gain[:, 0:4:2, :], norm_mix.rearrange("l (p k) -> p l k", k=KD)).then_inc(gain_in, 16)
            sp.dma_start(gain[:, 1:4:2, :], norm_ffn.rearrange("l (p k) -> p l k", k=KD)).then_inc(gain_in, 16)
            sp.dma_start(gu_slot(0), w_in0[0]).then_inc(gu_in[0], 16)
            sp.dma_start(chan_rows[0:TAPS, :], ev_conv_w[0]).then_inc(even_in, 16)
            for i, w in enumerate((ev_conv_b, ev_cnorm_g, ev_cnorm_b)):
                sp.dma_start(chan_rows[TAPS + i:TAPS + i + 1, :], w).then_inc(even_in, 16)
            sp.dma_start(wsp[:, :, :], ev_w_sp[0].rearrange("h t s -> t h s")).then_inc(even_in, 16)
            sp.dma_start(bsp[:, :], ev_b_sp.rearrange("a h t -> a (h t)")).then_inc(even_in, 16)
            sp.dma_start(gu_slot(1), w_in0[1]).then_inc(gu_in[1], 16)
            sp.dma_start(gu_slot(3), w_in0[3]).then_inc(gu_in[3], 16)
            sp.dma_start(vgb[:, 0, :], ev_vnorm_g.broadcast_to([P, CG * P])).then_inc(vec_in, 16)
            sp.dma_start(vgb[:, 1, :], ev_vnorm_b.broadcast_to([P, CG * P])).then_inc(vec_in, 16)
            sp.dma_start(gu_slot(2), w_in0[2]).then_inc(gu_in[2], 16)

            def load_w_out(w):
                for j in (2, 3, 0, 1):
                    sp.dma_start(wout[:, j, :].rearrange("p (c n) -> p c n", c=2), w[j]).then_inc(wo_in[j], 16)

            load_w_out(w_out0)
            for l in range(2):
                sp.dma_start(wgr[:, l, :, :], moe_w_group[l].rearrange("(p k) g -> p k g", k=KD)).then_inc(route_in, 16)
                sp.dma_start(wrt_in[:, l, :, :],
                             moe_w_router[l].rearrange("g (p k) e -> p g (k e)", k=KD)).then_inc(route_in, 16)
            sp.dma_start(brt[:, :, 0:GROUPS],
                         moe_b_group.rearrange("l (o g) -> o l g", o=1).broadcast_to([P, 2, GROUPS])).then_inc(route_in, 16)
            sp.dma_start(brt[:, :, GROUPS:NL],
                         moe_b_router.rearrange("l g (o e) -> o l (g e)", o=1).broadcast_to([P, 2, EXPERTS])
                         ).then_inc(route_in, 16)
            sp.dma_start(g_cq[:, :], od_g_cq[0].rearrange("(p c) -> p c", c=QR // P)).then_inc(odd_in, 16)
            sp.dma_start(g_ckv[:, :], od_g_ckv[0].rearrange("(p c) -> p c", c=1)).then_inc(odd_in, 16)
            sp.dma_start(sink[:, :], od_sink.broadcast_to([P, HEADS])).then_inc(odd_in, 16)
            sp.dma_start(cst[:, NFIRST:NCONST], const[:, NFIRST:NCONST]).then_inc(dist_in, 16)

            def load_gu(l, q, j, spare=False):
                slot, arrived = (spare_gu[j], spare_gu_in[j]) if spare else (ring_gu[:, j, :], gu_in[j])
                for half, w in enumerate((moe_w_gate, moe_w_up)):
                    w_e = w[l].rearrange("g e (p k) f -> (g e) p (k f)", k=KD)
                    sp.dma_start(slot[:, half * KD * F:(half + 1) * KD * F],
                                 w_e[bass.ds(q * QUAD + j, 1), :, :].rearrange("o p f -> p (o f)")
                                 ).then_inc(arrived, 16)

            def load_dn(l, q, j, spare=False):
                slot, arrived = (spare_dn[j], spare_dn_in[j]) if spare else (ring_dn[:, j, :], dn_in[j])
                w_e = moe_w_down[l].rearrange("g e (p c) n -> (g e) p (c n)", c=FC)
                sp.dma_start(slot, w_e[bass.ds(q * QUAD + j, 1), :, :].rearrange("o p f -> p (o f)")
                             ).then_inc(arrived, 16)

            def experts(l, gu_free):
                for j in range(QUAD):
                    load_dn(l, 0, j)
                for j, (semaphore, count) in gu_free:
                    sp.wait_ge(semaphore, count)
                    load_gu(l, 0, j)
                sp.wait_ge(out_done, 4 * (l + 1))
                for j in range(SPARE_GU):
                    load_gu(l, 1, j, spare=True)
                load_dn(l, 1, 1, spare=True)
                if l == 0:
                    sp.wait_ge(route_w_done, 10)
                load_dn(l, 1, 2, spare=True)
                sp.wait_ge(logits, l + 1)
                load_dn(l, 1, 0, spare=True)
                sp.wait_ge(M[l]["gu_used"], 1)
                for j in range(SPARE_GU, QUAD):
                    load_gu(l, 1, j)
                sp.wait_ge(M[l]["dn_used"], 1)
                for j in range(SPARE_DN, QUAD):
                    load_dn(l, 1, j)
                for j in range(SPARE_GU):
                    load_gu(l, 2, j)
                sp.wait_ge(M[l]["gu_used"], 2)
                for j in range(SPARE_GU, QUAD):
                    load_gu(l, 2, j)
                for j in range(SPARE_DN):
                    load_dn(l, 2, j)
                sp.wait_ge(M[l]["dn_used"], 2)
                for j in range(SPARE_DN, QUAD):
                    load_dn(l, 2, j)
                with sp.Fori(3, QUADS) as q:
                    sp.wait_ge(M[l]["gu_used"], q)
                    for j in range(QUAD):
                        load_gu(l, q, j)
                    sp.wait_ge(M[l]["dn_used"], q)
                    for j in range(QUAD):
                        load_dn(l, q, j)
                sp.wait_ge(nq_ok, l + 1)
                n = sp.value_load(nq[0:1, l:l + 1], min_val=QUADS, max_val=QUADS * MAX_ROUNDS)
                with sp.If(n > QUADS):
                    with sp.Fori(1, n - (QUADS - 1)) as i:
                        sp.wait_ge(M[l]["gu_used"], i + (QUADS - 1))
                        e = sp.snap((i - 1) % QUADS, min_val=0, max_val=QUADS - 1)
                        for j in range(QUAD):
                            load_gu(l, e, j)
                        sp.wait_ge(M[l]["dn_used"], i + (QUADS - 1))
                        for j in range(QUAD):
                            load_dn(l, e, j)
                return n

            n0 = experts(0, ((0, (vg_done, 4)), (1, (vg_done, 4)), (3, (v_done, 2)), (2, (u_done, 2))))
            sp.wait_ge(M[0]["gu_used"], n0)
            sp.dma_start(wA, w_in1[:, :, 0:COL_A]).then_inc(gu_in[0], 32)
            sp.dma_start(wC, w_in1[:, :, COL_A + COL_B:ODD_IN]).then_inc(gu_in[2], 16)
            sp.dma_start(wuq, od_w_uq[0].rearrange("(p c) n -> p c n", c=QR // P)).then_inc(gu_in[2], 16)
            sp.dma_start(wB, w_in1[:, :, COL_A:COL_A + COL_B]).then_inc(gu_in[1], 32)
            sp.dma_start(wukv, od_w_ukv[0]).then_inc(gu_in[3], 32)
            load_w_out(w_out1)
            sp.wait_ge(M[0]["dn_used"], n0)
            experts(1, ((0, (pa_done, 2)), (1, (pb_done, 2)), (2, (q_up, 2)), (3, (kv_up, 2))))
            sp.dma_start(gfin, norm_final.rearrange("(o n) -> o n", o=1).broadcast_to([P, D])).then_inc(gfin_in, 16)
            for t in range(NT):
                sp.wait_ge(o_sem, t + 1)
                sp.dma_start(out[0, t * P:(t + 1) * P, :], xhat[:, t, :]).then_inc(stored, 16)
            sp.wait_ge(stored, 32)

        @block.gpsimd
        def _(pool):
            pool.memset(zeros[:, :], 0.0).then_inc(zeros_ok, 1)
            pool.memset(aT[:, :, 0:HALO], 0.0).then_inc(pads_done, 1)
            pool.memset(aT[:, :, HALO + SEQ:APAD], 0.0).then_inc(pads_done, 1)
            pool.memset(gl[:, :, GROUPS:8], LOW).then_inc(pads_done, 1)
            pool.wait_ge(route_in, 6 * 16)
            for l in range(2):
                pool.tensor_copy(wrt[:, l, :, 0:GROUPS], wgr[:, l, :, :]).then_inc(route_w_done, 1)
                for g in range(GROUPS):
                    pool.tensor_copy(
                        wrt[:, l, :, GROUPS + g * PER_GROUP:GROUPS + (g + 1) * PER_GROUP],
                        wrt_in[:, l, g, :].rearrange("p (k e) -> p k e", e=PER_GROUP)).then_inc(route_w_done, 1)

        @block.scalar
        def _(act):
            def norm(i, early=False):
                def sums(t):
                    if i == 0:
                        act.wait_ge(x_in[t], 16)
                    else:
                        act.wait_ge(x_new, 4 * i + 2 * (t - 1))
                    act.activation(junk, X[:, t, 0:512], ACT.Square,
                                   accum_out=stat[:, i, t, 0:1]).then_inc(act_sum, 1)
                    act.wait_ge(var_done, NT * i + t + 1)
                    if i == 0:
                        act.wait_ge(const_in, 16)
                    act.activation(stat[:, i, t, 3:4], stat[:, i, t, 2:3], ACT.Sqrt, bias=eps_col).then_inc(std_done, 1)
                    if i == 4:
                        return
                    act.wait_ge(rstd_done, NT * i + t + 1)
                    act.activation(xhat[:, t, 512:D], X[:, t, 512:D], ACT.Copy,
                                   scale=stat[:, i, t, 4:5]).then_inc(xhat_act, 1)

                def gains(t):
                    if i == 0:
                        act.wait_ge(gain_in, 32)
                    act.wait_ge(norm_T, 4 * i + 2 * t + 2)
                    for k in range(4, KD):
                        j = act.activation(hT[:, k, t * P:(t + 1) * P], B[2 * t + 1][:, (k - 4) * P:(k - 3) * P], ACT.Copy,
                                           scale=gain[:, i, k:k + 1])
                    j.then_inc(hT_act, 1)

                for step_of, t in norm_order(i, early):
                    (sums if step_of == "sums" else gains)(t)

            def even_mixer():
                act.wait_ge(wsp_T, 1)
                act.activation(wspT[:, :, :].rearrange("p h t -> p (h t)"), B[1][:, :], ACT.Copy).then_inc(wsp_ok, 1)
                for c in range(CG):
                    act.wait_ge(vg_done, c + 1)
                    act.activation(sig[:, c, :], B[4 + c][:, SEQ:2 * SEQ], ACT.Sigmoid).then_inc(sig_done, 1)
                def diagonals(taps):
                    for j in taps:
                        if j >= DIAGS:
                            act.wait_ge(diag_used, j - DIAGS + 1)
                        act.activation(diag[:, j % DIAGS, :], ident, ACT.Copy, scale=chanp[:, CG - 1, j:j + 1]).then_inc(diag_ok, 1)

                act.wait_ge(taps_ok, 1)
                diagonals(range(DIAGS))
                for t in range(NT):
                    act.wait_ge(v_done, t + 1)
                    act.activation(vt[:, t, :], B[t][:, :], ACT.Gelu_apprx_tanh).then_inc(gelu_v, 1)
                diagonals(range(DIAGS, PE_TAPS))
                act.wait_ge(vvar, NT)
                act.activation(vstd[:, :], vag[:, :, 1], ACT.Sqrt, bias=eps_col).then_inc(vstd_ok, 1)
                act.wait_ge(diag_used, PE_TAPS)
                act.activation(conv[:, CG - 1, :], B[4][:, 0:SEQ], ACT.Identity,
                               bias=chanp[:, CG - 1, TAPS:TAPS + 1]).then_inc(conv3_ok, 1)
                act.wait_ge(vrs_ok, 1)
                act.wait_ge(gelu_v, NT)
                for t in range(NT):
                    for h in range(CG):
                        n = t * CG + h
                        i = act.activation(vn[:, t, h * P:(h + 1) * P], vt[:, t, h * P:(h + 1) * P], ACT.Identity,
                                           scale=vrs[:, n:n + 1], bias=vnb[:, n:n + 1])
                    i.then_inc(v_scaled, 1)
                def conv_roots(b):
                    act.wait_ge(cen_done, b + 1)
                    act.activation(sq[:, 2 * b:2 * b + 2, :], conv[:, 2 * b:2 * b + 2, :], ACT.Square).then_inc(sq_done, 1)
                    act.wait_ge(sq_done, b + 1)
                    act.wait_ge(cvar_done, b + 1)
                    act.activation(sq[:, 2 * b:2 * b + 2, :].rearrange("p c s -> p (c s)"), B[6 + b][:, :],
                                   ACT.Sqrt, bias=eps_col).then_inc(cstd_ok, 1)

                conv_roots(0)
                for b in range(2):
                    act.wait_ge(u_done, b + 1)
                    act.activation(uT[:, 2 * b:2 * b + 2, :].rearrange("p c s -> p (c s)"), B[2 + b][:, :],
                                   ACT.Gelu_apprx_tanh).then_inc(gelu_u, 1)
                act.preload_act_table(ACT.Sqrt)
                conv_roots(1)
                act.preload_act_table(ACT.Silu)
                for c in range(CG):
                    act.wait_ge(cn_done, c // 2 + 1)
                    act.activation(mixT[:, c, :], conv[:, c, :], ACT.Silu, scale=chanp[:, c, TAPS + 1:TAPS + 2],
                                   bias=chanp[:, c, TAPS + 2:TAPS + 3]).then_inc(silu_done, 1)
                act.preload_act_table(ACT.Sqrt)

            def odd_mixer():
                for t in range(NT):
                    act.wait_ge(pa_done, t + 1)
                    act.activation(lsq[:, t, 0:QR], B[4 + t][:, 0:QR], ACT.Square,
                                   accum_out=lst[:, 0, 0, t:t + 1]).then_inc(lsum, 1)
                    act.activation(lsq[:, t, QR:QR + KVR], B[4 + t][:, QR:QR + KVR], ACT.Square,
                                   accum_out=lst[:, 0, 1, t:t + 1]).then_inc(lsum, 1)
                act.wait_ge(pc_done, 1)
                act.activation(ksvs[:, :, :].rearrange("p t n -> p (t n)"), B[0][:, :], ACT.Copy).then_inc(ks_ok, 1)
                act.wait_ge(lvar, 2)
                act.activation(lst[:, 2, :, :], lst[:, 1, :, :], ACT.Sqrt).then_inc(lstd, 1)
                for t in range(NT):
                    act.wait_ge(pb_done, t + 1)
                    act.activation(qs[:, t, :].rearrange("p (r g d) -> p g r d", g=KVH, d=SWA_D),
                                   B[6 + t][:, :].rearrange("p (g r d) -> p g r d", g=KVH, d=SWA_D), ACT.Copy).then_inc(qs_ok, 1)
                for t in range(NT):
                    act.wait_ge(q_up, t + 1)
                    for b, (h0, nh) in enumerate(((0, 5), (5, 3))):
                        src = B[4 + 2 * t + b][:, 0:nh * QK].rearrange("p (h d) -> p h d", d=QK)
                        dst = qf[:, t, h0 * QK:(h0 + nh) * QK].rearrange("p (h d) -> p h d", d=QK)
                        act.activation(dst[:, :, 0:NOPE], src[:, :, 0:NOPE], ACT.Copy).then_inc(q_nope, 1)
                for t in range(NT):
                    act.wait_ge(kv_up, t + 1)
                    for b in range(2):
                        src = B[2 * t + b][:, :].rearrange("p (h d) -> p h d", d=NOPE + VD)
                        act.activation(kf[:, t, 4 * b:4 * b + 4, 0:NOPE], src[:, :, 0:NOPE], ACT.Copy).then_inc(k_nope, 1)
                for n, (dst, rows, views) in enumerate(head_blocks):
                    if n % 2:
                        act.wait_ge(head_T, n + 1)
                        act.activation(dst, B[n % 8][0:rows, 0:len(views) * P], ACT.Copy).then_inc(headT_act, 1)
                def unit_exp(u):
                    window = u >= UNITS // 2
                    act.wait_ge(negmax, u + 1)
                    if u >= 2:
                        act.wait_ge(prob_T, u - 1)
                    for i in range(2):
                        src = sw[:, u % 2, i, :] if window else score_bank(u, i)
                        act.activation(prob[:, u % 2, i, :], src, ACT.Exp, bias=us[:, u, 1, i:i + 1],
                                       scale=SWA_SCALE if window else MLA_SCALE,
                                       accum_out=us[:, u, 2, i:i + 1]).then_inc(expd, 1)
                    if window:
                        act.wait_ge(sink_d, u - UNITS // 2 + 1)
                        act.activation(us[:, u, 3, :], us[:, u, 3, :], ACT.Exp).then_inc(sink_e, 1)

                def unit_pT(u):
                    act.wait_ge(prob_T, u + 1)
                    if u >= 2:
                        act.wait_ge(pv, u - 1)
                    act.activation(pT[:, u % 2, :, :].rearrange("p a b -> p (a b)"), B[2 + u % 2][:, :],
                                   ACT.Copy).then_inc(pT_ok, 1)

                for u in range(UNITS + 2):
                    if u >= 2:
                        unit_pT(u - 2)
                    if u < UNITS:
                        unit_exp(u)
                for b in range(1, 4, 2):
                    act.wait_ge(o_T, b + 1)
                    act.activation(mixT[:, 2 * b:2 * b + 2, :].rearrange("p c s -> p (c s)"), B[b][:, :],
                                   ACT.Copy).then_inc(oT_act, 1)
                act.preload_act_table(ACT.Sqrt)

            def route(l):
                act.preload_act_table(ACT.Exp)
                act.wait_ge(ex_in, l + 1)
                act.activation(exo[:, :, :], exin[:, :, :], ACT.Exp).then_inc(ex_out, 1)
                act.wait_ge(rows_T, 2 * l + 1)
                act.activation(wrow[:, :, :].rearrange("p a s -> p (a s)"), B[3][:, :], ACT.Copy).then_inc(rows_ok, 1)
                act.preload_act_table(ACT.Silu)
                act.wait_ge(rows_T, 2 * l + 2)
                act.activation(keyrow[:, :, :].rearrange("p a s -> p (a s)"), B[2][:, :], ACT.Copy).then_inc(rows_ok, 1)

            def experts(l):
                m = M[l]
                act.wait_ge(nq_ok, l + 1)
                n = act.value_load(nq[0:1, l:l + 1], min_val=QUADS, max_val=QUADS * MAX_ROUNDS)
                with act.Fori(0, n) as q:
                    act.wait_ge(m["gath1"], q + 1)
                    for k in range(4, KD):
                        i = act.activation(xs[:, k, :], B[1][:, (k - 4) * P:(k - 3) * P], ACT.Copy,
                                           scale=gain[:, 2 * l + 1, k:k + 1])
                    i.then_inc(m["xs1"], 1)
                    act.wait_ge(m["gu_used"], q + 1)
                    act.activation(sg[:, :], B[2][:, 0:F], ACT.Silu).then_inc(m["silu_g"], 1)
                    act.wait_ge(m["dn_used"], q + 1)
                    act.activation(ys[:, 512:1024], B[1][:, :], ACT.Copy).then_inc(m["ys1"], 1)
                act.preload_act_table(ACT.Sqrt)

            act.preload_act_table(ACT.Sqrt)
            norm(0)
            even_mixer()
            for l in range(2):
                if l == 1:
                    norm(2)
                    odd_mixer()
                norm(2 * l + 1, early=True)
                route(l)
                experts(l)
            norm(4)

        @block.vector
        def _(dve):
            steps = [0]

            def step(ins):
                steps[0] += 1
                ins.then_inc(dve_step, 1)
                return steps[0]

            def chain(ins):
                dve.wait_ge(dve_step, step(ins))

            def norm(i, out_counts=None):
                def residual(t, half):
                    if i == 0:
                        return
                    if out_counts is not None:
                        dve.wait_ge(out_done, out_counts + 2 * t + half + 1)
                    v = X[:, t, half * 512:(half + 1) * 512]
                    dve.tensor_tensor(v, B[4 + 2 * t + half][:, :], v, ALU.add).then_inc(x_new, 1)

                def sums(t):
                    if i == 0:
                        dve.wait_ge(x_in[t], 16)
                    if t == 0 or out_counts is None:
                        residual(t, 0)
                    residual(t, 1)
                    if i:
                        dve.wait_ge(x_new, 4 * i + 2 * (t - 1))
                    dve.tensor_tensor_reduce(out=junk_v, in0=X[:, t, 512:D], in1=X[:, t, 512:D],
                                             scale=1.0, scalar=0.0, op0=ALU.mult, op1=ALU.add,
                                             accum_out=stat[:, i, t, 1:2]).then_inc(dve_sum, 1)
                    dve.wait_ge(dve_sum, NT * i + t + 1)
                    dve.wait_ge(act_sum, NT * i + t + 1)
                    dve.tensor_scalar(stat[:, i, t, 2:3], stat[:, i, t, 0:1], stat[:, i, t, 1:2], 1.0 / D,
                                      ALU.add, ALU.mult).then_inc(var_done, 1)
                    dve.wait_ge(std_done, NT * i + t + 1)
                    dve.reciprocal(stat[:, i, t, 4:5], stat[:, i, t, 3:4]).then_inc(rstd_done, 1)
                    dve.wait_ge(rstd_done, NT * i + t + 1)
                    if i == 4:
                        if t == 0:
                            dve.wait_ge(gfin_in, 16)
                        dve.scalar_tensor_tensor(out=xhat[:, t, :], in0=X[:, t, :], scalar=stat[:, i, t, 4:5], in1=gfin,
                                                 op0=ALU.mult, op1=ALU.mult).then_inc(o_sem, 1)
                        return
                    dve.tensor_scalar(xhat[:, t, 0:512], X[:, t, 0:512], stat[:, i, t, 4:5], None,
                                      ALU.mult).then_inc(xhat_dve, 1)
                    if t == 0 and out_counts is not None:
                        residual(1, 0)

                def gains(t):
                    if i == 0:
                        dve.wait_ge(gain_in, 32)
                    dve.wait_ge(norm_T, 4 * i + 2 * t + 1)
                    dve.tensor_tensor(hT[:, 0:4, t * P:(t + 1) * P], B[2 * t][:, :].rearrange("p (k s) -> p k s", s=P),
                                      gain[:, i, 0:4].unsqueeze(2).broadcast_to([P, 4, P]), ALU.mult).then_inc(hT_dve, 1)

                for step_of, t in norm_order(i, out_counts is not None):
                    (sums if step_of == "sums" else gains)(t)

            def even_mixer():
                dve.wait_ge(chan_T, 1)
                dve.tensor_copy(chanp[:, :, :].rearrange("p c r -> p (c r)"), B[0][:, 0:CG * NROW]).then_inc(taps_ok, 1)
                dve.wait_ge(taps_ok, 1)
                dve.wait_ge(pads_done, 3)

                def gate_value(c):
                    dve.wait_ge(sig_done, c + 1)
                    dve.tensor_tensor(aT[:, c, HALO:HALO + SEQ], B[4 + c][:, 0:SEQ], sig[:, c, :], ALU.mult).then_inc(a_done, 1)

                last = {}

                def tap(c, j):
                    src, w = aT[:, c, j:j + SEQ], chanp[:, c, j:j + 1]
                    if j == 0:
                        last[c] = step(dve.tensor_scalar(conv[:, c, :], src, w, chanp[:, c, TAPS:TAPS + 1],
                                                         ALU.mult, ALU.add))
                        return
                    if c == CG - 1 and j == PE_TAPS:
                        dve.wait_ge(conv3_ok, 1)
                    else:
                        dve.wait_ge(dve_step, last[c])
                    ins = dve.scalar_tensor_tensor(out=conv[:, c, :], in0=src, scalar=w, in1=conv[:, c, :],
                                                   op0=ALU.mult, op1=ALU.add)
                    if j < TAPS - 1:
                        last[c] = step(ins)
                    else:
                        ins.then_inc(conv_done, 1)

                def v_stats():
                    for t in range(NT):
                        dve.wait_ge(gelu_v, t + 1)
                        for h in range(CG):
                            k = step(dve.bn_stats(vst[:, t * CG + h, :], vt[:, t, h * P:(h + 1) * P]))
                        dve.wait_ge(dve_step, k)
                        for h in range(CG):
                            i = dve.bn_aggr(vag[:, t * CG + h, :], vst[:, t * CG + h, :])
                        i.then_inc(vvar, 1)

                AHEAD = 6
                gate_value(0)
                gate_value(1)
                dve.wait_ge(a_done, 2)
                for j in range(AHEAD):
                    tap(0, j)
                    tap(1, j)
                gate_value(2)
                gate_value(3)
                dve.wait_ge(a_done, 4)
                LATE, STATS_AT = 12, 20
                for j in range(AHEAD, TAPS):
                    tap(0, j)
                    tap(1, j)
                    if j >= LATE:
                        tap(2, j - LATE)
                    if j == STATS_AT:
                        v_stats()
                dve.wait_ge(vvar, NT)
                dve.wait_ge(vstd_ok, 1)
                k = step(dve.reciprocal(vrs[:, :], vstd[:, :]))
                tap(2, TAPS - LATE)
                dve.wait_ge(dve_step, k)
                dve.scalar_tensor_tensor(out=vnb[:, :], in0=vag[:, :, 0], scalar=-1.0, in1=vrs[:, :],
                                         op0=ALU.mult, op1=ALU.mult).then_inc(vrs_ok, 1)
                for j in range(TAPS - LATE + 1, TAPS - 5):
                    tap(2, j)
                    if j > TAPS - 5 - (TAPS - PE_TAPS) - 1:
                        tap(3, j + 5)
                dve.wait_ge(v_scaled, NT)
                dve.wait_ge(vec_in, 2 * 16)
                k = step(dve.tensor_tensor(vn[:, :, :], vn[:, :, :], vgb[:, 0:1, :].broadcast_to([P, NT, CG * P]), ALU.mult))
                tap(2, TAPS - 5)
                dve.wait_ge(dve_step, k)
                dve.tensor_tensor(vn[:, :, :], vn[:, :, :], vgb[:, 1:2, :].broadcast_to([P, NT, CG * P]), ALU.add
                                  ).then_inc(vn_done, 1)
                tap(2, TAPS - 4)

                def centre(b):
                    c = conv[:, 2 * b:2 * b + 2, :].rearrange("p c s -> p (c s)")
                    dve.wait_ge(mean_done, b + 1)
                    dve.tensor_tensor(c, c, B[6 + b][:, :], ALU.subtract).then_inc(cen_done, 1)

                def roots(b):
                    s = sq[:, 2 * b:2 * b + 2, :].rearrange("p c s -> p (c s)")
                    dve.wait_ge(cstd_ok, b + 1)
                    return step(dve.reciprocal(s, s))

                def scale(b, k):
                    c = conv[:, 2 * b:2 * b + 2, :].rearrange("p c s -> p (c s)")
                    s = sq[:, 2 * b:2 * b + 2, :].rearrange("p c s -> p (c s)")
                    dve.wait_ge(dve_step, k)
                    dve.wait_ge(cen_done, b + 1)
                    dve.tensor_tensor(c, c, s, ALU.mult).then_inc(cn_done, 1)

                dve.wait_ge(conv_done, 2)
                centre(0)
                for j in range(TAPS - 3, TAPS):
                    tap(2, j)
                scale(0, roots(0))
                dve.wait_ge(conv_done, 4)
                centre(1)
                for b in range(2):
                    dve.wait_ge(gelu_u, b + 1)
                    dve.wait_ge(sv_done, b + 1)
                    dve.tensor_tensor(mixT[:, 4 + 2 * b:6 + 2 * b, :].rearrange("p c s -> p (c s)"), B[b][:, :],
                                      uT[:, 2 * b:2 * b + 2, :].rearrange("p c s -> p (c s)"), ALU.mult).then_inc(gated, 1)
                scale(1, roots(1))

            def odd_mixer():
                dve.wait_ge(odd_in, 3 * 16)
                dve.wait_ge(lsum, 4)
                dve.tensor_scalar(lst[:, 1, 0, :], lst[:, 0, 0, :], 1.0 / QR, EPS, ALU.mult, ALU.add).then_inc(lvar, 1)
                dve.tensor_scalar(lst[:, 1, 1, :], lst[:, 0, 1, :], 1.0 / KVR, EPS, ALU.mult, ALU.add).then_inc(lvar, 1)

                def rope(dst, src, n, t, first=False):
                    def tab(name):
                        a = CONST[name][0] + t * ROPE
                        return cst[:, a:a + ROPE].unsqueeze(1).broadcast_to([P, n, ROPE])
                    cos, sin = tab("cos"), tab("sin")
                    a = rt1[:, 0:n * ROPE].rearrange("p (h d) -> p h d", d=ROPE)
                    b = rt2[:, 0:n * ROPE].rearrange("p (h d) -> p h d", d=ROPE)
                    H = ROPE // 2
                    dve.wait_ge(dve_step, steps[0])
                    step(dve.tensor_tensor(a, src, cos, ALU.mult))
                    step(dve.tensor_tensor(b[:, :, 0:H], src[:, :, H:ROPE], sin[:, :, 0:H], ALU.mult))
                    chain(dve.tensor_tensor(b[:, :, H:ROPE], src[:, :, 0:H], sin[:, :, H:ROPE], ALU.mult))
                    return dve.tensor_tensor(dst, a, b, ALU.add)

                for t in range(NT):
                    step(rope(kpe[:, t:t + 1, :], B[4 + t][:, QR + KVR:COL_A].rearrange("p (h d) -> p h d", h=1), 1, t))
                dve.wait_ge(dve_step, steps[0])
                for t in range(NT):
                    dve.tensor_copy(kf[:, t, :, NOPE:QK], kpe[:, t:t + 1, :].broadcast_to([P, HEADS, ROPE])).then_inc(k_rope, 1)
                dve.wait_ge(lstd, 1)
                dve.reciprocal(lst[:, 3, :, :], lst[:, 2, :, :]).then_inc(lrs, 1)
                dve.wait_ge(lrs, 1)
                for t in range(NT):
                    dve.tensor_scalar(lat[:, t, 0:QR], B[4 + t][:, 0:QR], lst[:, 3, 0, t:t + 1], None,
                                      ALU.mult).then_inc(cq_ok, 1)
                for t in range(NT):
                    dve.tensor_scalar(lat[:, t, QR:QR + KVR], B[4 + t][:, QR:QR + KVR], lst[:, 3, 1, t:t + 1], None,
                                      ALU.mult).then_inc(ckv_ok, 1)
                dve.wait_ge(lat_T, 1)
                for c in range(QR // P):
                    dve.tensor_scalar(cqT[:, c, :], B[1][:, c * SEQ:(c + 1) * SEQ], g_cq[:, c:c + 1], None,
                                      ALU.mult).then_inc(latT_ok, 1)
                dve.wait_ge(lat_T, 2)
                dve.tensor_scalar(ckvT[:, :], B[2][:, 0:SEQ], g_ckv[:, 0:1], None, ALU.mult).then_inc(latT_ok, 1)
                for t in range(NT):
                    dve.wait_ge(q_up, t + 1)
                    for b, (h0, nh) in enumerate(((0, 5), (5, 3))):
                        src = B[4 + 2 * t + b][:, 0:nh * QK].rearrange("p (h d) -> p h d", d=QK)
                        dst = qf[:, t, h0 * QK:(h0 + nh) * QK].rearrange("p (h d) -> p h d", d=QK)
                        dve.wait_ge(q_nope, 2 * t + b + 1)
                        rope(dst[:, :, NOPE:QK], src[:, :, NOPE:QK], nh, t).then_inc(q_rope, 1)
                        dve.wait_ge(q_rope, 2 * t + b + 1)
                for t in range(NT):
                    dve.wait_ge(kv_up, t + 1)
                    for b in range(2):
                        src = B[2 * t + b][:, :].rearrange("p (h d) -> p h d", d=NOPE + VD)
                        dve.wait_ge(k_nope, 2 * t + b + 1)
                        dve.tensor_copy(vm[:, t, 4 * b:4 * b + 4, :], src[:, :, NOPE:NOPE + VD]).then_inc(v_ok, 1)
                for n, (dst, rows, views) in enumerate(head_blocks):
                    if n % 2 == 0:
                        dve.wait_ge(head_T, n + 1)
                        dve.tensor_copy(dst, B[n % 8][0:rows, 0:len(views) * P]).then_inc(headT_dve, 1)

                def unit_max(u):
                    window = u >= UNITS // 2
                    w, t = (u - UNITS // 2 if window else u) // NT, u % NT
                    dve.wait_ge(score, u + 1)
                    if window:
                        if u - UNITS // 2 >= 2:
                            dve.wait_ge(expd, 2 * (u - 1))
                        d0 = CONST["dist"][0] + t * SEQ
                        for i in range(2):
                            slope = 2.0 ** -(w + 4 * i + 1)
                            k = step(dve.scalar_tensor_tensor(out=sw[:, u % 2, i, :], in0=cst[:, d0:d0 + SEQ],
                                                              scalar=-slope / SWA_SCALE, in1=score_bank(u, i),
                                                              op0=ALU.mult, op1=ALU.add))
                        dve.wait_ge(dve_step, k)
                        i = dve.tensor_reduce(us[:, u, 0, :], sw[:, u % 2, :, :], AX, ALU.max)
                        i.then_inc(biased, 1)
                        dve.wait_ge(biased, u - UNITS // 2 + 1)
                        chain(dve.scalar_tensor_tensor(out=us[:, u, 0, :], in0=us[:, u, 0, :], scalar=SWA_SCALE,
                                                       in1=sink[:, w:HEADS:4], op0=ALU.mult, op1=ALU.max))
                        dve.tensor_scalar(us[:, u, 1, :], us[:, u, 0, :], -1.0, None, ALU.mult).then_inc(negmax, 1)
                        dve.tensor_tensor(us[:, u, 3, :], sink[:, w:HEADS:4], us[:, u, 0, :], ALU.subtract).then_inc(sink_d, 1)
                    else:
                        chain(dve.tensor_reduce(us[:, u, 0, :], B[(0, 1, 6, 7)[u % 4]][:, :].rearrange("p (i s) -> p i s", i=2), AX, ALU.max))
                        dve.tensor_scalar(us[:, u, 1, :], us[:, u, 0, :], -MLA_SCALE, None, ALU.mult).then_inc(negmax, 1)

                def unit_out(u):
                    window = u >= UNITS // 2
                    w, t = (u - UNITS // 2 if window else u) // NT, u % NT
                    dve.wait_ge(expd, 2 * u + 2)
                    total = us[:, u, 2, :]
                    if window:
                        dve.wait_ge(sink_e, u - UNITS // 2 + 1)
                        total = us[:, u, 4, :]
                        chain(dve.tensor_tensor(total, us[:, u, 2, :], us[:, u, 3, :], ALU.add))
                    chain(dve.reciprocal(us[:, u, 5, :], total))
                    if window:
                        dst = osb[:, t, HEADS * VD:D].rearrange("p (g r d) -> p g r d", g=KVH, d=SWA_D)[:, :, w, :]
                    else:
                        dst = osb[:, t, w * P:(w + 1) * P].rearrange("p (g d) -> p g d", g=2)
                    dve.wait_ge(pv, u + 1)
                    dve.tensor_tensor(dst, B[4 + u % 2][:, 0:P].rearrange("p (g d) -> p g d", g=2),
                                      us[:, u, 5, :].unsqueeze(2).broadcast_to([P, 2, VD]), ALU.mult).then_inc(o_ok, 1)

                dve.wait_ge(dist_in, 16)
                for u in range(UNITS + 3):
                    if u < UNITS:
                        unit_max(u)
                    if u >= 3:
                        unit_out(u - 3)
                for b in range(0, 4, 2):
                    dve.wait_ge(o_T, b + 1)
                    dve.tensor_copy(mixT[:, 2 * b:2 * b + 2, :].rearrange("p c s -> p (c s)"), B[b][:, :]).then_inc(oT_dve, 1)

            def route(l):
                if l == 0:
                    dve.wait_ge(route_in, 6 * 16)
                dve.wait_ge(logits, l + 1)
                L = B[0][:, 0:NT * 64].rearrange("p (t n) -> p t n", t=NT)
                step(dve.tensor_tensor(gl[:, :, 0:GROUPS], L[:, :, 0:GROUPS],
                                       brt[:, l:l + 1, 0:GROUPS].broadcast_to([P, NT, GROUPS]), ALU.add))
                chain(dve.tensor_tensor(rl[:, :, :], L[:, :, GROUPS:NL],
                                        brt[:, l:l + 1, GROUPS:NL].broadcast_to([P, NT, EXPERTS]), ALU.add))
                for t in range(NT):
                    k = step(dve.max(gm8[:, t, :], gl[:, t, :]))
                dve.wait_ge(dve_step, k)
                for t in range(NT):
                    step(dve.max_index(gi8[:, t, :], gm8[:, t, :], gl[:, t, :]))
                chain(dve.tensor_tensor(exin[:, :, 0:GROUPS], gl[:, :, 0:GROUPS],
                                        gm8[:, :, 0:1].broadcast_to([P, NT, GROUPS]), ALU.subtract))
                chain(dve.tensor_copy(gif[:, :], gi8[:, :, 0]))
                iota_g = C("iota_g").unsqueeze(1).broadcast_to([P, NT, GROUPS])
                chain(dve.tensor_tensor(goh[:, :, :], iota_g, gif[:, :].unsqueeze(2).broadcast_to([P, NT, GROUPS]),
                                        ALU.is_equal))
                for t in range(NT):
                    k = step(dve.tensor_tensor(selp[:, t, :].rearrange("p (g e) -> p g e", g=GROUPS),
                                               rl[:, t, :].rearrange("p (g e) -> p g e", g=GROUPS),
                                               goh[:, t, :].unsqueeze(2).broadcast_to([P, GROUPS, PER_GROUP]), ALU.mult))
                dve.wait_ge(dve_step, k)
                chain(dve.tensor_reduce(sel[:, :, :], selp[:, :, :].rearrange("p t (g e) -> p t e g", g=GROUPS), AX, ALU.add))
                for t in range(NT):
                    k = step(dve.max(em8[:, t, :], sel[:, t, :]))
                dve.wait_ge(dve_step, k)
                for t in range(NT):
                    step(dve.max_index(ei8[:, t, :], em8[:, t, :], sel[:, t, :]))
                dve.tensor_tensor(exin[:, :, 4], em8[:, :, 1], em8[:, :, 0], ALU.subtract).then_inc(ex_in, 1)
                dve.wait_ge(dve_step, steps[0])
                chain(dve.tensor_copy(eif[:, :, :], ei8[:, :, 0:2]))
                chain(dve.scalar_tensor_tensor(out=eid[:, :, :], in0=gif[:, :].unsqueeze(2).broadcast_to([P, NT, 2]),
                                               scalar=float(PER_GROUP), in1=eif[:, :, :], op0=ALU.mult, op1=ALU.add))
                e4 = eoh[:, :, :, :].rearrange("p t k e -> p (t k) e")
                eid4 = eid[:, :, :].rearrange("p t k -> p (t k)")
                chain(dve.tensor_tensor(e4, C("iota_e").unsqueeze(1).broadcast_to([P, NT * 2, EXPERTS]),
                                        eid4.unsqueeze(2).broadcast_to([P, NT * 2, EXPERTS]), ALU.is_equal))
                dve.tensor_tensor(member[:, :, :], eoh[:, :, 0, :], eoh[:, :, 1, :], ALU.add).then_inc(member_ok, 1)
                dve.wait_ge(ex_out, l + 1)
                step(dve.tensor_reduce(gsum[:, :], exo[:, :, 0:GROUPS], AX, ALU.add))
                chain(dve.tensor_scalar(den[:, :], exo[:, :, 4], 1.0, None, ALU.add))
                chain(dve.tensor_tensor(den2[:, :], den[:, :], gsum[:, :], ALU.mult))
                chain(dve.reciprocal(weight[:, :, 0], den2[:, :]))
                dve.tensor_tensor(weight[:, :, 1], weight[:, :, 0], exo[:, :, 4], ALU.mult).then_inc(weight_ok, 1)
                dve.wait_ge(ranks, l + 1)
                chain(dve.tensor_reduce(cmax[:, :], B[1][:, 64:64 + EXPERTS], AX, ALU.max))
                chain(dve.tensor_scalar(cge[:, :], C("steps"), cmax[:, 0:1], None, ALU.is_lt))
                chain(dve.tensor_reduce(extra[:, :], cge[:, :], AX, ALU.add))
                dve.tensor_scalar(nq[:, l:l + 1], extra[:, :], float(QUADS), float(QUADS), ALU.mult, ALU.add).then_inc(nq_ok, 1)
                for t in range(NT):
                    k = step(dve.tensor_tensor(rkp[:, t, :, :], eoh[:, t, :, :],
                                               B[1][:, t * EXPERTS:(t + 1) * EXPERTS].unsqueeze(1).broadcast_to([P, 2, EXPERTS]),
                                               ALU.mult))
                dve.wait_ge(dve_step, k)
                rank4 = rank[:, :, :].rearrange("p t k -> p (t k)")
                chain(dve.tensor_reduce(rank4, rkp[:, :, :, :].rearrange("p t k e -> p (t k) e"), AX, ALU.add))
                NS = MAX_ROUNDS - 1
                rge4 = rge[:, :, :, :].rearrange("p t k e -> p (t k) e")
                chain(dve.tensor_tensor(rge4, rank4.unsqueeze(2).broadcast_to([P, NT * 2, NS]),
                                        C("steps").unsqueeze(1).broadcast_to([P, NT * 2, NS]), ALU.is_ge))
                turn4 = turn[:, :, :].rearrange("p t k -> p (t k)")
                key04 = key0[:, :, :].rearrange("p t k -> p (t k)")
                key4 = key[:, :, :].rearrange("p t k -> p (t k)")
                chain(dve.tensor_reduce(turn4, rge4, AX, ALU.add))
                chain(dve.scalar_tensor_tensor(out=key04, in0=turn4, scalar=float(ROUND - SLOTS), in1=rank4,
                                               op0=ALU.mult, op1=ALU.add))
                dve.scalar_tensor_tensor(out=key4, in0=eid4, scalar=float(SLOTS), in1=key04,
                                         op0=ALU.mult, op1=ALU.add).then_inc(key_ok, 1)
                step(dve.tensor_copy(slot_row[:, :], C("slot_row")))
                chain(dve.tensor_copy(slot_col[:, :], C("slot_col")))
                dve.wait_ge(key_ok, l + 1)

            def experts(l):
                m = M[l]
                n = dve.value_load(nq[0:1, l:l + 1], min_val=QUADS, max_val=QUADS * MAX_ROUNDS)
                PER = 5
                with dve.Fori(0, n) as q:
                    for t in range(NT):
                        dve.tensor_scalar(pick[:, t, :], slot_row[:, :], key[:, t, 0:1], None, ALU.is_equal
                                          ).then_inc(m["moe_step"], 1)
                    for t in range(NT):
                        dve.wait_ge(m["moe_step"], q * PER + (t + 1))
                        dve.scalar_tensor_tensor(out=pick[:, t, :], in0=slot_row[:, :], scalar=key[:, t, 1:2],
                                                 in1=pick[:, t, :], op0=ALU.is_equal, op1=ALU.add).then_inc(m["pick_ok"], 1)
                    dve.wait_ge(m["gath0"], q + 1)
                    for k in range(4):
                        i = dve.tensor_scalar(xs[:, k, :], B[0][:, k * P:(k + 1) * P], gain[:, 2 * l + 1, k:k + 1],
                                              None, ALU.mult)
                    i.then_inc(m["xs0"], 1)
                    dve.wait_ge(rows_ok, 2 * l + 2)
                    dve.scalar_tensor_tensor(out=back[:, :, :].rearrange("p a s -> p (a s)"),
                                             in0=keyrow[:, :, :].rearrange("p a s -> p (a s)"), scalar=slot_col[:, 0:1],
                                             in1=wrow[:, :, :].rearrange("p a s -> p (a s)"),
                                             op0=ALU.is_equal, op1=ALU.mult).then_inc(m["moe_step"], 1)
                    dve.wait_ge(m["moe_step"], q * PER + 3)
                    dve.tensor_tensor(backs[:, :], back[:, 0, :], back[:, 1, :], ALU.add).then_inc(m["back_ok"], 1)
                    dve.tensor_scalar(slot_row[:, :], slot_row[:, :], float(P), None, ALU.add).then_inc(m["moe_step"], 1)
                    dve.tensor_scalar(slot_col[:, :], slot_col[:, :], float(P), None, ALU.add).then_inc(m["moe_step"], 1)
                    dve.wait_ge(m["silu_g"], q + 1)
                    dve.tensor_tensor(hid[:, :], B[2][:, F:2 * F], sg[:, :], ALU.mult).then_inc(m["hid_ok"], 1)
                    dve.wait_ge(m["hid_T"], q + 1)
                    dve.tensor_copy(hidT[:, :, :].rearrange("p c s -> p (c s)"), B[3][:, 0:FC * P]).then_inc(m["hidT_ok"], 1)
                    dve.wait_ge(m["down0"], q + 1)
                    dve.tensor_copy(ys[:, 0:512], B[0][:, :]).then_inc(m["ys0"], 1)
                    dve.wait_ge(m["moe_step"], q * PER + PER)
                dve.wait_ge(m["y_done"], 1)

            norm(0)
            even_mixer()
            for l in range(2):
                if l == 1:
                    norm(2)
                    odd_mixer()
                norm(2 * l + 1, out_counts=4 * l)
                route(l)
                experts(l)
            norm(4)

        @block.tensor
        def _(pe):
            def norm_tile(i, t):
                xh = xhat[:, :, :].rearrange("p t (d k) -> p t d k", k=KD)
                pe.wait_ge(xhat_dve, NT * i + t + 1)
                pe.wait_ge(xhat_act, NT * i + t + 1)
                for k in range(KD):
                    mm = pe.transpose(B[2 * t + k // 4][:, (k % 4) * P:(k % 4 + 1) * P], xh[:, t, :, k], ident)
                    if k % 4 == 3:
                        mm.then_inc(norm_T, 1)

            def norm_wait(i, t):
                pe.wait_ge(hT_dve, NT * i + t + 1)
                pe.wait_ge(hT_act, NT * i + t + 1)

            def norm(i):
                for t in range(NT):
                    norm_tile(i, t)
                for t in range(NT):
                    norm_wait(i, t)

            def product(dst, pairs, then=None):
                for n, (a, b) in enumerate(pairs):
                    mm = pe.matmul(dst, a, b, start=n == 0, stop=n == len(pairs) - 1)
                if then is not None:
                    mm.then_inc(then, 1)

            def tok(k, t):
                return hT[:, k, t * P:(t + 1) * P]

            def even_mixer():
                for j in range(2):
                    pe.wait_ge(gu_in[j], 16)
                    for c in range(CG):
                        product(B[4 + c][:, j * SEQ:(j + 1) * SEQ],
                                [(gu_slot(j)[:, k, c * P:(c + 1) * P], hT[:, k, :]) for k in range(KD)],
                                vg_done if j else None)
                    if j == 0:
                        pe.wait_ge(even_in, 6 * 16)
                        for c in range(CG):
                            mm = pe.transpose(B[0][:, c * NROW:(c + 1) * NROW], chan_rows[:, c * P:(c + 1) * P],
                                              ident[0:NROW, 0:NROW])
                        mm.then_inc(chan_T, 1)
                        for h in range(CG):
                            mm = pe.transpose(B[1][:, h * P:(h + 1) * P], wsp[:, h, :], ident)
                        mm.then_inc(wsp_T, 1)
                pe.wait_ge(gu_in[3], 16)
                pe.wait_ge(a_done, 1)
                pe.wait_ge(wsp_ok, 1)
                for t in range(NT):
                    product(B[t][:, :], [(tok(k, t), gu_slot(3)[:, k, :]) for k in range(KD)], v_done)
                pe.wait_ge(a_done, 4)
                for j in range(PE_TAPS):
                    pe.wait_ge(diag_ok, j + 1)
                    pe.matmul(B[4][:, 0:SEQ], diag[:, j % DIAGS, :], aT[:, CG - 1, j:j + SEQ],
                              start=j == 0, stop=j == PE_TAPS - 1).then_inc(diag_used, 1)
                pe.wait_ge(gu_in[2], 16)

                def u_product(c):
                    product(B[2 + c // 2][:, (c % 2) * SEQ:(c % 2 + 1) * SEQ],
                            [(gu_slot(2)[:, k, c * P:(c + 1) * P], hT[:, k, :]) for k in range(KD)],
                            u_done if c % 2 else None)

                def over_channels(b, src, then):
                    pe.matmul(B[6 + b][:, :], meanm, src[:, 2 * b:2 * b + 2, :].rearrange("p c s -> p (c s)"),
                              start=True, stop=True).then_inc(then, 1)

                u_product(0)
                u_product(1)
                pe.wait_ge(conv_done, 2)
                over_channels(0, conv, mean_done)
                u_product(2)
                pe.wait_ge(sq_done, 1)
                over_channels(0, sq, cvar_done)
                u_product(3)
                pe.wait_ge(conv_done, 4)
                over_channels(1, conv, mean_done)
                pe.wait_ge(vn_done, 1)
                pe.wait_ge(gelu_v, NT)
                for h in range(CG):
                    for n in range(NT):
                        dst = B[h // 2][:, (h % 2) * SEQ + n * P:(h % 2) * SEQ + (n + 1) * P]
                        pe.matmul(dst, vn[:, n, h * P:(h + 1) * P], wspT[:, h, :], start=True, stop=False)
                        mm = pe.matmul(dst, ones[0:1, :], bsp[0:1, h * P:(h + 1) * P], start=False, stop=True)
                    if h % 2:
                        mm.then_inc(sv_done, 1)
                    if h == 1:
                        pe.wait_ge(sq_done, 2)
                        over_channels(1, sq, cvar_done)
                pe.wait_ge(gated, 2)
                for j in (2, 3):
                    pe.wait_ge(wo_in[j], 16)
                for t in range(NT):
                    if t:
                        pe.wait_ge(cstd_ok, 2)
                    for half in range(2):
                        w_out(range(4, 8), t, half, True, False)
                for j in (0, 1):
                    pe.wait_ge(wo_in[j], 16)
                pe.wait_ge(silu_done, 4)
                w_out_and_norm(range(0, 4), 1, False)

            def w_out_and_norm(chunks, i, first):
                w_out(chunks, 0, 0, first, True)
                w_out(chunks, 0, 1, first, True)
                w_out(chunks, 1, 0, first, True)
                norm_tile(i, 0)
                w_out(chunks, 1, 1, first, True)
                norm_wait(i, 0)
                logits_of(i // 2, 0)
                norm_tile(i, 1)
                norm_wait(i, 1)
                logits_of(i // 2, 1)

            def w_out(chunks, t, half, first, last):
                for kk in chunks:
                    mm = pe.matmul(B[4 + 2 * t + half][:, :], mixT[:, kk, t * P:(t + 1) * P],
                                   wout[:, kk // 2, (kk % 2) * D + half * 512:(kk % 2) * D + (half + 1) * 512],
                                   start=first and kk == chunks[0], stop=last and kk == chunks[-1])
                if last:
                    mm.then_inc(out_done, 1)

            def odd_mixer(g1):
                pe.wait_ge(gu_in[0], g1[0] + 32)
                for t in range(NT):
                    product(B[4 + t][:, 0:COL_A], [(tok(k, t), wA[:, k, :]) for k in range(KD)], pa_done)
                pe.wait_ge(gu_in[2], g1[2] + 32)
                for t in range(NT):
                    product(B[0][:, t * COL_C:(t + 1) * COL_C], [(tok(k, t), wC[:, k, :]) for k in range(KD)],
                            pc_done if t else None)
                pe.wait_ge(gu_in[1], g1[1] + 32)
                for t in range(NT):
                    product(B[6 + t][:, :], [(tok(k, t), wB[:, k, :]) for k in range(KD)], pb_done)
                pe.wait_ge(cq_ok, NT)
                cq = lat[:, :, 0:QR].rearrange("p t (r c) -> p t r c", c=QR // P)
                for c in range(QR // P):
                    for t in range(NT):
                        mm = pe.transpose(B[1][:, c * SEQ + t * P:c * SEQ + (t + 1) * P], cq[:, t, :, c], ident)
                mm.then_inc(lat_T, 1)
                pe.wait_ge(ckv_ok, NT)
                for t in range(NT):
                    mm = pe.transpose(B[2][:, t * P:(t + 1) * P], lat[:, t, QR:QR + KVR], ident)
                mm.then_inc(lat_T, 1)
                pe.wait_ge(latT_ok, 2)
                for t in range(NT):
                    if t:
                        pe.wait_ge(qs_ok, NT)
                    for b, (h0, nh) in enumerate(((0, 5), (5, 3))):
                        product(B[4 + 2 * t + b][:, 0:nh * QK],
                                [(cqT[:, c, t * P:(t + 1) * P], wuq[:, c, h0 * QK:(h0 + nh) * QK]) for c in range(QR // P)],
                                q_up if b else None)
                pe.wait_ge(gu_in[3], g1[3] + 32)
                pe.wait_ge(latT_ok, 3)
                pe.wait_ge(ks_ok, 1)
                for t in range(NT):
                    for b in range(2):
                        product(B[2 * t + b][:, :], [(ckvT[:, t * P:(t + 1) * P], wukv[:, b * 512:(b + 1) * 512])],
                                kv_up if b else None)
                pe.wait_ge(q_nope, 4)
                pe.wait_ge(q_rope, 4)
                pe.wait_ge(k_nope, 4)
                pe.wait_ge(k_rope, 2)
                pe.wait_ge(v_ok, 4)
                for n, (dst, rows, views) in enumerate(head_blocks):
                    if n >= 8:
                        m = n - 8
                        pe.wait_ge(headT_act if m % 2 else headT_dve, m // 2 + 1)
                    for i, v in enumerate(views):
                        mm = pe.transpose(B[n % 8][0:rows, i * P:(i + 1) * P], v, ident)
                    mm.then_inc(head_T, 1)
                pe.wait_ge(headT_act, HB_ACT)
                pe.wait_ge(headT_dve, HB_DVE)

                def unit_score(u):
                    window = u >= UNITS // 2
                    w, t = (u - UNITS // 2 if window else u) // NT, u % NT
                    h = UNITS // 2
                    if u >= h + 2:
                        pe.wait_ge(biased, u - 2 - h + 1)
                    elif u >= 4:
                        pe.wait_ge(expd, 2 * (u - 4) + 2 if u < h else 2 * h)
                    for i in range(2):
                        dst = score_bank(u, i)
                        if window:
                            r = slice(64 * i, 64 * i + 64)
                            mm = pe.matmul(dst, qsT[r, w, t * P:(t + 1) * P], ksT[r, :], start=True, stop=True)
                        else:
                            mm = pe.matmul(dst, qT[0:QK, 2 * w + i, t * P:(t + 1) * P], kT[0:QK, 2 * w + i, :],
                                           start=True, stop=True)
                    mm.then_inc(score, 1)

                def unit_prob_T(u):
                    pe.wait_ge(expd, 2 * u + 2)
                    if u >= 2:
                        pe.wait_ge(pT_ok, u - 1)
                    for i in range(2):
                        for kc in range(NT):
                            mm = pe.transpose(B[2 + u % 2][:, (2 * i + kc) * P:(2 * i + kc + 1) * P],
                                              prob[:, u % 2, i, kc * P:(kc + 1) * P], ident)
                    mm.then_inc(prob_T, 1)

                def unit_out(u):
                    window = u >= UNITS // 2
                    w = (u - UNITS // 2 if window else u) // NT
                    pe.wait_ge(pT_ok, u + 1)
                    if u >= 2:
                        pe.wait_ge(o_ok, u - 1)
                    for i in range(2):
                        dst = B[4 + u % 2][:, i * VD:(i + 1) * VD]
                        product(dst, [(pT[:, u % 2, 2 * i + kc, :],
                                       ksvs[:, kc, P + i * SWA_D:P + (i + 1) * SWA_D] if window else vm[:, kc, 2 * w + i, :])
                                      for kc in range(NT)], pv if i else None)

                for u in range(UNITS + 3):
                    if u < UNITS:
                        unit_score(u)
                    if 2 <= u < UNITS + 2:
                        unit_prob_T(u - 2)
                    if u >= 3:
                        unit_out(u - 3)
                pe.wait_ge(o_ok, UNITS)
                for b in range(4):
                    for kk in range(2):
                        for t in range(NT):
                            mm = pe.transpose(B[b][:, kk * SEQ + t * P:kk * SEQ + (t + 1) * P],
                                              osb[:, t, (2 * b + kk) * P:(2 * b + kk + 1) * P], ident)
                    mm.then_inc(o_T, 1)
                for j in range(QUAD):
                    pe.wait_ge(wo_in[j], 32)
                pe.wait_ge(oT_act, 2)
                pe.wait_ge(oT_dve, 2)
                w_out_and_norm(range(0, 8), 3, True)

            def logits_of(l, t):
                if l == 0 and t == 0:
                    pe.wait_ge(route_w_done, 10)
                product(B[0][:, t * 64:t * 64 + NL], [(tok(k, t), wrt[:, l, k, :]) for k in range(KD)],
                        logits if t else None)

            def route(l):
                for b in range(4):
                    pe.matmul(B[4 + b][:, :], zeros[:, 0:P], zeros[:, :], start=True, stop=False)
                pe.wait_ge(member_ok, l + 1)
                product(B[1][:, 0:EXPERTS], [(before, member[:, 0, :])])
                product(B[1][:, EXPERTS:2 * EXPERTS], [(before, member[:, 1, :]), (ones, member[:, 0, :])])
                product(B[1][:, 64:64 + EXPERTS], [(ones, member[:, 0, :]), (ones, member[:, 1, :])], ranks)
                for b, cols, ready in ((3, weight, weight_ok), (2, key, key_ok)):
                    pe.wait_ge(ready, l + 1)
                    for k in range(2):
                        for t in range(NT):
                            product(B[b][:, k * SEQ + t * P:k * SEQ + (t + 1) * P],
                                    [(cols[:, t, k:k + 1].broadcast_to([P, P]), ident)],
                                    rows_T if (k, t) == (1, 1) else None)

            def experts(l, g0, d0):
                m = M[l]
                n = pe.value_load(nq[0:1, l:l + 1], min_val=QUADS, max_val=QUADS * MAX_ROUNDS)

                def turn(q, spare=False, late=False):
                    pe.wait_ge(m["pick_ok"], q * 2 + 2)
                    xh = xhat[:, :, :].rearrange("p t (d k) -> p t d k", k=KD)
                    for k in range(KD):
                        for t in range(NT):
                            mm = pe.matmul(B[k // 4][:, (k % 4) * P:(k % 4 + 1) * P], xh[:, t, :, k], pick[:, t, :],
                                           start=t == 0, stop=t == NT - 1)
                        if k == 3:
                            mm.then_inc(m["gath0"], 1)
                    mm.then_inc(m["gath1"], 1)
                    pe.wait_ge(m["xs0"], q + 1)
                    pe.wait_ge(m["xs1"], q + 1)
                    pe.wait_ge(rows_ok, 2 * l + 2)
                    for j in range(QUAD):
                        if spare and j < SPARE_GU:
                            pe.wait_ge(spare_gu_in[j], 32 * (l + 1))
                        else:
                            pe.wait_ge(gu_in[j], q * 32 + (g0[j] + (0 if late and j < SPARE_GU else 32)))
                    for k in range(KD):
                        for j in range(QUAD):
                            slot = spare_gu[j] if spare and j < SPARE_GU else ring_gu[:, j, :]
                            w = slot.rearrange("p (a k f) -> p a k f", a=2, k=KD)[:, :, k, :]
                            mm = pe.matmul(B[2][SLOTS * j:SLOTS * (j + 1), :], xs[:, k, SLOTS * j:SLOTS * (j + 1)], w,
                                           start=k == 0, stop=k == KD - 1, tile_position=(0, SLOTS * j))
                    mm.then_inc(m["gu_used"], 1)
                    pe.wait_ge(m["hid_ok"], q + 1)
                    hv = hid[:, :].rearrange("p (f c) -> p f c", c=FC)
                    for c in range(FC):
                        mm = pe.transpose(B[3][:, c * P:(c + 1) * P], hv[:, :, c], ident)
                    mm.then_inc(m["hid_T"], 1)
                    pe.wait_ge(m["hidT_ok"], q + 1)
                    for j in range(QUAD):
                        if spare and j < SPARE_DN:
                            pe.wait_ge(spare_dn_in[j], 16 * (l + 1))
                        else:
                            pe.wait_ge(dn_in[j], q * 16 + (d0[j] + (0 if late and j < SPARE_DN else 16)))
                    for half in range(2):
                        for c in range(FC):
                            for j in range(QUAD):
                                slot = spare_dn[j] if spare and j < SPARE_DN else ring_dn[:, j, :]
                                mm = pe.matmul(B[half][SLOTS * j:SLOTS * (j + 1), :], hidT[:, c, SLOTS * j:SLOTS * (j + 1)],
                                               slot[:, c * D + half * 512:c * D + (half + 1) * 512],
                                               start=c == 0, stop=c == FC - 1, tile_position=(0, SLOTS * j))
                        mm.then_inc(m["dn_used"] if half else m["down0"], 1)
                    pe.wait_ge(m["back_ok"], q + 1)
                    pe.wait_ge(m["ys0"], q + 1)
                    pe.wait_ge(m["ys1"], q + 1)
                    for half in range(2):
                        for t in range(NT):
                            pe.matmul(B[4 + 2 * t + half][:, :], backs[:, t * P:(t + 1) * P], ys[:, half * 512:(half + 1) * 512],
                                      start=False, stop=False)
                turn(0)
                turn(1, spare=True)
                with pe.Fori(2, n) as q:
                    turn(q, late=True)
                for b in range(4):
                    mm = pe.matmul(B[4 + b][:, :], zeros[:, 0:P], zeros[:, :], start=False, stop=True)
                mm.then_inc(m["y_done"], 1)
                return n

            pe.wait_ge(const_in, 16)
            pe.wait_ge(zeros_ok, 1)
            norm(0)
            even_mixer()
            route(0)
            n0 = experts(0, [16] * QUAD, [0] * QUAD)
            g1 = [n0 * 32 + (16 - 32 * (j < SPARE_GU)) for j in range(QUAD)]
            norm(2)
            odd_mixer(g1)
            route(1)
            experts(1, [n0 * 32 + (48 - 32 * (j < SPARE_GU)) for j in range(QUAD)],
                    [n0 * 16 - (16 if j < SPARE_DN else 0) for j in range(QUAD)])


_INS = ['x', 'norm_mix', 'norm_ffn', 'norm_final', 'ev_w_in', 'ev_conv_w', 'ev_conv_b', 'ev_cnorm_g', 'ev_cnorm_b',
        'ev_vnorm_g', 'ev_vnorm_b', 'ev_w_sp', 'ev_b_sp', 'ev_w_out', 'od_w_in', 'od_g_cq', 'od_w_uq', 'od_g_ckv',
        'od_w_ukv', 'od_sink', 'od_w_out', 'moe_w_group', 'moe_b_group', 'moe_w_router', 'moe_b_router',
        'moe_w_gate', 'moe_w_up', 'moe_w_down']


def kernel(**inputs):
    import concourse.bacc as bacc
    from concourse.bass_utils import run_bass_kernel_spmd as run

    nc = bacc.Bacc("TRN2", target_bir_lowering=False, num_devices=1)
    arrays, args = {}, []
    for name in _INS:
        a = np.ascontiguousarray(inputs[name])
        arrays[f"in_{name}"] = a
        args.append(nc.dram_tensor(f"in_{name}", a.shape, mybir.dt.from_np(a.dtype), kind="ExternalInput").ap())
    arrays["constants"] = constants()
    args.append(nc.dram_tensor("constants", (P, NCONST), mybir.dt.float32, kind="ExternalInput").ap())
    args.append(nc.dram_tensor("out_x", (1, SEQ, D), mybir.dt.float32, kind="ExternalOutput").ap())
    program(nc, *args)
    return run(nc, [arrays], core_ids=[0]).results[0]["out_x"]
```

```python
import concourse.bass as bass
from concourse import mybir
from concourse.alu_op_type import AluOpType as ALU
from contextlib import ExitStack
import numpy as np

D, SEQ, P = 1024, 256, 128
NT = SEQ // P
KD = D // P
GROUPS, PER_GROUP, F = 4, 8, 256
EXPERTS = GROUPS * PER_GROUP
SLOTS = 32
QUAD = P // SLOTS
QUADS = EXPERTS // QUAD
ROUND = EXPERTS * SLOTS
MAX_ROUNDS = SEQ // SLOTS
FC = F // P
GU = 2 * KD * F
DN = FC * D
TAPS, CG = 31, 4
HALO = TAPS // 2
APAD = SEQ + 2 * HALO + 2
HEADS, NOPE, ROPE, VD = 8, 64, 32, 64
QK = NOPE + ROPE
QR, KVR = 256, 128
MLA_SCALE = float(QK) ** -0.5
SWA_D, KVH, WINDOW = 64, 2, 128
SWA_SCALE = float(SWA_D) ** -0.5
COL_A = QR + KVR + ROPE
COL_B = HEADS * SWA_D
COL_C = 2 * KVH * SWA_D
ODD_IN = COL_A + COL_B + COL_C
EPS = 1e-6
FAR = 1e30
LOW = -3e38
NROW = TAPS + 3

CONST = {}
_at = 0
for _n, _w in (("ident", P), ("before", P), ("ones", P), ("mean", P), ("slot_row", P), ("slot_col", 1),
               ("iota_e", EXPERTS), ("iota_g", GROUPS), ("steps", MAX_ROUNDS - 1), ("eps", 1),
               ("cos", NT * ROPE), ("sin", NT * ROPE), ("dist", NT * SEQ)):
    CONST[_n] = (_at, _at + _w)
    _at += _w
NCONST = _at
NFIRST = CONST["dist"][0]
NSCRATCH = 9760


def constants():
    c = np.zeros((P, NCONST), np.float32)

    def put(name, value):
        a, b = CONST[name]
        c[:, a:b] = np.asarray(value, np.float32).reshape(-1, b - a)

    i = np.arange(P)
    put("ident", np.eye(P))
    put("before", i[:, None] < i[None, :])
    put("ones", np.ones((P, P)))
    put("mean", np.full((P, P), 1.0 / P))
    put("slot_row", np.tile(i, (P, 1)))
    put("slot_col", i[:, None])
    put("iota_e", np.tile(np.arange(EXPERTS), (P, 1)))
    put("iota_g", np.tile(np.arange(GROUPS), (P, 1)))
    put("steps", np.tile(SLOTS * np.arange(1, MAX_ROUNDS), (P, 1)))
    put("eps", np.full((P, 1), EPS))
    inv = (np.float32(1.0) / (np.float32(10000.0) ** (np.arange(0, ROPE, 2, dtype=np.float32) / np.float32(ROPE)))).astype(np.float32)
    ang = np.arange(SEQ, dtype=np.float32)[:, None] * inv[None, :]
    ang = np.concatenate([ang, ang], axis=-1).astype(np.float32)
    sin = np.sin(ang)
    sin[:, :ROPE // 2] *= -1
    put("cos", np.cos(ang).reshape(NT, P, ROPE).transpose(1, 0, 2).reshape(P, -1))
    put("sin", sin.reshape(NT, P, ROPE).transpose(1, 0, 2).reshape(P, -1))
    dist = np.abs(np.arange(SEQ)[:, None] - np.arange(SEQ)[None, :]).astype(np.float32)
    dist[dist > WINDOW] = FAR
    put("dist", dist.reshape(NT, P, SEQ).transpose(1, 0, 2).reshape(P, -1))
    return c


def program(nc, x, norm_mix, norm_ffn, norm_final, ev_w_in, ev_conv_w, ev_conv_b, ev_cnorm_g, ev_cnorm_b,
            ev_vnorm_g, ev_vnorm_b, ev_w_sp, ev_b_sp, ev_w_out, od_w_in, od_g_cq, od_w_uq, od_g_ckv,
            od_w_ukv, od_sink, od_w_out, moe_w_group, moe_b_group, moe_w_router, moe_b_router,
            moe_w_gate, moe_w_up, moe_w_down, const, out):
    fp32, i32, u32 = mybir.dt.float32, mybir.dt.int32, mybir.dt.uint32
    ACT = mybir.ActivationFunctionType
    AX = mybir.AxisListType.X

    ctx = ExitStack()
    with ctx:
        def sb(name, shape, dt=fp32):
            return ctx.enter_context(nc.sbuf_tensor(name, shape, dt))

        def sem(name):
            return ctx.enter_context(nc.semaphore(name))

        scratch = sb("scratch", [P, NSCRATCH])
        place = [0]

        def carve(shape, dt=fp32, at=None):
            size = int(np.prod(shape[1:]))
            a = place[0] if at is None else at
            if at is None:
                place[0] += size
            assert a + size <= NSCRATCH, (a, size)
            v = scratch[0:shape[0], a:a + size]
            if dt != fp32:
                v = v.bitcast(dt)
            names = "abc"[:len(shape) - 1]
            if len(shape) > 2:
                v = v.rearrange(f"p ({' '.join(names)}) -> p {' '.join(names)}",
                                **{n: w for n, w in zip(names[1:], shape[2:])})
            return v

        ring_gu = sb("ring_gu", [P, QUAD, GU])
        ring_dn = sb("ring_dn", [P, QUAD, DN])
        wout = sb("wout", [P, QUAD, 2 * D])
        X = sb("X", [P, NT, D])
        xhat = sb("xhat", [P, NT, D])
        hT = sb("hT", [P, KD, SEQ])
        mixT = sb("mixT", [P, KD, SEQ])
        zeros = sb("zeros", [1, P], mybir.dt.bfloat16)
        cst = sb("cst", [P, NCONST])
        gain = sb("gain", [P, 4, KD])
        gfin = mixT[:, 0:4, :].rearrange("p k s -> p (k s)")
        stat = sb("stat", [P, 5, NT, 5])
        xhat_flat = xhat[:, :, :].rearrange("p t n -> p (t n)")
        mixT_flat = mixT[:, :, :].rearrange("p k s -> p (k s)")

        def rows3(v, b, c):
            return v.rearrange("p (b c) -> p b c", b=b, c=c)

        def C(name):
            a, b = CONST[name]
            return cst[:, a:b]

        ident, before, ones, meanm = C("ident"), C("before"), C("ones"), C("mean")
        eps_col = C("eps")

        chan_rows = carve([NROW, CG * P])
        chanp = carve([P, CG, NROW])
        wsp = carve([P, CG, P])
        wspT = carve([P, CG, P])
        bsp = carve([1, CG * P])
        vgb = carve([P, 2, CG * P])
        sig = rows3(xhat_flat[:, 0:D], CG, SEQ)
        aT = carve([P, CG, APAD])
        conv = carve([P, CG, SEQ])
        junk, junk_v = (conv[:, a:a + 2, :].rearrange("p c s -> p (c s)") for a in (0, 2))
        DIAGS = 8
        PE_TAPS = 26
        diag = rows3(mixT_flat[:, 0:DIAGS * P], DIAGS, P)
        sq = sig
        uT = carve([P, CG, SEQ])
        vt = rows3(xhat_flat[:, D:2 * D], NT, CG * P)
        vn = vt
        vst = carve([P, NT * CG, 6])
        vag = carve([P, NT * CG, 2])
        vstd = carve([P, NT * CG])
        vrs = carve([P, NT * CG])
        vnb = carve([P, NT * CG])

        even_end = place[0]
        place[0] = 0
        g_cq = sb("g_cq", [P, QR // P])
        g_ckv = sb("g_ckv", [P, 1])
        sink = sb("sink", [P, HEADS])
        qs_at = place[0]
        qs = carve([P, NT, COL_B])
        ksvs = carve([P, NT, COL_C])
        qsT = carve([P, HEADS // 2, SEQ])
        lat = mixT_flat[:, 0:NT * (QR + KVR)].rearrange("p (t n) -> p t n", t=NT)
        lsq = lat
        mid = NT * (QR + KVR)
        cqT = mixT_flat[:, mid:mid + QR // P * SEQ].rearrange("p (c s) -> p c s", s=SEQ)
        mid += QR // P * SEQ
        ckvT = mixT_flat[:, mid:mid + SEQ]
        mid += SEQ
        rt1, rt2 = mixT_flat[:, mid:mid + 5 * ROPE], mixT_flat[:, mid + 5 * ROPE:mid + 10 * ROPE]
        kpe = carve([P, NT, ROPE])
        lst = carve([P, 4, 2, NT])
        qf_at = place[0]
        qf = carve([P, NT, HEADS * QK])
        kf = carve([P, NT, HEADS, QK])
        vm = carve([P, NT, HEADS, VD])
        qT = rows3(xhat_flat, HEADS, SEQ)
        kT = hT
        ksT = carve([P, SEQ])
        sw = carve([P, 2, 2, SEQ], at=qs_at)
        prob = mixT_flat[:, 0:D].rearrange("p (a b c) -> p a b c", a=2, b=2)
        pT = mixT_flat[:, D:2 * D].rearrange("p (a b c) -> p a b c", a=2, b=4)
        pairs = [(w, t) for w in range(HEADS // 2) for t in range(NT)]
        unit = [(False, *pairs[0])]
        for n in range(1, len(pairs)):
            unit += [(False, *pairs[n]), (True, *pairs[n - 1])]
        unit.append((True, *pairs[-1]))
        UNITS = len(unit)
        before_w = [sum(v[0] for v in unit[:u]) for u in range(UNITS + 1)]
        us = carve([P, UNITS, 6, 2])
        osb = carve([P, NT, D], at=qf_at)
        odd_end = place[0]

        place[0] = 0
        EX0 = 8
        NL = EX0 + EXPERTS
        wrt_in = carve([P, 2, GROUPS, KD * PER_GROUP], at=even_end)
        route_w_end = even_end + 2 * KD * (EXPERTS + GROUPS)
        wrt = sb("wrt", [P, 2, KD, NL])
        wgr = carve([P, 2, KD, GROUPS], at=even_end + 2 * KD * EXPERTS)
        brt = sb("brt", [P, 2, NL])
        nq = sb("nq", [P, 2], i32)
        key = carve([P, NT, 2])
        keyrow = carve([P, 2, SEQ])
        wrow = carve([P, 2, SEQ])
        slot_row = carve([P, P])
        slot_col = carve([P, 1])
        pick = carve([P, NT, P])
        back = carve([P, 2, SEQ])
        backs = carve([P, SEQ])
        hidT = back[:, 0, :].rearrange("p (c s) -> p c s", c=FC)
        sg = carve([P, F])
        hid = sg
        turns_at = place[0]
        lg = carve([P, NT, NL])
        gl, rl = lg[:, :, 0:EX0], lg[:, :, EX0:NL]
        gm8 = carve([P, NT, 8])
        gi8 = carve([P, NT, 8], u32)
        em8 = carve([P, NT, 8])
        ei8 = carve([P, NT, 8], u32)
        gif = carve([P, NT])
        goh = carve([P, NT, GROUPS])
        selp = carve([P, NT, EXPERTS])
        sel = carve([P, NT, PER_GROUP])
        eif = carve([P, NT, 2])
        exin = carve([P, NT, 5])
        exo = carve([P, NT, 5])
        gsum = carve([P, NT])
        den = carve([P, NT])
        weight = carve([P, NT, 2])
        eid = carve([P, NT, 2])
        eid32 = carve([P, NT, 2])
        eoh = carve([P, NT, 2, EXPERTS])
        member = carve([P, NT, EXPERTS])
        rkp = carve([P, NT, 2, EXPERTS])
        rank = carve([P, NT, 2])
        cmax = carve([P, 1])
        cge = carve([P, MAX_ROUNDS - 1])
        extra = carve([P, 1])
        rge = carve([P, NT, 2, MAX_ROUNDS - 1])
        turn = carve([P, NT, 2])
        key0 = carve([P, NT, 2])
        xs = carve([P, KD, P], at=turns_at)
        ys = carve([P, D], at=turns_at)
        experts_end = max(place[0], turns_at + D)
        SPARE_GATE, SPARE_UP = 4, 2
        wout_pair = [wout[:, 2 * j:2 * j + 2, :].rearrange("p a n -> p (a n)") for j in range(2)]
        assert KD * F == DN
        spare_gate = [wout_pair[0][:, 0:KD * F], wout_pair[1][:, 0:KD * F], X[:, :, :].rearrange("p t n -> p (t n)"),
                      carve([P, DN], at=NSCRATCH - 3 * DN)]
        spare_up = [wout_pair[0][:, KD * F:GU], wout_pair[1][:, KD * F:GU]]
        assert experts_end <= NSCRATCH - 3 * DN and max(route_w_end, odd_end) <= NSCRATCH - DN
        spare_dn = [hT[:, :, :].rearrange("p k s -> p (k s)"), mixT_flat,
                    carve([P, DN], at=NSCRATCH - 2 * DN), carve([P, DN], at=NSCRATCH - DN)]

        B = [ctx.enter_context(nc.psum_tensor(f"B{i}", [P, 512], fp32)) for i in range(8)]

        x_in = [sem(f"x_in{t}") for t in range(NT)]
        wo_in = [sem(f"wo_in{j}") for j in range(QUAD)]
        dist_in, vec_in, weight_ok = sem("dist_in"), sem("vec_in"), sem("weight_ok")
        const_in, gain_in, even_in, odd_in, route_in, gfin_in = (
            sem(n) for n in ("const_in", "gain_in", "even_in", "odd_in", "route_in", "gfin_in"))
        gu_in = [sem(f"gu_in{j}") for j in range(QUAD)]
        dn_in = [sem(f"dn_in{c}") for c in range(FC)]
        up_in = [sem("up_in_01"), sem("up_in_23")]
        spare_gate_in, spare_up_in, spare_dn_in = sem("spare_gate_in"), sem("spare_up_in"), sem("spare_dn_in")
        x_moved = sem("x_moved")
        half_out = sem("half_out")
        pads_done, route_w_done = sem("pads_done"), sem("route_w_done")
        act_sum, dve_sum, var_done, std_done, rstd_done = (
            sem(n) for n in ("act_sum", "dve_sum", "var_done", "std_done", "rstd_done"))
        xhat_act, xhat_dve, norm_T = sem("xhat_act"), sem("xhat_dve"), sem("norm_T")
        hT_dve, hT_act = sem("hT_dve"), sem("hT_act")
        x_new, x_new_act = sem("x_new"), sem("x_new_act")
        X_NEW = {1: 0, 2: 4, 3: 6}
        XHAT = {0: 0, 1: 1, 3: 2}
        dve_step = sem("dve_step")
        chan_T, wsp_T, wsp_ok = sem("chan_T"), sem("wsp_T"), sem("wsp_ok")
        vg_done, sig_done, a_done, v_done, u_done = (sem(n) for n in ("vg_done", "sig_done", "a_done", "v_done", "u_done"))
        gelu_v, gelu_u, vvar, vstd_ok, vrs_ok, v_scaled, vn_done = (
            sem(n) for n in ("gelu_v", "gelu_u", "vvar", "vstd_ok", "vrs_ok", "v_scaled", "vn_done"))
        sv_done, gated, conv_done, mean_done = (sem(n) for n in ("sv_done", "gated", "conv_done", "mean_done"))
        cen_done, sq_done, cvar_done, cstd_ok, cn_done, silu_done = (
            sem(n) for n in ("cen_done", "sq_done", "cvar_done", "cstd_ok", "cn_done", "silu_done"))
        taps_ok, diag_ok, diag_used, conv3_ok = (sem(n) for n in ("taps_ok", "diag_ok", "diag_used", "conv3_ok"))
        out_done = sem("out_done")
        pa_done, pb_done, pc_done = (sem(n) for n in ("pa_done", "pb_done", "pc_done"))
        lsum, lvar, lstd, lrs = (sem(n) for n in ("lsum", "lvar", "lstd", "lrs"))
        cq_ok, ckv_ok, lat_T, latT_ok, qs_ok, ks_ok = (
            sem(n) for n in ("cq_ok", "ckv_ok", "lat_T", "latT_ok", "qs_ok", "ks_ok"))
        q_up, kv_up, q_nope, q_rope, k_nope, v_ok, k_rope = (
            sem(n) for n in ("q_up", "kv_up", "q_nope", "q_rope", "k_nope", "v_ok", "k_rope"))
        head_T, headT_act, headT_dve = sem("head_T"), sem("headT_act"), sem("headT_dve")
        score, biased, negmax, expd, sink_d, sink_e = (
            sem(n) for n in ("score", "biased", "negmax", "expd", "sink_d", "sink_e"))
        prob_T, pT_ok, pv, o_ok, o_T, oT_act, oT_dve = (
            sem(n) for n in ("prob_T", "pT_ok", "pv", "o_ok", "o_T", "oT_act", "oT_dve"))
        logits, ex_in, ex_out, member_ok, ranks, nq_ok, key_ok, rows_T, rows_ok = (
            sem(n) for n in ("logits", "ex_in", "ex_out", "member_ok", "ranks", "nq_ok", "key_ok", "rows_T", "rows_ok"))
        M = [{n: sem(f"{n}_{l}") for n in (
            "pick_ok", "gath0", "gath1", "xs0", "xs1", "gate_used", "up_used", "silu_g", "hid_ok", "hid_T", "hidT_ok",
            "down0", "dn_used", "ys0", "ys1", "back_ok", "moe_step", "y_done")} for l in range(2)]
        o_sem = sem("o_sem")
        stored = sem("stored")

        block = ctx.enter_context(nc.Block())

        w_in0 = ev_w_in[0].rearrange("(p k) (b n) -> b p k n", k=KD, b=4)
        w_out0 = ev_w_out[0].rearrange("(j c p) n -> j p c n", p=P, c=2)
        w_out1 = od_w_out[0].rearrange("(j c p) n -> j p c n", p=P, c=2)
        w_in1 = od_w_in[0].rearrange("(p k) n -> p k n", k=KD)

        def gu_slot(j):
            return ring_gu[:, j, :].rearrange("p (k n) -> p k n", k=KD)

        wA = ring_gu[:, 0, 0:KD * COL_A].rearrange("p (k n) -> p k n", k=KD)
        wB = gu_slot(1)
        wC = ring_gu[:, 2, 0:KD * COL_C].rearrange("p (k n) -> p k n", k=KD)
        UQ0 = KD * COL_C
        NUQ = HEADS * QK
        NUKV = HEADS * (NOPE + VD)
        wuq = ring_gu[:, 2, UQ0:UQ0 + QR // P * NUQ].rearrange("p (c n) -> p c n", n=NUQ)
        wukv = ring_gu[:, 3, 0:NUKV]

        head_blocks = []
        for r in range(0, HEADS // KVH, 2):
            head_blocks.append((qsT[:, r:r + 2, :].rearrange("p h s -> p (h s)"), P,
                                [qs[:, t, rr * P:(rr + 1) * P] for rr in (r, r + 1) for t in range(NT)]))
        head_blocks.append((ksT[:, :], P, [ksvs[:, t, 0:P] for t in range(NT)]))
        EARLY = len(head_blocks)
        for pair in range(0, HEADS, 2):
            head_blocks.append((qT[0:QK, pair:pair + 2, :].rearrange("p h s -> p (h s)"), QK,
                                [qf[:, t, h * QK:(h + 1) * QK] for h in (pair, pair + 1) for t in range(NT)]))
            head_blocks.append((kT[0:QK, pair:pair + 2, :].rearrange("p h s -> p (h s)"), QK,
                                [kf[:, t, h, :] for h in (pair, pair + 1) for t in range(NT)]))
        NHB = len(head_blocks)
        head_bank = [B[(n + 4) % 8] for n in range(NHB)]
        HEAD_COPIES_ACT = NHB // 2
        HEAD_COPIES_DVE = NHB - HEAD_COPIES_ACT

        def by_k(row):
            return row.rearrange("s (p k) -> s p k", k=KD)

        def score_bank(u, i):
            return B[u % 2 + 6 * i][:, 0:SEQ]

        @block.sync
        def _(sp):
            for t in range(NT):
                sp.dma_start(X[:, t, :], x[0, t * P:(t + 1) * P, :]).then_inc(x_in[t], 16)
                if t == 0:
                    sp.dma_start(cst[:, 0:NFIRST], const[:, 0:NFIRST]).then_inc(const_in, 16)
            sp.dma_start(gain[:, 0:4:2, :], norm_mix.rearrange("l (p k) -> p l k", k=KD)).then_inc(gain_in, 16)
            sp.dma_start(gain[:, 1:4:2, :], norm_ffn.rearrange("l (p k) -> p l k", k=KD)).then_inc(gain_in, 16)
            sp.dma_start(gu_slot(0), w_in0[0]).then_inc(gu_in[0], 16)
            sp.dma_start(chan_rows[0:TAPS, :], ev_conv_w[0]).then_inc(even_in, 16)
            for i, w in enumerate((ev_conv_b, ev_cnorm_g, ev_cnorm_b)):
                sp.dma_start(chan_rows[TAPS + i:TAPS + i + 1, :], w).then_inc(even_in, 16)
            sp.dma_start(wsp[:, :, :], ev_w_sp[0].rearrange("h t s -> t h s")).then_inc(even_in, 16)
            sp.dma_start(bsp[:, :], ev_b_sp.rearrange("a h t -> a (h t)")).then_inc(even_in, 16)
            sp.dma_start(gu_slot(1), w_in0[1]).then_inc(gu_in[1], 16)
            sp.dma_start(gu_slot(3), w_in0[3]).then_inc(gu_in[3], 16)
            sp.dma_start(vgb[:, 0, :], ev_vnorm_g.broadcast_to([P, CG * P])).then_inc(vec_in, 16)
            sp.dma_start(vgb[:, 1, :], ev_vnorm_b.broadcast_to([P, CG * P])).then_inc(vec_in, 16)
            sp.dma_start(gu_slot(2), w_in0[2]).then_inc(gu_in[2], 16)

            def load_w_out(w):
                for j in (2, 3, 0, 1):
                    sp.dma_start(wout[:, j, :].rearrange("p (c n) -> p c n", c=2), w[j]).then_inc(wo_in[j], 16)

            load_w_out(w_out0)
            for l in range(2):
                sp.dma_start(wgr[:, l, :, :], moe_w_group[l].rearrange("(p k) g -> p k g", k=KD)).then_inc(route_in, 16)
                sp.dma_start(wrt_in[:, l, :, :],
                             moe_w_router[l].rearrange("g (p k) e -> p g (k e)", k=KD)).then_inc(route_in, 16)
            sp.dma_start(brt[:, :, 0:GROUPS],
                         moe_b_group.rearrange("l (o g) -> o l g", o=1).broadcast_to([P, 2, GROUPS])).then_inc(route_in, 16)
            sp.dma_start(brt[:, :, EX0:NL],
                         moe_b_router.rearrange("l g (o e) -> o l (g e)", o=1).broadcast_to([P, 2, EXPERTS])
                         ).then_inc(route_in, 16)
            sp.dma_start(g_cq[:, :], od_g_cq[0].rearrange("(p c) -> p c", c=QR // P)).then_inc(odd_in, 16)
            sp.dma_start(g_ckv[:, :], od_g_ckv[0].rearrange("(p c) -> p c", c=1)).then_inc(odd_in, 16)
            sp.dma_start(sink[:, :], od_sink.broadcast_to([P, HEADS])).then_inc(odd_in, 16)
            sp.dma_start(cst[:, NFIRST:NCONST], const[:, NFIRST:NCONST]).then_inc(dist_in, 16)

            def load_gate(l, q, j, spare=False):
                slot, arrived = (spare_gate[j], spare_gate_in) if spare else (ring_gu[:, j, 0:KD * F], gu_in[j])
                w_e = moe_w_gate[l].rearrange("g e (p k) f -> (g e) p (k f)", k=KD)
                sp.dma_start(slot, w_e[bass.ds(q * QUAD + j, 1), :, :].rearrange("o p f -> p (o f)")
                             ).then_inc(arrived, 16)

            def load_up(l, q, j, spare=False):
                slot, arrived = (spare_up[j], spare_up_in) if spare else (ring_gu[:, j, KD * F:GU], up_in[j // 2])
                w_e = moe_w_up[l].rearrange("g e (p k) f -> (g e) p (k f)", k=KD)
                sp.dma_start(slot, w_e[bass.ds(q * QUAD + j, 1), :, :].rearrange("o p f -> p (o f)")
                             ).then_inc(arrived, 16)

            def load_dn_chunk(l, q, j, c, spare=False):
                slot, arrived = (spare_dn[j], spare_dn_in) if spare else (ring_dn[:, j, :], dn_in[c])
                w_e = moe_w_down[l].rearrange("g e (p c) n -> c (g e) p n", c=FC)[c]
                sp.dma_start(slot[:, c * D:(c + 1) * D], w_e[bass.ds(q * QUAD + j, 1), :, :].rearrange("o p f -> p (o f)")
                             ).then_inc(arrived, 16)

            def load_dn(l, q):
                for c in range(FC):
                    for j in range(QUAD):
                        load_dn_chunk(l, q, j, c)

            def load_spare_dn(l, j):
                for c in range(FC):
                    load_dn_chunk(l, 1, j, c, spare=True)

            def experts(l, gu_free):
                load_dn(l, 0)
                for j, (semaphore, count) in gu_free:
                    sp.wait_ge(semaphore, count)
                    load_gate(l, 0, j)
                    load_up(l, 0, j)
                load_spare_dn(l, 3)
                first = 1 - l
                sp.wait_ge(half_out, l + 1)
                load_gate(l, 1, first, spare=True)
                load_up(l, 1, first, spare=True)
                if l == 0:
                    sp.wait_ge(route_w_done, 10)
                load_spare_dn(l, 2)
                sp.wait_ge(out_done, 4 * (l + 1))
                load_gate(l, 1, 1 - first, spare=True)
                load_up(l, 1, 1 - first, spare=True)
                load_spare_dn(l, 1)
                sp.wait_ge(logits, l + 1)
                load_spare_dn(l, 0)
                sp.wait_ge(x_moved, l + 1)
                sp.wait_ge(xhat_dve, NT * (XHAT[2 * l + 1] + 1))
                sp.wait_ge(xhat_act, NT * (XHAT[2 * l + 1] + 1))
                load_gate(l, 1, 2, spare=True)
                sp.wait_ge(var_done, NT * (2 * l + 2))
                load_gate(l, 1, 3, spare=True)
                sp.wait_ge(M[l]["gate_used"], 1)
                load_gate(l, 2, 0)
                sp.wait_ge(M[l]["up_used"], 1)
                for j in range(SPARE_UP, QUAD):
                    load_up(l, 1, j)
                for j in range(1, QUAD):
                    load_gate(l, 2, j)
                for j in range(SPARE_UP):
                    load_up(l, 2, j)
                sp.wait_ge(M[l]["up_used"], 2)
                for j in range(SPARE_UP, QUAD):
                    load_up(l, 2, j)
                sp.wait_ge(M[l]["dn_used"], 1)
                load_dn(l, 2)

                def quad(e, turn):
                    sp.wait_ge(M[l]["gate_used"], turn)
                    for j in range(QUAD):
                        load_gate(l, e, j)
                    sp.wait_ge(M[l]["up_used"], turn)
                    for j in range(QUAD):
                        load_up(l, e, j)
                    sp.wait_ge(M[l]["dn_used"], turn)
                    load_dn(l, e)

                with sp.Fori(3, QUADS) as q:
                    quad(q, q)
                sp.wait_ge(nq_ok, l + 1)
                n = sp.value_load(nq[0:1, l:l + 1], min_val=QUADS, max_val=QUADS * MAX_ROUNDS)
                with sp.If(n > QUADS):
                    with sp.Fori(1, n - (QUADS - 1)) as i:
                        quad(sp.snap((i - 1) % QUADS, min_val=0, max_val=QUADS - 1), i + (QUADS - 1))
                return n

            n0 = experts(0, ((0, (vg_done, 4)), (1, (vg_done, 4)), (3, (v_done, 2)), (2, (u_done, 2))))
            sp.wait_ge(M[0]["up_used"], n0)
            sp.dma_start(wA, w_in1[:, :, 0:COL_A]).then_inc(gu_in[0], 32)
            sp.dma_start(wC, w_in1[:, :, COL_A + COL_B:ODD_IN]).then_inc(gu_in[2], 16)
            sp.dma_start(wuq, od_w_uq[0].rearrange("(p c) n -> p c n", c=QR // P)).then_inc(gu_in[2], 16)
            sp.dma_start(wB, w_in1[:, :, COL_A:COL_A + COL_B]).then_inc(gu_in[1], 32)
            sp.dma_start(wukv, od_w_ukv[0]).then_inc(gu_in[3], 32)
            load_w_out(w_out1)
            sp.wait_ge(M[0]["dn_used"], n0)
            experts(1, ((0, (pa_done, 2)), (1, (pb_done, 2)), (2, (q_up, 2)), (3, (kv_up, 2))))
            sp.dma_start(gfin, norm_final.rearrange("(o n) -> o n", o=1).broadcast_to([P, D])).then_inc(gfin_in, 16)
            for t in range(NT):
                sp.wait_ge(o_sem, t + 1)
                sp.dma_start(out[0, t * P:(t + 1) * P, :], xhat[:, t, :]).then_inc(stored, 16)
            sp.wait_ge(stored, 32)

        @block.gpsimd
        def _(pool):
            pool.memset(zeros[:, :], 0.0).then_inc(pads_done, 1)
            pool.memset(aT[:, :, 0:HALO], 0.0).then_inc(pads_done, 1)
            pool.memset(aT[:, :, HALO + SEQ:APAD], 0.0).then_inc(pads_done, 1)
            pool.memset(brt[:, :, GROUPS:EX0], LOW).then_inc(pads_done, 1)
            pool.memset(wrt[:, :, :, GROUPS:EX0], 0.0).then_inc(pads_done, 1)
            pool.wait_ge(route_in, 6 * 16)
            for l in range(2):
                pool.tensor_copy(wrt[:, l, :, 0:GROUPS], wgr[:, l, :, :]).then_inc(route_w_done, 1)
                for g in range(GROUPS):
                    pool.tensor_copy(
                        wrt[:, l, :, EX0 + g * PER_GROUP:EX0 + (g + 1) * PER_GROUP],
                        wrt_in[:, l, g, :].rearrange("p (k e) -> p k e", e=PER_GROUP)).then_inc(route_w_done, 1)

        @block.scalar
        def _(act):
            def square(i, t, src):
                act.activation(junk, src, ACT.Square, accum_out=stat[:, i, t, 0:1]).then_inc(act_sum, 1)

            def root(i, t):
                act.wait_ge(var_done, NT * i + t + 1)
                act.activation(stat[:, i, t, 3:4], stat[:, i, t, 2:3], ACT.Sqrt, bias=eps_col).then_inc(std_done, 1)

            def scale(i, t):
                act.wait_ge(rstd_done, NT * i + t + 1)
                act.activation(xhat[:, t, 512:D], X[:, t, 512:D], ACT.Copy,
                               scale=stat[:, i, t, 4:5]).then_inc(xhat_act, 1)

            def gains(i, t, half):
                act.wait_ge(norm_T, 4 * i + 2 * t + half + 1)
                for k in range(4 * half, 4 * half + 4):
                    j = act.activation(hT[:, k, t * P:(t + 1) * P],
                                       B[2 * t + half][:, (k % 4) * P:(k % 4 + 1) * P], ACT.Copy, scale=gain[:, i, k:k + 1])
                j.then_inc(hT_act, 1)

            def norm_first():
                for t in range(NT):
                    act.wait_ge(x_in[t], 16)
                    square(0, t, X[:, t, 0:512])
                    act.wait_ge(const_in, 16)
                    root(0, t)
                    scale(0, t)
                act.wait_ge(gain_in, 32)
                for t in range(NT):
                    gains(0, t, 1)

            def norm_experts(i):
                x0 = X_NEW[i]
                act.wait_ge(x_new, x0 + 1)
                square(i, 0, by_k(X[:, 0, :])[:, :, 0:4])
                root(i, 0)
                scale(i, 0)
                gains(i, 0, 0)
                act.wait_ge(x_new, x0 + 3)
                square(i, 1, by_k(X[:, 1, :])[:, :, 0:4])
                gains(i, 1, 0)
                root(i, 1)
                scale(i, 1)

            def norm_odd():
                act.wait_ge(M[0]["y_done"], 1)
                for t in range(NT):
                    act.activation(X[:, t, 512:D], B[4 + 2 * t + 1][:, :], ACT.Copy).then_inc(x_new_act, 1)
                for t in range(NT):
                    gains(2, t, 1)
                for t in range(NT):
                    act.wait_ge(x_new, X_NEW[2] + t + 1)
                    square(2, t, X[:, t, 0:512])
                    root(2, t)

            def norm_last():
                act.wait_ge(M[1]["y_done"], 1)
                for half in range(2):
                    act.activation((junk, junk_v)[half], B[6 + half][:, :], ACT.Square,
                                   accum_out=stat[:, 4, 1, half:half + 1]).then_inc(act_sum, 1)
                for t in range(NT):
                    root(4, t)

            def even_mixer():
                act.wait_ge(wsp_T, 1)
                act.activation(wspT[:, :, :].rearrange("p h t -> p (h t)"), B[1][:, :], ACT.Copy).then_inc(wsp_ok, 1)
                for c in range(CG):
                    act.wait_ge(vg_done, c + 1)
                    act.activation(sig[:, c, :], B[4 + c][:, SEQ:2 * SEQ], ACT.Sigmoid).then_inc(sig_done, 1)
                def diagonals(taps):
                    for j in taps:
                        if j >= DIAGS:
                            act.wait_ge(diag_used, j - DIAGS + 1)
                        act.activation(diag[:, j % DIAGS, :], ident, ACT.Copy, scale=chanp[:, CG - 1, j:j + 1]).then_inc(diag_ok, 1)

                act.wait_ge(taps_ok, 1)
                diagonals(range(DIAGS))
                for t in range(NT):
                    act.wait_ge(v_done, t + 1)
                    act.activation(vt[:, t, :], B[t][:, :], ACT.Gelu_apprx_tanh).then_inc(gelu_v, 1)
                diagonals(range(DIAGS, PE_TAPS))
                act.wait_ge(vvar, NT)
                act.activation(vstd[:, :], vag[:, :, 1], ACT.Sqrt, bias=eps_col).then_inc(vstd_ok, 1)
                act.wait_ge(diag_used, PE_TAPS)
                act.activation(conv[:, CG - 1, :], B[4][:, 0:SEQ], ACT.Identity,
                               bias=chanp[:, CG - 1, TAPS:TAPS + 1]).then_inc(conv3_ok, 1)
                act.wait_ge(vrs_ok, 1)
                act.wait_ge(gelu_v, NT)
                for t in range(NT):
                    for h in range(CG):
                        n = t * CG + h
                        i = act.activation(vn[:, t, h * P:(h + 1) * P], vt[:, t, h * P:(h + 1) * P], ACT.Identity,
                                           scale=vrs[:, n:n + 1], bias=vnb[:, n:n + 1])
                    i.then_inc(v_scaled, 1)
                def conv_roots(b):
                    act.wait_ge(cen_done, b + 1)
                    act.activation(sq[:, 2 * b:2 * b + 2, :], conv[:, 2 * b:2 * b + 2, :], ACT.Square).then_inc(sq_done, 1)
                    act.wait_ge(sq_done, b + 1)
                    act.wait_ge(cvar_done, b + 1)
                    act.activation(sq[:, 2 * b:2 * b + 2, :].rearrange("p c s -> p (c s)"), B[6 + b][:, :],
                                   ACT.Sqrt, bias=eps_col).then_inc(cstd_ok, 1)

                conv_roots(0)
                for b in range(2):
                    act.wait_ge(u_done, b + 1)
                    act.activation(uT[:, 2 * b:2 * b + 2, :].rearrange("p c s -> p (c s)"), B[2 + b][:, :],
                                   ACT.Gelu_apprx_tanh).then_inc(gelu_u, 1)
                act.preload_act_table(ACT.Sqrt)
                conv_roots(1)
                act.preload_act_table(ACT.Silu)
                for c in range(CG):
                    act.wait_ge(cn_done, c // 2 + 1)
                    act.activation(mixT[:, c, :], conv[:, c, :], ACT.Silu, scale=chanp[:, c, TAPS + 1:TAPS + 2],
                                   bias=chanp[:, c, TAPS + 2:TAPS + 3]).then_inc(silu_done, 1)
                act.preload_act_table(ACT.Sqrt)

            def odd_mixer():
                for t in range(NT):
                    act.wait_ge(pa_done, t + 1)
                    act.wait_ge(rstd_done, NT * 2 + t + 1)
                    act.activation(lsq[:, t, 0:QR], B[4 + t][:, 0:QR], ACT.Square, scale=stat[:, 2, t, 4:5],
                                   accum_out=lst[:, 0, 0, t:t + 1]).then_inc(lsum, 1)
                    act.activation(lsq[:, t, QR:QR + KVR], B[4 + t][:, QR:QR + KVR], ACT.Square, scale=stat[:, 2, t, 4:5],
                                   accum_out=lst[:, 0, 1, t:t + 1]).then_inc(lsum, 1)
                act.wait_ge(pc_done, 1)
                for t in range(NT):
                    i = act.activation(ksvs[:, t, :], B[0][:, t * COL_C:(t + 1) * COL_C], ACT.Copy, scale=stat[:, 2, t, 4:5])
                i.then_inc(ks_ok, 1)
                act.wait_ge(lvar, 2)
                act.activation(lst[:, 2, :, :], lst[:, 1, :, :], ACT.Sqrt).then_inc(lstd, 1)
                for t in range(NT):
                    act.wait_ge(pb_done, t + 1)
                    act.activation(qs[:, t, :].rearrange("p (r g d) -> p g r d", g=KVH, d=SWA_D),
                                   B[6 + t][:, :].rearrange("p (g r d) -> p g r d", g=KVH, d=SWA_D), ACT.Copy,
                                   scale=stat[:, 2, t, 4:5]).then_inc(qs_ok, 1)
                for t in range(NT):
                    act.wait_ge(q_up, t + 1)
                    for b, (h0, nh) in enumerate(((0, 5), (5, 3))):
                        src = B[4 + 2 * t + b][:, 0:nh * QK].rearrange("p (h d) -> p h d", d=QK)
                        dst = qf[:, t, h0 * QK:(h0 + nh) * QK].rearrange("p (h d) -> p h d", d=QK)
                        act.activation(dst[:, :, 0:NOPE], src[:, :, 0:NOPE], ACT.Copy).then_inc(q_nope, 1)
                for t in range(NT):
                    act.wait_ge(kv_up, t + 1)
                    for b in range(2):
                        src = B[2 * t + b][:, :].rearrange("p (h d) -> p h d", d=NOPE + VD)
                        act.activation(kf[:, t, 4 * b:4 * b + 4, 0:NOPE], src[:, :, 0:NOPE], ACT.Copy).then_inc(k_nope, 1)
                for n, (dst, rows, views) in enumerate(head_blocks):
                    if n % 2:
                        act.wait_ge(head_T, n + 1)
                        act.activation(dst, head_bank[n][0:rows, 0:len(views) * P], ACT.Copy).then_inc(headT_act, 1)
                def unit_exp(u):
                    window = unit[u][0]
                    act.wait_ge(negmax, u + 1)
                    if u >= 2:
                        act.wait_ge(prob_T, u - 1)
                    for i in range(2):
                        src = sw[:, u % 2, i, :] if window else score_bank(u, i)
                        act.activation(prob[:, u % 2, i, :], src, ACT.Exp, bias=us[:, u, 1, i:i + 1],
                                       scale=SWA_SCALE if window else MLA_SCALE,
                                       accum_out=us[:, u, 2, i:i + 1]).then_inc(expd, 1)
                    if window:
                        act.wait_ge(sink_d, before_w[u] + 1)
                        act.activation(us[:, u, 3, :], us[:, u, 3, :], ACT.Exp).then_inc(sink_e, 1)

                def unit_pT(u):
                    act.wait_ge(prob_T, u + 1)
                    if u >= 2:
                        act.wait_ge(pv, u - 1)
                    act.activation(pT[:, u % 2, :, :].rearrange("p a b -> p (a b)"), B[2 + u % 2][:, :],
                                   ACT.Copy).then_inc(pT_ok, 1)

                for u in range(UNITS + 2):
                    if u >= 2:
                        unit_pT(u - 2)
                    if u < UNITS:
                        unit_exp(u)
                for b in range(1, 4, 2):
                    act.wait_ge(o_T, b + 1)
                    act.activation(mixT[:, 2 * b:2 * b + 2, :].rearrange("p c s -> p (c s)"), B[b][:, :],
                                   ACT.Copy).then_inc(oT_act, 1)
                act.preload_act_table(ACT.Sqrt)

            def route(l):
                act.preload_act_table(ACT.Exp)
                act.wait_ge(ex_in, 2 * l + 2)
                act.activation(exo[:, :, 4], exin[:, :, 4], ACT.Exp).then_inc(ex_out, 1)
                for t in range(NT):
                    act.activation(exo[:, t, 0:GROUPS], exin[:, t, 0:GROUPS], ACT.Exp,
                                   accum_out=gsum[:, t:t + 1]).then_inc(ex_out, 1)
                act.wait_ge(rows_T, 2 * l + 1)
                act.activation(wrow[:, :, :].rearrange("p a s -> p (a s)"), B[3][:, :], ACT.Copy).then_inc(rows_ok, 1)
                act.preload_act_table(ACT.Silu)
                act.wait_ge(rows_T, 2 * l + 2)
                act.activation(keyrow[:, :, :].rearrange("p a s -> p (a s)"), B[2][:, :], ACT.Copy).then_inc(rows_ok, 1)

            def experts(l):
                m = M[l]
                act.wait_ge(nq_ok, l + 1)
                n = act.value_load(nq[0:1, l:l + 1], min_val=QUADS, max_val=QUADS * MAX_ROUNDS)
                with act.Fori(0, n) as q:
                    act.wait_ge(m["gath1"], q + 1)
                    for k in range(4, KD):
                        i = act.activation(xs[:, k, :], B[1][:, (k - 4) * P:(k - 3) * P], ACT.Copy,
                                           scale=gain[:, 2 * l + 1, k:k + 1])
                    i.then_inc(m["xs1"], 1)
                    act.wait_ge(m["gate_used"], q + 1)
                    act.activation(sg[:, :], B[2][:, 0:F], ACT.Silu).then_inc(m["silu_g"], 1)
                    act.wait_ge(m["dn_used"], q + 1)
                    act.activation(ys[:, 512:1024], B[1][:, :], ACT.Copy).then_inc(m["ys1"], 1)
                act.preload_act_table(ACT.Sqrt)

            act.preload_act_table(ACT.Sqrt)
            norm_first()
            even_mixer()
            norm_experts(1)
            route(0)
            experts(0)
            norm_odd()
            odd_mixer()
            norm_experts(3)
            route(1)
            experts(1)
            norm_last()

        @block.vector
        def _(dve):
            steps = [0]

            def step(ins):
                steps[0] += 1
                ins.then_inc(dve_step, 1)
                return steps[0]

            def chain(ins):
                dve.wait_ge(dve_step, step(ins))

            def residual(i, t, half):
                dve.wait_ge(out_done, 2 * (i - 1) + 2 * t + half + 1)
                v = by_k(X[:, t, :])[:, :, 4 * half:4 * half + 4]
                dve.tensor_tensor(v, B[4 + 2 * t + half][:, :].rearrange("s (p k) -> s p k", k=4), v, ALU.add
                                  ).then_inc(x_new, 1)

            def square(i, t, src, sink):
                dve.tensor_tensor_reduce(out=sink, in0=src, in1=src, scale=1.0, scalar=0.0, op0=ALU.mult, op1=ALU.add,
                                         accum_out=stat[:, i, t, 1:2]).then_inc(dve_sum, 1)

            def mean(i, t):
                dve.wait_ge(dve_sum, NT * i + t + 1)
                dve.wait_ge(act_sum, NT * i + t + 1)
                dve.tensor_scalar(stat[:, i, t, 2:3], stat[:, i, t, 0:1], stat[:, i, t, 1:2], 1.0 / D,
                                  ALU.add, ALU.mult).then_inc(var_done, 1)

            def inverse(i, t):
                dve.wait_ge(std_done, NT * i + t + 1)
                dve.reciprocal(stat[:, i, t, 4:5], stat[:, i, t, 3:4]).then_inc(rstd_done, 1)

            def scale(i, t):
                dve.wait_ge(rstd_done, NT * i + t + 1)
                dve.tensor_scalar(xhat[:, t, 0:512], X[:, t, 0:512], stat[:, i, t, 4:5], None,
                                  ALU.mult).then_inc(xhat_dve, 1)

            def gains(i, t, half):
                dve.wait_ge(norm_T, 4 * i + 2 * t + half + 1)
                g = slice(4 * half, 4 * half + 4)
                dve.tensor_tensor(hT[:, g, t * P:(t + 1) * P], B[2 * t + half][:, :].rearrange("p (k s) -> p k s", s=P),
                                  gain[:, i, g].unsqueeze(2).broadcast_to([P, 4, P]), ALU.mult).then_inc(hT_dve, 1)

            def norm_first():
                for t in range(NT):
                    dve.wait_ge(x_in[t], 16)
                    square(0, t, X[:, t, 512:D], junk_v)
                    mean(0, t)
                    inverse(0, t)
                    scale(0, t)
                dve.wait_ge(gain_in, 32)
                for t in range(NT):
                    gains(0, t, 0)

            def norm_experts(i):
                def second_half(t):
                    dve.wait_ge(x_new, X_NEW[i] + 2 * t + 2)
                    square(i, t, by_k(X[:, t, :])[:, :, 4:8], junk_v.rearrange("s (p k) -> s p k", k=4))

                residual(i, 0, 0)
                residual(i, 0, 1)
                second_half(0)
                mean(i, 0)
                inverse(i, 0)
                scale(i, 0)
                residual(i, 1, 0)
                gains(i, 0, 1)
                residual(i, 1, 1)
                second_half(1)
                mean(i, 1)
                gains(i, 1, 1)
                inverse(i, 1)
                scale(i, 1)

            def norm_odd():
                for t in range(NT):
                    dve.tensor_copy(X[:, t, 0:512], B[4 + 2 * t][:, :]).then_inc(x_new, 1)
                for t in range(NT):
                    gains(2, t, 0)
                for t in range(NT):
                    dve.wait_ge(x_new_act, t + 1)
                    square(2, t, X[:, t, 512:D], junk_v)
                    mean(2, t)
                    inverse(2, t)

            def norm_last():
                for t in range(NT):
                    if t == 0:
                        for half in range(2):
                            k = step(dve.bn_stats(vst[:, half, :], B[4 + half][:, :]))
                        dve.wait_ge(dve_step, k)
                        chain(dve.bn_aggr(vag[:, 0, :], vst[:, 0:2, :].rearrange("p c n -> p (c n)")))
                        dve.scalar_tensor_tensor(out=stat[:, 4, 0, 2:3], in0=vag[:, 0, 0:1], scalar=vag[:, 0, 0:1],
                                                 in1=vag[:, 0, 1:2], op0=ALU.mult, op1=ALU.add).then_inc(var_done, 1)
                    else:
                        dve.wait_ge(act_sum, NT * 4 + 2)
                        dve.tensor_scalar(stat[:, 4, 1, 2:3], stat[:, 4, 1, 0:1], stat[:, 4, 1, 1:2], 1.0 / D,
                                          ALU.add, ALU.mult).then_inc(var_done, 1)
                for t in range(NT):
                    inverse(4, t)
                dve.wait_ge(gfin_in, 16)
                for t in range(NT):
                    dve.wait_ge(rstd_done, NT * 4 + t + 1)
                    for half in range(2):
                        c = slice(half * 512, (half + 1) * 512)
                        i = dve.scalar_tensor_tensor(out=xhat[:, t, c], in0=B[4 + 2 * t + half][:, :],
                                                     scalar=stat[:, 4, t, 4:5], in1=gfin[:, c], op0=ALU.mult, op1=ALU.mult)
                    i.then_inc(o_sem, 1)

            def even_mixer():
                dve.wait_ge(chan_T, 1)
                dve.tensor_copy(chanp[:, :, :].rearrange("p c r -> p (c r)"), B[0][:, 0:CG * NROW]).then_inc(taps_ok, 1)
                dve.wait_ge(taps_ok, 1)
                dve.wait_ge(pads_done, 5)

                def gate_value(c):
                    dve.wait_ge(sig_done, c + 1)
                    dve.tensor_tensor(aT[:, c, HALO:HALO + SEQ], B[4 + c][:, 0:SEQ], sig[:, c, :], ALU.mult).then_inc(a_done, 1)

                last = {}

                def tap(c, j):
                    src, w = aT[:, c, j:j + SEQ], chanp[:, c, j:j + 1]
                    if j == 0:
                        last[c] = step(dve.tensor_scalar(conv[:, c, :], src, w, chanp[:, c, TAPS:TAPS + 1],
                                                         ALU.mult, ALU.add))
                        return
                    if c == CG - 1 and j == PE_TAPS:
                        dve.wait_ge(conv3_ok, 1)
                    else:
                        dve.wait_ge(dve_step, last[c])
                    ins = dve.scalar_tensor_tensor(out=conv[:, c, :], in0=src, scalar=w, in1=conv[:, c, :],
                                                   op0=ALU.mult, op1=ALU.add)
                    if j < TAPS - 1:
                        last[c] = step(ins)
                    else:
                        ins.then_inc(conv_done, 1)

                def v_stats():
                    for t in range(NT):
                        dve.wait_ge(gelu_v, t + 1)
                        for h in range(CG):
                            k = step(dve.bn_stats(vst[:, t * CG + h, :], vt[:, t, h * P:(h + 1) * P]))
                        dve.wait_ge(dve_step, k)
                        for h in range(CG):
                            i = dve.bn_aggr(vag[:, t * CG + h, :], vst[:, t * CG + h, :])
                        i.then_inc(vvar, 1)

                AHEAD = 6
                gate_value(0)
                gate_value(1)
                dve.wait_ge(a_done, 2)
                for j in range(AHEAD):
                    tap(0, j)
                    tap(1, j)
                gate_value(2)
                gate_value(3)
                dve.wait_ge(a_done, 4)
                LATE, STATS_AT = 12, 20
                for j in range(AHEAD, TAPS):
                    tap(0, j)
                    tap(1, j)
                    if j >= LATE:
                        tap(2, j - LATE)
                    if j == STATS_AT:
                        v_stats()
                dve.wait_ge(vvar, NT)
                dve.wait_ge(vstd_ok, 1)
                k = step(dve.reciprocal(vrs[:, :], vstd[:, :]))
                tap(2, TAPS - LATE)
                dve.wait_ge(dve_step, k)
                dve.scalar_tensor_tensor(out=vnb[:, :], in0=vag[:, :, 0], scalar=-1.0, in1=vrs[:, :],
                                         op0=ALU.mult, op1=ALU.mult).then_inc(vrs_ok, 1)
                for j in range(TAPS - LATE + 1, TAPS - 5):
                    tap(2, j)
                    if j > TAPS - 5 - (TAPS - PE_TAPS) - 1:
                        tap(3, j + 5)
                dve.wait_ge(v_scaled, NT)
                dve.wait_ge(vec_in, 2 * 16)
                k = step(dve.tensor_tensor(vn[:, :, :], vn[:, :, :], vgb[:, 0:1, :].broadcast_to([P, NT, CG * P]), ALU.mult))
                tap(2, TAPS - 5)
                dve.wait_ge(dve_step, k)
                dve.tensor_tensor(vn[:, :, :], vn[:, :, :], vgb[:, 1:2, :].broadcast_to([P, NT, CG * P]), ALU.add
                                  ).then_inc(vn_done, 1)
                tap(2, TAPS - 4)

                def centre(b):
                    c = conv[:, 2 * b:2 * b + 2, :].rearrange("p c s -> p (c s)")
                    dve.wait_ge(mean_done, b + 1)
                    dve.tensor_tensor(c, c, B[6 + b][:, :], ALU.subtract).then_inc(cen_done, 1)

                def roots(b):
                    s = sq[:, 2 * b:2 * b + 2, :].rearrange("p c s -> p (c s)")
                    dve.wait_ge(cstd_ok, b + 1)
                    return step(dve.reciprocal(s, s))

                def scale(b, k):
                    c = conv[:, 2 * b:2 * b + 2, :].rearrange("p c s -> p (c s)")
                    s = sq[:, 2 * b:2 * b + 2, :].rearrange("p c s -> p (c s)")
                    dve.wait_ge(dve_step, k)
                    dve.wait_ge(cen_done, b + 1)
                    dve.tensor_tensor(c, c, s, ALU.mult).then_inc(cn_done, 1)

                dve.wait_ge(conv_done, 2)
                centre(0)
                for j in range(TAPS - 3, TAPS):
                    tap(2, j)
                dve.wait_ge(conv_done, 4)
                centre(1)
                for b in range(2):
                    dve.wait_ge(gelu_u, b + 1)
                    dve.wait_ge(sv_done, b + 1)
                    dve.tensor_tensor(mixT[:, 4 + 2 * b:6 + 2 * b, :].rearrange("p c s -> p (c s)"), B[b][:, :],
                                      uT[:, 2 * b:2 * b + 2, :].rearrange("p c s -> p (c s)"), ALU.mult).then_inc(gated, 1)
                for b in range(2):
                    scale(b, roots(b))

            def odd_mixer():
                dve.wait_ge(odd_in, 3 * 16)
                dve.wait_ge(lsum, 4)
                dve.tensor_scalar(lst[:, 1, 0, :], lst[:, 0, 0, :], 1.0 / QR, EPS, ALU.mult, ALU.add).then_inc(lvar, 1)
                dve.tensor_scalar(lst[:, 1, 1, :], lst[:, 0, 1, :], 1.0 / KVR, EPS, ALU.mult, ALU.add).then_inc(lvar, 1)

                def rope(dst, src, n, t, first=False):
                    def tab(name):
                        a = CONST[name][0] + t * ROPE
                        return cst[:, a:a + ROPE].unsqueeze(1).broadcast_to([P, n, ROPE])
                    cos, sin = tab("cos"), tab("sin")
                    a = rt1[:, 0:n * ROPE].rearrange("p (h d) -> p h d", d=ROPE)
                    b = rt2[:, 0:n * ROPE].rearrange("p (h d) -> p h d", d=ROPE)
                    H = ROPE // 2
                    dve.wait_ge(dve_step, steps[0])
                    step(dve.tensor_tensor(a, src, cos, ALU.mult))
                    step(dve.tensor_tensor(b[:, :, 0:H], src[:, :, H:ROPE], sin[:, :, 0:H], ALU.mult))
                    chain(dve.tensor_tensor(b[:, :, H:ROPE], src[:, :, 0:H], sin[:, :, H:ROPE], ALU.mult))
                    return dve.tensor_tensor(dst, a, b, ALU.add)

                for t in range(NT):
                    step(rope(kpe[:, t:t + 1, :], B[4 + t][:, QR + KVR:COL_A].rearrange("p (h d) -> p h d", h=1), 1, t))
                dve.wait_ge(dve_step, steps[0])
                for t in range(NT):
                    dve.tensor_scalar(kf[:, t, :, NOPE:QK], kpe[:, t:t + 1, :].broadcast_to([P, HEADS, ROPE]),
                                      stat[:, 2, t, 4:5], None, ALU.mult).then_inc(k_rope, 1)
                dve.wait_ge(lstd, 1)
                dve.reciprocal(lst[:, 3, :, :], lst[:, 2, :, :]).then_inc(lrs, 1)
                dve.wait_ge(lrs, 1)
                for t in range(NT):
                    dve.tensor_scalar(lat[:, t, 0:QR], B[4 + t][:, 0:QR], lst[:, 3, 0, t:t + 1], stat[:, 2, t, 4:5],
                                      ALU.mult, ALU.mult).then_inc(cq_ok, 1)
                for t in range(NT):
                    dve.tensor_scalar(lat[:, t, QR:QR + KVR], B[4 + t][:, QR:QR + KVR], lst[:, 3, 1, t:t + 1], stat[:, 2, t, 4:5],
                                      ALU.mult, ALU.mult).then_inc(ckv_ok, 1)
                dve.wait_ge(lat_T, 1)
                for c in range(QR // P):
                    dve.tensor_scalar(cqT[:, c, :], B[1][:, c * SEQ:(c + 1) * SEQ], g_cq[:, c:c + 1], None,
                                      ALU.mult).then_inc(latT_ok, 1)
                dve.wait_ge(lat_T, 2)
                dve.tensor_scalar(ckvT[:, :], B[2][:, 0:SEQ], g_ckv[:, 0:1], None, ALU.mult).then_inc(latT_ok, 1)
                for t in range(NT):
                    dve.wait_ge(q_up, t + 1)
                    for b, (h0, nh) in enumerate(((0, 5), (5, 3))):
                        src = B[4 + 2 * t + b][:, 0:nh * QK].rearrange("p (h d) -> p h d", d=QK)
                        dst = qf[:, t, h0 * QK:(h0 + nh) * QK].rearrange("p (h d) -> p h d", d=QK)
                        dve.wait_ge(q_nope, 2 * t + b + 1)
                        rope(dst[:, :, NOPE:QK], src[:, :, NOPE:QK], nh, t).then_inc(q_rope, 1)
                        dve.wait_ge(q_rope, 2 * t + b + 1)
                for t in range(NT):
                    dve.wait_ge(kv_up, t + 1)
                    for b in range(2):
                        src = B[2 * t + b][:, :].rearrange("p (h d) -> p h d", d=NOPE + VD)
                        dve.wait_ge(k_nope, 2 * t + b + 1)
                        dve.tensor_copy(vm[:, t, 4 * b:4 * b + 4, :], src[:, :, NOPE:NOPE + VD]).then_inc(v_ok, 1)
                for n, (dst, rows, views) in enumerate(head_blocks):
                    if n % 2 == 0:
                        dve.wait_ge(head_T, n + 1)
                        dve.tensor_copy(dst, head_bank[n][0:rows, 0:len(views) * P]).then_inc(headT_dve, 1)

                def unit_max(u):
                    window, w, t = unit[u]
                    dve.wait_ge(score, u + 1)
                    if window:
                        if u >= 2:
                            dve.wait_ge(expd, 2 * (u - 1))
                        d0 = CONST["dist"][0] + t * SEQ
                        for i in range(2):
                            slope = 2.0 ** -(w + 4 * i + 1)
                            k = step(dve.scalar_tensor_tensor(out=sw[:, u % 2, i, :], in0=cst[:, d0:d0 + SEQ],
                                                              scalar=-slope / SWA_SCALE, in1=score_bank(u, i),
                                                              op0=ALU.mult, op1=ALU.add))
                        dve.wait_ge(dve_step, k)
                        i = dve.tensor_reduce(us[:, u, 0, :], sw[:, u % 2, :, :], AX, ALU.max)
                        i.then_inc(biased, 1)
                        dve.wait_ge(biased, before_w[u] + 1)
                        chain(dve.scalar_tensor_tensor(out=us[:, u, 0, :], in0=us[:, u, 0, :], scalar=SWA_SCALE,
                                                       in1=sink[:, w:HEADS:4], op0=ALU.mult, op1=ALU.max))
                        dve.tensor_scalar(us[:, u, 1, :], us[:, u, 0, :], -1.0, None, ALU.mult).then_inc(negmax, 1)
                        dve.tensor_tensor(us[:, u, 3, :], sink[:, w:HEADS:4], us[:, u, 0, :], ALU.subtract).then_inc(sink_d, 1)
                    else:
                        for i in range(2):
                            k = step(dve.tensor_reduce(us[:, u, 0, i:i + 1], score_bank(u, i), AX, ALU.max))
                        dve.wait_ge(dve_step, k)
                        dve.tensor_scalar(us[:, u, 1, :], us[:, u, 0, :], -MLA_SCALE, None, ALU.mult).then_inc(negmax, 1)

                def unit_out(u):
                    window, w, t = unit[u]
                    dve.wait_ge(expd, 2 * u + 2)
                    total = us[:, u, 2, :]
                    if window:
                        dve.wait_ge(sink_e, before_w[u] + 1)
                        total = us[:, u, 4, :]
                        chain(dve.tensor_tensor(total, us[:, u, 2, :], us[:, u, 3, :], ALU.add))
                    chain(dve.reciprocal(us[:, u, 5, :], total))
                    if window:
                        dst = osb[:, t, HEADS * VD:D].rearrange("p (g r d) -> p g r d", g=KVH, d=SWA_D)[:, :, w, :]
                    else:
                        dst = osb[:, t, w * P:(w + 1) * P].rearrange("p (g d) -> p g d", g=2)
                    dve.wait_ge(pv, u + 1)
                    dve.tensor_tensor(dst, B[4 + u % 2][:, 0:P].rearrange("p (g d) -> p g d", g=2),
                                      us[:, u, 5, :].unsqueeze(2).broadcast_to([P, 2, VD]), ALU.mult).then_inc(o_ok, 1)

                def untransposed(b):
                    dve.wait_ge(o_T, b + 1)
                    dve.tensor_copy(mixT[:, 2 * b:2 * b + 2, :].rearrange("p c s -> p (c s)"), B[b][:, :]).then_inc(oT_dve, 1)

                dve.wait_ge(dist_in, 16)
                for u in range(UNITS + 3):
                    if u < UNITS:
                        unit_max(u)
                    if u == UNITS + 2:
                        untransposed(0)
                    if u >= 3:
                        unit_out(u - 3)
                untransposed(2)

            def fill_slots(l, mine, numbers=None):
                m = M[l]
                if numbers is not None:
                    dve.wait_ge(m["moe_step"], numbers)
                for t in range(NT):
                    dve.tensor_scalar(pick[:, t, :], slot_row[:, :], key[:, t, 0:1], None, ALU.is_equal
                                      ).then_inc(m["moe_step"], 1)
                for t in range(NT):
                    dve.wait_ge(m["moe_step"], mine + t)
                    dve.scalar_tensor_tensor(out=pick[:, t, :], in0=slot_row[:, :], scalar=key[:, t, 1:2],
                                             in1=pick[:, t, :], op0=ALU.is_equal, op1=ALU.add).then_inc(m["pick_ok"], 1)

            def route(l):
                if l == 0:
                    dve.wait_ge(route_in, 6 * 16)
                dve.wait_ge(logits, l + 1)
                for t in range(NT):
                    k = step(dve.scalar_tensor_tensor(out=lg[:, t, :], in0=B[0][:, t * 64:t * 64 + NL],
                                                      scalar=stat[:, 2 * l + 1, t, 4:5], in1=brt[:, l, :],
                                                      op0=ALU.mult, op1=ALU.add))
                dve.wait_ge(dve_step, k)
                for t in range(NT):
                    k = step(dve.max(gm8[:, t, :], gl[:, t, :]))
                dve.wait_ge(dve_step, k)
                for t in range(NT):
                    step(dve.max_index(gi8[:, t, :], gm8[:, t, :], gl[:, t, :]))
                dve.wait_ge(dve_step, steps[0])
                chain(dve.tensor_copy(gif[:, :], gi8[:, :, 0]))
                iota_g = C("iota_g").unsqueeze(1).broadcast_to([P, NT, GROUPS])
                chain(dve.tensor_tensor(goh[:, :, :], iota_g, gif[:, :].unsqueeze(2).broadcast_to([P, NT, GROUPS]),
                                        ALU.is_equal))
                for t in range(NT):
                    k = step(dve.tensor_tensor(selp[:, t, :].rearrange("p (g e) -> p g e", g=GROUPS),
                                               rl[:, t, :].rearrange("p (g e) -> p g e", g=GROUPS),
                                               goh[:, t, :].unsqueeze(2).broadcast_to([P, GROUPS, PER_GROUP]), ALU.mult))
                dve.wait_ge(dve_step, k)
                chain(dve.tensor_reduce(sel[:, :, :], selp[:, :, :].rearrange("p t (g e) -> p t e g", g=GROUPS), AX, ALU.add))
                for t in range(NT):
                    k = step(dve.max(em8[:, t, :], sel[:, t, :]))
                dve.wait_ge(dve_step, k)
                for t in range(NT):
                    step(dve.max_index(ei8[:, t, :], em8[:, t, :], sel[:, t, :]))
                dve.wait_ge(dve_step, steps[0])
                chain(dve.tensor_copy(eif[:, :, :], ei8[:, :, 0:2]))
                chain(dve.scalar_tensor_tensor(out=eid[:, :, :], in0=gif[:, :].unsqueeze(2).broadcast_to([P, NT, 2]),
                                               scalar=float(PER_GROUP), in1=eif[:, :, :], op0=ALU.mult, op1=ALU.add))
                e4 = eoh[:, :, :, :].rearrange("p t k e -> p (t k) e")
                eid4 = eid[:, :, :].rearrange("p t k -> p (t k)")
                chain(dve.tensor_tensor(e4, C("iota_e").unsqueeze(1).broadcast_to([P, NT * 2, EXPERTS]),
                                        eid4.unsqueeze(2).broadcast_to([P, NT * 2, EXPERTS]), ALU.is_equal))
                dve.tensor_tensor(member[:, :, :], eoh[:, :, 0, :], eoh[:, :, 1, :], ALU.add).then_inc(member_ok, 1)
                dve.tensor_tensor(exin[:, :, 4], em8[:, :, 1], em8[:, :, 0], ALU.subtract).then_inc(ex_in, 1)
                dve.tensor_tensor(exin[:, :, 0:GROUPS], gl[:, :, 0:GROUPS],
                                  gm8[:, :, 0:1].broadcast_to([P, NT, GROUPS]), ALU.subtract).then_inc(ex_in, 1)
                step(dve.tensor_scalar(eid32[:, :, :], eid[:, :, :], float(SLOTS), None, ALU.mult))
                step(dve.tensor_copy(slot_row[:, :], C("slot_row")))
                step(dve.tensor_copy(slot_col[:, :], C("slot_col")))
                dve.wait_ge(ex_out, (NT + 1) * (l + 1))
                chain(dve.scalar_tensor_tensor(out=den[:, :], in0=exo[:, :, 4], scalar=1.0, in1=gsum[:, :],
                                               op0=ALU.add, op1=ALU.mult))
                chain(dve.reciprocal(weight[:, :, 0], den[:, :]))
                dve.tensor_tensor(weight[:, :, 1], weight[:, :, 0], exo[:, :, 4], ALU.mult).then_inc(weight_ok, 1)
                dve.wait_ge(ranks, l + 1)
                for t in range(NT):
                    k = step(dve.tensor_tensor(rkp[:, t, :, :], eoh[:, t, :, :],
                                               B[1][:, t * EXPERTS:(t + 1) * EXPERTS].unsqueeze(1).broadcast_to([P, 2, EXPERTS]),
                                               ALU.mult))
                dve.wait_ge(dve_step, k)
                rank4 = rank[:, :, :].rearrange("p t k -> p (t k)")
                chain(dve.tensor_reduce(rank4, rkp[:, :, :, :].rearrange("p t k e -> p (t k) e"), AX, ALU.add))
                NS = MAX_ROUNDS - 1
                rge4 = rge[:, :, :, :].rearrange("p t k e -> p (t k) e")
                chain(dve.tensor_tensor(rge4, rank4.unsqueeze(2).broadcast_to([P, NT * 2, NS]),
                                        C("steps").unsqueeze(1).broadcast_to([P, NT * 2, NS]), ALU.is_ge))
                turn4 = turn[:, :, :].rearrange("p t k -> p (t k)")
                key04 = key0[:, :, :].rearrange("p t k -> p (t k)")
                key4 = key[:, :, :].rearrange("p t k -> p (t k)")
                step(dve.tensor_reduce(turn4, rge4, AX, ALU.add))
                chain(dve.tensor_tensor(key04, rank4, eid32[:, :, :].rearrange("p t k -> p (t k)"), ALU.add))
                dve.scalar_tensor_tensor(out=key4, in0=turn4, scalar=float(ROUND - SLOTS), in1=key04,
                                         op0=ALU.mult, op1=ALU.add).then_inc(key_ok, 1)
                dve.wait_ge(key_ok, l + 1)
                dve.wait_ge(dve_step, steps[0])
                fill_slots(l, 1)
                chain(dve.tensor_reduce(cmax[:, :], B[1][:, 64:64 + EXPERTS], AX, ALU.max))
                chain(dve.tensor_scalar(cge[:, :], C("steps"), cmax[:, 0:1], None, ALU.is_lt))
                chain(dve.tensor_reduce(extra[:, :], cge[:, :], AX, ALU.add))
                dve.tensor_scalar(nq[:, l:l + 1], extra[:, :], float(QUADS), float(QUADS), ALU.mult, ALU.add).then_inc(nq_ok, 1)

            def experts(l):
                m = M[l]
                PER, BASE = 5, 2
                dve.wait_ge(nq_ok, l + 1)
                n = dve.value_load(nq[0:1, l:l + 1], min_val=QUADS, max_val=QUADS * MAX_ROUNDS)
                with dve.Fori(0, n) as q:
                    dve.wait_ge(m["gath0"], q + 1)
                    for k in range(4):
                        i = dve.tensor_scalar(xs[:, k, :], B[0][:, k * P:(k + 1) * P], gain[:, 2 * l + 1, k:k + 1],
                                              None, ALU.mult)
                    i.then_inc(m["xs0"], 1)
                    dve.wait_ge(rows_ok, 2 * l + 2)
                    dve.scalar_tensor_tensor(out=back[:, :, :].rearrange("p a s -> p (a s)"),
                                             in0=keyrow[:, :, :].rearrange("p a s -> p (a s)"), scalar=slot_col[:, 0:1],
                                             in1=wrow[:, :, :].rearrange("p a s -> p (a s)"),
                                             op0=ALU.is_equal, op1=ALU.mult).then_inc(m["moe_step"], 1)
                    dve.wait_ge(m["moe_step"], q * PER + (BASE + 1))
                    dve.tensor_tensor(backs[:, :], back[:, 0, :], back[:, 1, :], ALU.add).then_inc(m["back_ok"], 1)
                    dve.tensor_scalar(slot_row[:, :], slot_row[:, :], float(P), None, ALU.add).then_inc(m["moe_step"], 1)
                    dve.tensor_scalar(slot_col[:, :], slot_col[:, :], float(P), None, ALU.add).then_inc(m["moe_step"], 1)
                    dve.wait_ge(m["silu_g"], q + 1)
                    dve.wait_ge(m["up_used"], q + 1)
                    dve.tensor_tensor(hid[:, :], B[3][:, 0:F], sg[:, :], ALU.mult).then_inc(m["hid_ok"], 1)
                    dve.wait_ge(m["hid_T"], q + 1)
                    dve.tensor_copy(hidT[:, :, :].rearrange("p c s -> p (c s)"), B[2][:, 0:FC * P]).then_inc(m["hidT_ok"], 1)
                    dve.wait_ge(m["gath1"], q + 1)
                    fill_slots(l, q * PER + BASE + 4, q * PER + BASE + 2)
                    dve.wait_ge(m["down0"], q + 1)
                    dve.tensor_copy(ys[:, 0:512], B[0][:, :]).then_inc(m["ys0"], 1)
                    dve.wait_ge(m["moe_step"], q * PER + (BASE + PER))
                dve.wait_ge(m["y_done"], 1)

            norm_first()
            even_mixer()
            norm_experts(1)
            route(0)
            experts(0)
            norm_odd()
            odd_mixer()
            norm_experts(3)
            route(1)
            experts(1)
            norm_last()

        @block.tensor
        def _(pe):
            def turn_over(i, t, half, src):
                for k in range(4 * half, 4 * half + 4):
                    mm = pe.transpose(B[2 * t + half][:, (k % 4) * P:(k % 4 + 1) * P], by_k(src[:, t, :])[:, :, k], ident)
                mm.then_inc(norm_T, 1)

            def wait_hT(i):
                pe.wait_ge(hT_dve, NT * i + NT)
                pe.wait_ge(hT_act, NT * i + NT)

            def norm_first():
                for t in range(NT):
                    pe.wait_ge(xhat_dve, t + 1)
                    pe.wait_ge(xhat_act, t + 1)
                    for half in range(2):
                        turn_over(0, t, half, xhat)
                wait_hT(0)

            def norm_odd():
                for t in range(NT):
                    pe.wait_ge(x_new, X_NEW[2] + t + 1)
                    pe.wait_ge(x_new_act, t + 1)
                    for half in range(2):
                        turn_over(2, t, half, X)

            def product(dst, pairs, then=None):
                for n, (a, b) in enumerate(pairs):
                    mm = pe.matmul(dst, a, b, start=n == 0, stop=n == len(pairs) - 1)
                if then is not None:
                    mm.then_inc(then, 1)

            def tok(k, t):
                return hT[:, k, t * P:(t + 1) * P]

            def even_mixer():
                for j in range(2):
                    pe.wait_ge(gu_in[j], 16)
                    for c in range(CG):
                        product(B[4 + c][:, j * SEQ:(j + 1) * SEQ],
                                [(gu_slot(j)[:, k, c * P:(c + 1) * P], hT[:, k, :]) for k in range(KD)],
                                vg_done if j else None)
                    if j == 0:
                        pe.wait_ge(even_in, 6 * 16)
                        for c in range(CG):
                            mm = pe.transpose(B[0][:, c * NROW:(c + 1) * NROW], chan_rows[:, c * P:(c + 1) * P],
                                              ident[0:NROW, 0:NROW])
                        mm.then_inc(chan_T, 1)
                        for h in range(CG):
                            mm = pe.transpose(B[1][:, h * P:(h + 1) * P], wsp[:, h, :], ident)
                        mm.then_inc(wsp_T, 1)
                pe.wait_ge(gu_in[3], 16)
                pe.wait_ge(a_done, 1)
                pe.wait_ge(wsp_ok, 1)
                for t in range(NT):
                    product(B[t][:, :], [(tok(k, t), gu_slot(3)[:, k, :]) for k in range(KD)], v_done)
                pe.wait_ge(a_done, 4)
                for j in range(PE_TAPS):
                    pe.wait_ge(diag_ok, j + 1)
                    pe.matmul(B[4][:, 0:SEQ], diag[:, j % DIAGS, :], aT[:, CG - 1, j:j + SEQ],
                              start=j == 0, stop=j == PE_TAPS - 1).then_inc(diag_used, 1)
                pe.wait_ge(gu_in[2], 16)

                def u_product(c):
                    product(B[2 + c // 2][:, (c % 2) * SEQ:(c % 2 + 1) * SEQ],
                            [(gu_slot(2)[:, k, c * P:(c + 1) * P], hT[:, k, :]) for k in range(KD)],
                            u_done if c % 2 else None)

                def over_channels(b, src, then):
                    pe.matmul(B[6 + b][:, :], meanm, src[:, 2 * b:2 * b + 2, :].rearrange("p c s -> p (c s)"),
                              start=True, stop=True).then_inc(then, 1)

                u_product(0)
                u_product(1)
                pe.wait_ge(conv_done, 2)
                over_channels(0, conv, mean_done)
                u_product(2)
                u_product(3)
                pe.wait_ge(vn_done, 1)
                pe.wait_ge(gelu_v, NT)
                for h in range(CG):
                    for n in range(NT):
                        dst = B[h // 2][:, (h % 2) * SEQ + n * P:(h % 2) * SEQ + (n + 1) * P]
                        pe.matmul(dst, vn[:, n, h * P:(h + 1) * P], wspT[:, h, :], start=True, stop=False)
                        mm = pe.matmul(dst, ones[0:1, :], bsp[0:1, h * P:(h + 1) * P], start=False, stop=True)
                    if h % 2:
                        mm.then_inc(sv_done, 1)
                    if h == 1:
                        pe.wait_ge(sq_done, 1)
                        over_channels(0, sq, cvar_done)
                        pe.wait_ge(conv_done, 4)
                        over_channels(1, conv, mean_done)
                pe.wait_ge(gated, 2)
                for j in (2, 3):
                    pe.wait_ge(wo_in[j], 16)
                for t in range(NT):
                    if t:
                        pe.wait_ge(cstd_ok, 2)
                    for half in range(2):
                        mm = w_out(range(4, 8), t, half, True, False)
                        if (t, half) == (0, 0):
                            pe.wait_ge(sq_done, 2)
                            over_channels(1, sq, cvar_done)
                mm.then_inc(half_out, 1)
                for j in (0, 1):
                    pe.wait_ge(wo_in[j], 16)
                pe.wait_ge(silu_done, 4)
                w_out_and_norm(range(0, 4), 1, False)

            def w_out_and_norm(chunks, i, first):
                x0 = X_NEW[i]
                w_out(chunks, 0, 0, first, True)
                w_out(chunks, 0, 1, first, True)
                w_out(chunks, 1, 0, first, True)
                for n, (t, half) in enumerate(((0, 0), (0, 1), (1, 0))):
                    pe.wait_ge(x_new, x0 + n + 1)
                    turn_over(i, t, half, X)
                w_out(chunks, 1, 1, first, True)
                pe.wait_ge(hT_act, NT * i + 1)
                pe.wait_ge(hT_dve, NT * i + 1)
                logits_of(i // 2, 0, 0)
                logits_of(i // 2, 0, 1)
                pe.wait_ge(x_new, x0 + 4)
                turn_over(i, 1, 1, X)
                pe.wait_ge(hT_act, NT * i + 2)
                logits_of(i // 2, 1, 0)
                pe.wait_ge(hT_dve, NT * i + 2)
                logits_of(i // 2, 1, 1)

            def w_out(chunks, t, half, first, last):
                for kk in chunks:
                    w = wout[:, kk // 2, (kk % 2) * D:(kk % 2 + 1) * D]
                    mm = pe.matmul(B[4 + 2 * t + half][:, :], mixT[:, kk, t * P:(t + 1) * P],
                                   by_k(w)[:, :, 4 * half:4 * half + 4],
                                   start=first and kk == chunks[0], stop=last and kk == chunks[-1])
                if last:
                    mm.then_inc(out_done, 1)
                return mm

            def odd_mixer(g1):
                pe.wait_ge(gu_in[0], g1[0] + 32)
                for t in range(NT):
                    pe.wait_ge(hT_dve, NT * 2 + t + 1)
                    pe.wait_ge(hT_act, NT * 2 + t + 1)
                    product(B[4 + t][:, 0:COL_A], [(tok(k, t), wA[:, k, :]) for k in range(KD)], pa_done)
                pe.wait_ge(gu_in[2], g1[2] + 32)
                for t in range(NT):
                    product(B[0][:, t * COL_C:(t + 1) * COL_C], [(tok(k, t), wC[:, k, :]) for k in range(KD)],
                            pc_done if t else None)
                pe.wait_ge(gu_in[1], g1[1] + 32)

                def q_window(t):
                    product(B[6 + t][:, :], [(tok(k, t), wB[:, k, :]) for k in range(KD)], pb_done)

                q_window(0)
                pe.wait_ge(cq_ok, NT)
                cq = lat[:, :, 0:QR].rearrange("p t (r c) -> p t r c", c=QR // P)
                for c in range(QR // P):
                    for t in range(NT):
                        mm = pe.transpose(B[1][:, c * SEQ + t * P:c * SEQ + (t + 1) * P], cq[:, t, :, c], ident)
                mm.then_inc(lat_T, 1)
                pe.wait_ge(ckv_ok, NT)
                for t in range(NT):
                    mm = pe.transpose(B[2][:, t * P:(t + 1) * P], lat[:, t, QR:QR + KVR], ident)
                mm.then_inc(lat_T, 1)
                q_window(1)
                pe.wait_ge(latT_ok, 2)
                for t in range(NT):
                    if t:
                        pe.wait_ge(qs_ok, NT)
                    for b, (h0, nh) in enumerate(((0, 5), (5, 3))):
                        product(B[4 + 2 * t + b][:, 0:nh * QK],
                                [(cqT[:, c, t * P:(t + 1) * P], wuq[:, c, h0 * QK:(h0 + nh) * QK]) for c in range(QR // P)],
                                q_up if b else None)
                pe.wait_ge(gu_in[3], g1[3] + 32)
                pe.wait_ge(latT_ok, 3)
                pe.wait_ge(ks_ok, 1)
                for t in range(NT):
                    for b in range(2):
                        product(B[2 * t + b][:, :], [(ckvT[:, t * P:(t + 1) * P], wukv[:, b * 512:(b + 1) * 512])],
                                kv_up if b else None)
                pe.wait_ge(q_nope, 4)
                pe.wait_ge(q_rope, 4)
                for n, (dst, rows, views) in enumerate(head_blocks):
                    if n >= 8:
                        m = n - 8
                        pe.wait_ge(headT_act if m % 2 else headT_dve, m // 2 + 1)
                    if n == EARLY:
                        pe.wait_ge(k_nope, 4)
                        pe.wait_ge(k_rope, 2)
                        pe.wait_ge(v_ok, 4)
                    for i, v in enumerate(views):
                        mm = pe.transpose(head_bank[n][0:rows, i * P:(i + 1) * P], v, ident)
                    mm.then_inc(head_T, 1)
                pe.wait_ge(headT_act, HEAD_COPIES_ACT)
                pe.wait_ge(headT_dve, HEAD_COPIES_DVE)

                def unit_score(u):
                    window, w, t = unit[u]
                    if u >= 2 and unit[u - 2][0]:
                        pe.wait_ge(biased, before_w[u - 2] + 1)
                    elif u >= 2:
                        pe.wait_ge(expd, 2 * (u - 2) + 2)
                    for i in range(2):
                        dst = score_bank(u, i)
                        if window:
                            r = slice(64 * i, 64 * i + 64)
                            mm = pe.matmul(dst, qsT[r, w, t * P:(t + 1) * P], ksT[r, :], start=True, stop=True)
                        else:
                            mm = pe.matmul(dst, qT[0:QK, 2 * w + i, t * P:(t + 1) * P], kT[0:QK, 2 * w + i, :],
                                           start=True, stop=True)
                    mm.then_inc(score, 1)

                def unit_prob_T(u):
                    pe.wait_ge(expd, 2 * u + 2)
                    if u >= 2:
                        pe.wait_ge(pT_ok, u - 1)
                    for i in range(2):
                        for kc in range(NT):
                            mm = pe.transpose(B[2 + u % 2][:, (2 * i + kc) * P:(2 * i + kc + 1) * P],
                                              prob[:, u % 2, i, kc * P:(kc + 1) * P], ident)
                    mm.then_inc(prob_T, 1)

                def unit_out(u):
                    window, w, _ = unit[u]
                    pe.wait_ge(pT_ok, u + 1)
                    if u >= 2:
                        pe.wait_ge(o_ok, u - 1)
                    for i in range(2):
                        dst = B[4 + u % 2][:, i * VD:(i + 1) * VD]
                        product(dst, [(pT[:, u % 2, 2 * i + kc, :],
                                       ksvs[:, kc, P + i * SWA_D:P + (i + 1) * SWA_D] if window else vm[:, kc, 2 * w + i, :])
                                      for kc in range(NT)], pv if i else None)

                def outputs_T(b):
                    for kk in range(2):
                        for t in range(NT):
                            mm = pe.transpose(B[b][:, kk * SEQ + t * P:kk * SEQ + (t + 1) * P],
                                              osb[:, t, (2 * b + kk) * P:(2 * b + kk + 1) * P], ident)
                    mm.then_inc(o_T, 1)

                for u in range(UNITS + 3):
                    if u < UNITS:
                        unit_score(u)
                    if 2 <= u < UNITS + 2:
                        unit_prob_T(u - 2)
                    if u == UNITS + 2:
                        pe.wait_ge(o_ok, UNITS - 2)
                        pe.wait_ge(biased, UNITS // 2)
                        outputs_T(0)
                        outputs_T(1)
                    if u >= 3:
                        unit_out(u - 3)
                for j in range(QUAD):
                    pe.wait_ge(wo_in[j], 32)
                pe.wait_ge(oT_act, 1)
                pe.wait_ge(oT_dve, 1)
                for half in range(2):
                    w_out(range(0, 4), 1, half, True, False)
                pe.wait_ge(o_ok, UNITS)
                outputs_T(2)
                outputs_T(3)
                for half in range(2):
                    mm = w_out(range(0, 4), 0, half, True, False)
                mm.then_inc(half_out, 1)
                pe.wait_ge(oT_act, 2)
                pe.wait_ge(oT_dve, 2)
                w_out_and_norm(range(4, 8), 3, False)

            def logits_of(l, t, half):
                if (l, t, half) == (0, 0, 0):
                    pe.wait_ge(route_w_done, 10)
                    pe.wait_ge(pads_done, 5)
                for k in range(4 * half, 4 * half + 4):
                    mm = pe.matmul(B[0][:, t * 64:t * 64 + NL], tok(k, t), wrt[:, l, k, :], start=k == 0, stop=k == KD - 1)
                if (t, half) == (1, 1):
                    mm.then_inc(logits, 1)

            def route(l):
                for t in range(NT):
                    for half in range(2):
                        mm = pe.matmul(B[4 + 2 * t + half][:, :], ident, X[:, t, half * 512:(half + 1) * 512],
                                       start=True, stop=False)
                mm.then_inc(x_moved, 1)
                pe.wait_ge(member_ok, l + 1)
                product(B[1][:, 0:EXPERTS], [(before, member[:, 0, :])])
                product(B[1][:, EXPERTS:2 * EXPERTS], [(before, member[:, 1, :]), (ones, member[:, 0, :])])
                product(B[1][:, 64:64 + EXPERTS], [(ones, member[:, 0, :]), (ones, member[:, 1, :])], ranks)
                for b, cols, ready in ((3, weight, weight_ok), (2, key, key_ok)):
                    pe.wait_ge(ready, l + 1)
                    for k in range(2):
                        for t in range(NT):
                            product(B[b][:, k * SEQ + t * P:k * SEQ + (t + 1) * P],
                                    [(cols[:, t, k:k + 1].broadcast_to([P, P]), ident)],
                                    rows_T if (k, t) == (1, 1) else None)

            def experts(l, g0, u0, d0):
                m = M[l]

                def turn(q, spare=False, late=False):
                    pe.wait_ge(m["pick_ok"], q * 2 + 2)
                    pe.wait_ge(xhat_dve, NT * (XHAT[2 * l + 1] + 1))
                    pe.wait_ge(xhat_act, NT * (XHAT[2 * l + 1] + 1))
                    xh = xhat[:, :, :].rearrange("p t (d k) -> p t d k", k=KD)
                    for k in range(KD):
                        if k == 4 and not (spare or late):
                            pe.wait_ge(nq_ok, l + 1)
                        for t in range(NT):
                            mm = pe.matmul(B[k // 4][:, (k % 4) * P:(k % 4 + 1) * P], xh[:, t, :, k], pick[:, t, :],
                                           start=t == 0, stop=t == NT - 1)
                        if k == 3:
                            mm.then_inc(m["gath0"], 1)
                    mm.then_inc(m["gath1"], 1)
                    pe.wait_ge(m["xs0"], q + 1)
                    pe.wait_ge(rows_ok, 2 * l + 2)
                    for j in range(QUAD):
                        if spare and j < SPARE_GATE:
                            pe.wait_ge(spare_gate_in, 16 * SPARE_GATE * (l + 1))
                        else:
                            pe.wait_ge(gu_in[j], q * 16 + (g0[j] + (0 if late and j < SPARE_GATE else 16)))
                    for a, used in enumerate(("gate_used", "up_used")):
                        if a and spare:
                            pe.wait_ge(spare_up_in, 16 * SPARE_UP * (l + 1))
                        elif a:
                            pe.wait_ge(up_in[0], q * 32 + (u0[0] + (0 if late else 32)))
                        if a:
                            pe.wait_ge(up_in[1], q * 32 + (u0[1] + 32))
                        for k in range(KD):
                            if a == 0 and k == KD // 2:
                                pe.wait_ge(m["xs1"], q + 1)
                            for j in range(QUAD):
                                w = ring_gu[:, j, a * KD * F:(a + 1) * KD * F]
                                if spare and j < (SPARE_UP if a else SPARE_GATE):
                                    w = (spare_up if a else spare_gate)[j]
                                mm = pe.matmul(B[2 + a][SLOTS * j:SLOTS * (j + 1), 0:F], xs[:, k, SLOTS * j:SLOTS * (j + 1)],
                                               w[:, k * F:(k + 1) * F],
                                               start=k == 0, stop=k == KD - 1, tile_position=(0, SLOTS * j))
                        mm.then_inc(m[used], 1)
                    pe.wait_ge(m["hid_ok"], q + 1)
                    hv = hid[:, :].rearrange("p (f c) -> p f c", c=FC)
                    for c in range(FC):
                        mm = pe.transpose(B[2][:, c * P:(c + 1) * P], hv[:, :, c], ident)
                    mm.then_inc(m["hid_T"], 1)
                    pe.wait_ge(m["hidT_ok"], q + 1)
                    for c in range(FC):
                        if spare:
                            pe.wait_ge(spare_dn_in, 16 * FC * QUAD * (l + 1))
                        else:
                            pe.wait_ge(dn_in[c], q * (16 * QUAD) + (d0 + (0 if late else 16 * QUAD)))
                        for half in range(2):
                            for j in range(QUAD):
                                slot = spare_dn[j] if spare else ring_dn[:, j, :]
                                mm = pe.matmul(B[half][SLOTS * j:SLOTS * (j + 1), :], hidT[:, c, SLOTS * j:SLOTS * (j + 1)],
                                               slot[:, c * D + half * 512:c * D + (half + 1) * 512],
                                               start=c == 0, stop=c == FC - 1, tile_position=(0, SLOTS * j))
                            if c == FC - 1:
                                mm.then_inc(m["dn_used"] if half else m["down0"], 1)
                    pe.wait_ge(m["back_ok"], q + 1)
                    for half in range(2):
                        pe.wait_ge(m["ys1"] if half else m["ys0"], q + 1)
                        for t in range(NT):
                            pe.matmul(B[4 + 2 * t + half][:, :], backs[:, t * P:(t + 1) * P], ys[:, half * 512:(half + 1) * 512],
                                      start=False, stop=False)
                turn(0)
                turn(1, spare=True)
                pe.wait_ge(nq_ok, l + 1)
                n = pe.value_load(nq[0:1, l:l + 1], min_val=QUADS, max_val=QUADS * MAX_ROUNDS)
                with pe.Fori(2, n) as q:
                    turn(q, late=True)
                for b in range(4):
                    mm = pe.matmul(B[4 + b][:, :].rearrange("p (a n) -> p a n", n=P), zeros[:, :],
                                   zeros[:, :].unsqueeze(1).broadcast_to([1, 4, P]), start=False, stop=True)
                mm.then_inc(m["y_done"], 1)
                return n

            pe.wait_ge(const_in, 16)
            norm_first()
            even_mixer()
            route(0)
            n0 = experts(0, [16] * QUAD, [0, 0], 0)
            g1 = [n0 * 16 - (16 if j < SPARE_GATE else 0) for j in range(QUAD)]
            norm_odd()
            odd_mixer([g + 16 for g in g1])
            route(1)
            experts(1, [g + 48 for g in g1], [n0 * 32 - 32, n0 * 32], n0 * (16 * QUAD) - 16 * QUAD)


_INS = ['x', 'norm_mix', 'norm_ffn', 'norm_final', 'ev_w_in', 'ev_conv_w', 'ev_conv_b', 'ev_cnorm_g', 'ev_cnorm_b',
        'ev_vnorm_g', 'ev_vnorm_b', 'ev_w_sp', 'ev_b_sp', 'ev_w_out', 'od_w_in', 'od_g_cq', 'od_w_uq', 'od_g_ckv',
        'od_w_ukv', 'od_sink', 'od_w_out', 'moe_w_group', 'moe_b_group', 'moe_w_router', 'moe_b_router',
        'moe_w_gate', 'moe_w_up', 'moe_w_down']


def kernel(**inputs):
    import concourse.bacc as bacc
    from concourse.bass_utils import run_bass_kernel_spmd as run

    nc = bacc.Bacc("TRN2", target_bir_lowering=False, num_devices=1)
    arrays, args = {}, []
    for name in _INS:
        a = np.ascontiguousarray(inputs[name])
        arrays[f"in_{name}"] = a
        args.append(nc.dram_tensor(f"in_{name}", a.shape, mybir.dt.from_np(a.dtype), kind="ExternalInput").ap())
    arrays["constants"] = constants()
    args.append(nc.dram_tensor("constants", (P, NCONST), mybir.dt.float32, kind="ExternalInput").ap())
    args.append(nc.dram_tensor("out_x", (1, SEQ, D), mybir.dt.float32, kind="ExternalOutput").ap())
    program(nc, *args)
    return run(nc, [arrays], core_ids=[0]).results[0]["out_x"]
```
